# Optimizing a Trainium2 kernel written in Bass

```python
import math
import jax, jax.numpy as jnp
from jax import lax
import numpy as np

D_MODEL = 1024
BATCH = 1
SEQ = 512
DEPTH = 2
DEC_BATCH = 8
DEC_SEQ = 8
PAST_LEN = 4096
PAGE_SIZE = 128

HEAD_DIM = 64
HG_HEADS = 4
HG_DK = 64
HG_DV = 64
ATT_HEADS = 6
GLA_HEADS = 6
GLA_DK = 32
GLA_DV = 64
GLA_GATE_RANK = 16
GLA_TAU = 16.0
MIX_WIDTH = HG_HEADS * HG_DV + ATT_HEADS * HEAD_DIM + GLA_HEADS * GLA_DV
D_FF = 4 * D_MODEL
D_PLE = 256
ROPE_THETA = 500000.0
ROT_FRACTION = 4
DILATED_PATTERNS = ((128, 1), (512, 4), (2048, 16))
MAX_WINDOW = 2048
QUERY_BLOCK = 128
RECUR_CHUNK = 64
EPS = 1e-6
IN_SPLITS = (HG_HEADS * HG_DK, HG_HEADS * HG_DK, HG_HEADS * HG_DV, HG_HEADS * HG_DV,
             ATT_HEADS * HEAD_DIM, ATT_HEADS * HEAD_DIM, ATT_HEADS * HEAD_DIM,
             GLA_HEADS * GLA_DK, GLA_HEADS * GLA_DK, GLA_HEADS * GLA_DV, GLA_GATE_RANK, GLA_HEADS * GLA_DV)
D_IN = sum(IN_SPLITS)

kernel_name = 'hybrid_hgrn2_dilated_gla_decode_step'

def rms_norm(x, w):
    x32 = x.astype(jnp.float32)
    y = x32 * lax.rsqrt(jnp.mean(x32 * x32, axis=-1, keepdims=True) + EPS)
    return (y * w.astype(jnp.float32)).astype(x.dtype)

def partial_rotary(x, pos):
    rd = x.shape[-1] // ROT_FRACTION
    half = rd // 2
    inv = jnp.exp(-math.log(ROPE_THETA) * jnp.arange(half, dtype=jnp.float32) * (2.0 / rd))
    ang = pos[:, None] * inv[None, :]
    cos = jnp.cos(ang)[None, :, None, :]
    sin = jnp.sin(ang)[None, :, None, :]
    x32 = x.astype(jnp.float32)
    x1 = x32[..., :half]
    x2 = x32[..., half:rd]
    out = jnp.concatenate([x1 * cos - x2 * sin, x2 * cos + x1 * sin, x32[..., rd:]], axis=-1)
    return out.astype(x.dtype)

def gated_linear_recurrence(q, k, v, log_f, s0):
    B, T, H, Dk = q.shape
    Dv = v.shape[-1]
    c = min(RECUR_CHUNK, T)
    n = -(-T // c)
    pad = n * c - T

    def prep(a):
        a = jnp.pad(a.astype(jnp.float32), ((0, 0), (0, pad), (0, 0), (0, 0)))
        return jnp.moveaxis(a.reshape(B, n, c, H, a.shape[-1]), 1, 0)

    qs, ks, vs, gs = prep(q), prep(k), prep(v), prep(log_f)
    causal = jnp.tril(jnp.ones((c, c), dtype=bool))[None, :, :, None, None]

    def step(S, blk):
        qc, kc, vc, gc = blk
        b = jnp.cumsum(gc, axis=1)
        o_inter = jnp.einsum('bthk,bhkv->bthv', qc * jnp.exp(b), S)
        diff = b[:, :, None] - b[:, None, :]
        decay = jnp.exp(jnp.where(causal, diff, -jnp.inf))
        A = jnp.einsum('bthk,bshk,btshk->bths', qc, kc, decay)
        o_intra = jnp.einsum('bths,bshv->bthv', A, vc)
        b_last = b[:, -1]
        k_dec = kc * jnp.exp(b_last[:, None] - b)
        S_new = jnp.exp(b_last)[..., None] * S + jnp.einsum('bshk,bshv->bhkv', k_dec, vc)
        return S_new, o_inter + o_intra

    S_T, o = lax.scan(step, s0.astype(jnp.float32), (qs, ks, vs, gs))
    o = jnp.moveaxis(o, 0, 1).reshape(B, n * c, H, Dv)[:, :T]
    return o.astype(v.dtype), S_T.astype(s0.dtype)

def dilated_window_attention(q, k_all, v_all, q_start):
    B, T, H, Dh = q.shape
    bs = QUERY_BLOCK if T % QUERY_BLOCK == 0 else T
    nb = T // bs
    qb = jnp.moveaxis(q.reshape(B, nb, bs, H, Dh), 1, 0)
    scale = Dh ** -0.5

    def block(args):
        bidx, qc = args
        iq = q_start + bidx * bs + jnp.arange(bs)
        q32 = qc.astype(jnp.float32) * scale
        outs, lses = [], []
        for (w, d) in DILATED_PATTERNS:
            n_keys = w // d + 1
            kidx = iq[:, None] - d * jnp.arange(n_keys)[None, :]
            valid = kidx >= 0
            kidx = jnp.maximum(kidx, 0)
            kg = k_all[:, kidx].astype(jnp.float32)
            vg = v_all[:, kidx].astype(jnp.float32)
            s = jnp.einsum('bqhd,bqnhd->bhqn', q32, kg)
            s = jnp.where(valid[None, None], s, -jnp.inf)
            lse = jax.nn.logsumexp(s, axis=-1)
            p = jnp.exp(s - lse[..., None])
            outs.append(jnp.einsum('bhqn,bqnhd->bqhd', p, vg))
            lses.append(lse)
        wts = jax.nn.softmax(jnp.stack(lses, axis=0), axis=0)
        wts = jnp.transpose(wts, (0, 1, 3, 2))[..., None]
        return jnp.sum(wts * jnp.stack(outs, axis=0), axis=0).astype(q.dtype)

    o = lax.map(block, (jnp.arange(nb), qb))
    return jnp.moveaxis(o, 0, 1).reshape(B, T, H, Dh)

def trunk_layer(h, p_i, s_hgrn, s_gla, k_past, v_past, pos_offset, lb,
                norm_pre_mix, w_in, hgrn_norm, attn_norm, gla_w_gate2, gla_b_gate, gla_norm, w_out,
                norm_post_mix, norm_pre_mlp, w_up, w_down, norm_post_mlp, w_ple_gate, w_ple):
    B, T, _ = h.shape
    xn = rms_norm(h, norm_pre_mix)
    proj = xn @ w_in
    split_points = [int(v) for v in np.cumsum(IN_SPLITS)[:-1]]
    hq, hf, hi, hg, aq, ak, av, gq, gk, gv, g_lr, gr = jnp.split(proj, split_points, axis=-1)

    def heads(a, n):
        return a.reshape(B, T, n, -1)

    lb_h = lb.reshape(HG_HEADS, HG_DK)
    f = lb_h + (1.0 - lb_h) * jax.nn.sigmoid(heads(hf, HG_HEADS).astype(jnp.float32))
    o_h, s_hgrn_new = gated_linear_recurrence(heads(hq, HG_HEADS), 1.0 - f, heads(hi, HG_HEADS), jnp.log(f), s_hgrn)
    o_h = rms_norm(o_h, hgrn_norm.reshape(HG_HEADS, HG_DV)) * jax.nn.silu(heads(hg, HG_HEADS))

    pos = jnp.arange(T, dtype=jnp.float32) + pos_offset
    qa = partial_rotary(heads(aq, ATT_HEADS), pos)
    ka = partial_rotary(heads(ak, ATT_HEADS), pos)
    k_all = jnp.concatenate([k_past, ka.astype(k_past.dtype)], axis=1)
    v_all = jnp.concatenate([v_past, heads(av, ATT_HEADS).astype(v_past.dtype)], axis=1)
    o_a = dilated_window_attention(qa, k_all, v_all, k_past.shape[1]).reshape(B, T, -1)
    o_a = rms_norm(o_a, attn_norm)
    L = k_all.shape[1]
    new_len = min(MAX_WINDOW, L)
    k_buf = k_all[:, L - new_len:]
    v_buf = v_all[:, L - new_len:]

    log_a = jax.nn.log_sigmoid((g_lr @ gla_w_gate2 + gla_b_gate).astype(jnp.float32)) / GLA_TAU
    o_g, s_gla_new = gated_linear_recurrence(heads(gq, GLA_HEADS) * (GLA_DK ** -0.5), heads(gk, GLA_HEADS),
                                             heads(gv, GLA_HEADS), heads(log_a, GLA_HEADS), s_gla)
    o_g = rms_norm(o_g, gla_norm.reshape(GLA_HEADS, GLA_DV)) * jax.nn.silu(heads(gr, GLA_HEADS))

    mix = jnp.concatenate([o_h.reshape(B, T, -1), o_a, o_g.reshape(B, T, -1)], axis=-1) @ w_out
    h = h + rms_norm(mix, norm_post_mix)

    u = jnp.square(jax.nn.relu(rms_norm(h, norm_pre_mlp) @ w_up))
    h = h + rms_norm(u @ w_down, norm_post_mlp)

    h = h + jax.nn.sigmoid(h @ w_ple_gate) * (p_i @ w_ple)
    return h, s_hgrn_new, s_gla_new, k_buf, v_buf

def setup_inputs(seed: int = 0) -> dict:
    key = jax.random.key(seed)
    ks = jax.random.split(key, 24)
    f32 = jnp.float32
    win = min(MAX_WINDOW, PAST_LEN)

    def nrm(k, shape, scale):
        return jax.random.normal(k, shape, f32) * scale

    def gain(k, n):
        return 1.0 + 0.1 * jax.random.normal(k, (DEPTH, n), f32)

    return {
        'x_prompt': nrm(ks[0], (BATCH, SEQ, D_MODEL), 1.0),
        'x_sample': nrm(ks[1], (DEC_BATCH, DEC_SEQ, D_MODEL), 1.0),
        'state_hgrn': nrm(ks[2], (DEPTH, DEC_BATCH, HG_HEADS, HG_DK, HG_DV), 0.5),
        'state_gla': nrm(ks[3], (DEPTH, DEC_BATCH, GLA_HEADS, GLA_DK, GLA_DV), 0.5),
        'cache_k': nrm(ks[4], (DEPTH, DEC_BATCH, win, ATT_HEADS, HEAD_DIM), 1.0),
        'cache_v': nrm(ks[5], (DEPTH, DEC_BATCH, win, ATT_HEADS, HEAD_DIM), 1.0),
        'p_prompt': nrm(ks[6], (DEPTH, BATCH, SEQ, D_PLE), 1.0),
        'p_sample': nrm(ks[7], (DEPTH, DEC_BATCH, DEC_SEQ, D_PLE), 1.0),
        'norm_pre_mix': gain(ks[8], D_MODEL),
        'w_in': nrm(ks[9], (DEPTH, D_MODEL, D_IN), D_MODEL ** -0.5),
        'hgrn_lb': nrm(ks[10], (DEPTH, HG_HEADS * HG_DK), 0.5),
        'hgrn_norm': gain(ks[11], HG_HEADS * HG_DV),
        'attn_norm': gain(ks[12], ATT_HEADS * HEAD_DIM),
        'gla_w_gate2': nrm(ks[13], (DEPTH, GLA_GATE_RANK, GLA_HEADS * GLA_DK), GLA_GATE_RANK ** -0.5),
        'gla_b_gate': nrm(ks[14], (DEPTH, GLA_HEADS * GLA_DK), 0.1),
        'gla_norm': gain(ks[15], GLA_HEADS * GLA_DV),
        'w_out': nrm(ks[16], (DEPTH, MIX_WIDTH, D_MODEL), MIX_WIDTH ** -0.5),
        'norm_post_mix': gain(ks[17], D_MODEL),
        'norm_pre_mlp': gain(ks[18], D_MODEL),
        'w_up': nrm(ks[19], (DEPTH, D_MODEL, D_FF), D_MODEL ** -0.5),
        'w_down': nrm(ks[20], (DEPTH, D_FF, D_MODEL), D_FF ** -0.5),
        'norm_post_mlp': gain(ks[21], D_MODEL),
        'w_ple_gate': nrm(ks[22], (DEPTH, D_MODEL, D_MODEL), D_MODEL ** -0.5),
        'w_ple': nrm(ks[23], (DEPTH, D_PLE, D_MODEL), D_PLE ** -0.5),
    }

def reference(x_prompt, x_sample, state_hgrn, state_gla, cache_k, cache_v, p_prompt, p_sample,
              norm_pre_mix, w_in, hgrn_lb, hgrn_norm, attn_norm, gla_w_gate2, gla_b_gate, gla_norm, w_out,
              norm_post_mix, norm_pre_mlp, w_up, w_down, norm_post_mlp, w_ple_gate, w_ple):
    lb_cum = jnp.cumsum(jax.nn.softmax(hgrn_lb.astype(jnp.float32), axis=0), axis=0)
    lower_bounds = lb_cum - lb_cum[0:1]
    bp = x_prompt.shape[0]
    dt = x_prompt.dtype
    zero_hgrn = jnp.zeros((bp, HG_HEADS, HG_DK, HG_DV), dt)
    zero_gla = jnp.zeros((bp, GLA_HEADS, GLA_DK, GLA_DV), dt)
    zero_kv = jnp.zeros((bp, 0, ATT_HEADS, HEAD_DIM), dt)
    hp, hs = x_prompt, x_sample
    hgrn_p, gla_p, kp, vp = [], [], [], []
    hgrn_s, gla_s, ksm, vsm = [], [], [], []
    for i in range(DEPTH):
        w = (norm_pre_mix[i], w_in[i], hgrn_norm[i], attn_norm[i], gla_w_gate2[i], gla_b_gate[i], gla_norm[i],
             w_out[i], norm_post_mix[i], norm_pre_mlp[i], w_up[i], w_down[i], norm_post_mlp[i],
             w_ple_gate[i], w_ple[i])
        hp, sh, sg, kb, vb = trunk_layer(hp, p_prompt[i], zero_hgrn, zero_gla, zero_kv, zero_kv, 0,
                                         lower_bounds[i], *w)
        hgrn_p.append(sh); gla_p.append(sg); kp.append(kb); vp.append(vb)
        hs, sh, sg, kb, vb = trunk_layer(hs, p_sample[i], state_hgrn[i], state_gla[i], cache_k[i], cache_v[i],
                                         PAST_LEN, lower_bounds[i], *w)
        hgrn_s.append(sh); gla_s.append(sg); ksm.append(kb); vsm.append(vb)
    return (hp, hs,
            jnp.stack(hgrn_p), jnp.stack(gla_p), jnp.stack(kp), jnp.stack(vp),
            jnp.stack(hgrn_s), jnp.stack(gla_s), jnp.stack(ksm), jnp.stack(vsm))


_drawn_inputs = setup_inputs


def setup_inputs(seed=0):
    import zlib

    import numpy as np

    out = dict(_drawn_inputs(seed))
    spreads = {}
    factors = {}
    for name, (base, spread) in spreads.items():
        noise = np.random.default_rng([zlib.crc32(name.encode()), seed]).standard_normal(out[name].shape)
        drawn = base * np.exp(spread * noise) if base else spread * noise
        out[name] = __import__('jax').numpy.asarray(drawn.astype(out[name].dtype))
    for name, factor in factors.items():
        out[name] = (out[name] * factor).astype(out[name].dtype)
    return out
```

```python
import math
from contextlib import ExitStack

import numpy as np

import concourse.bass as bass
from concourse import mybir
from concourse.alu_op_type import AluOpType as ALU

F32 = mybir.dt.float32
U32 = mybir.dt.uint32
ACT = mybir.ActivationFunctionType
AX_X = mybir.AxisListType.X

P = 128
D_MODEL, DEPTH = 1024, 2
SEQ, DEC_BATCH, DEC_SEQ = 512, 8, 8
NEW = DEC_BATCH * DEC_SEQ
T = SEQ + NEW
HALF = T // 2
KT = D_MODEL // P
D_FF = 4 * D_MODEL
FT = D_FF // P
PAST, WIN = 4096, 2048
CH = 64
NC = SEQ // CH
TT = SEQ // P
EPS = 1e-6
ROPE_THETA = 500000.0
PATTERNS = ((128, 1), (512, 4), (2048, 16))
NEG = -1e30
KEYS = 1280
KC = KEYS // P
KEPT = WIN - DEC_SEQ

IN1 = ["hf0", "hf1", "gq1", "hq0", "hq1", "gq0", "gk0", "gk1"]
IN2 = ["aq0", "aq1", "aq2", "ak0", "ak1", "ak2", "hg0", "hg1", "gr0", "gr1", "gr2"]
R_IN1, R_V = 0, 8
R_IN2 = R_V + 8
R_OUT = R_IN2 + len(IN2)
R_PLE = R_OUT + KT
R_UP = R_PLE + 2
R_DOWN = R_UP + FT
R_GATE = R_DOWN + FT
UNITS = R_GATE + KT
RING = 8

HEADS = 10
HEAD_AT = [(0, 0, 64), (0, 64, 64), (1, 0, 64), (1, 64, 64)] + \
          [(2, 32 * j, 32) for j in range(4)] + [(3, 0, 32), (3, 32, 32)]
GROUPS = [(0, 2), (1, 3), (4, 8), (5, 9), (6,), (7,)]
SLOT = {h: i for i, h in enumerate([h for g in GROUPS for h in g])}
FIRST_SLOT = [sum(len(g) for g in GROUPS[:i]) for i in range(len(GROUPS))]
LEVELS = [0, 1, 2, 4, 8, 16, 32]
SMALL = [l for l, h in enumerate(LEVELS) if 2 * h <= DEC_SEQ]

LIN = (["sum_pre", "hf0", "hf1", "gq1", "z0", "z1", "hq0", "hq1", "gq0", "gk0", "gk1"]
       + [f"v{g}{tt}" for g in range(2) for tt in range(TT + 1)]
       + IN2 + [f"sum_o{i}" for i in range(5)] + [f"rot{i}" for i in range(6)]
       + [f"pv{i}" for i in range(3)] + ["sum_att"]
       + [f"out{n}" for n in range(KT)] + ["ple0", "ple1", "sum_mix"] + [f"ple{n}" for n in range(2, KT)]
       + ["sum_mlp"] + [f"up{n}" for n in range(FT)] + [f"down{n}" for n in range(KT)]
       + ["sum_down"] + [f"gate{n}" for n in range(KT)])
Q = {name: i for i, name in enumerate(LIN)}
assert len(Q) == len(LIN)

C_IDENT, C_ONES, C_HEADSUM, C_ROT = 0, P, 2 * P, 3 * P
C_COS = 4 * P
C_SIN = C_COS + T
C_RESET = C_SIN + T
C_BIAS = C_RESET + T
C_MASK = C_BIAS + 4 * P
C_BATCH = C_MASK + len(LEVELS) * CH
C_SBIAS = C_BATCH + DEC_BATCH
C_NBIAS = C_SBIAS + KEYS
C_SCALE = C_NBIAS + DEC_BATCH * NEW
C_EPS = C_SCALE + 1
C_END = C_EPS + 1
W_PRE, W_MIX, W_MLP, W_DOWN, W_O = 0, 8, 16, 24, 32
W_B = 40
W_LB = 42
W_FLAG = 46
W_G2 = 47
W_END = W_G2 + 2 * P


def multiplicity(delta):
    m = np.zeros(delta.shape)
    for w, d in PATTERNS:
        m += (delta >= 0) & (delta <= w) & (delta % d == 0)
    return np.where(m > 0, np.log(np.maximum(m, 1)), NEG).astype(np.float32)


def cache_order():
    j = np.arange(WIN)
    wide = (j < WIN - 512) & (j % 16 < DEC_SEQ)
    read = np.concatenate([j[wide], j[j >= WIN - 512]])
    assert len(read) == KEYS and (read[:DEC_SEQ] == np.arange(DEC_SEQ)).all()
    return np.concatenate([read, j[(j < WIN - 512) & ~wide]])


def constants():
    c = np.zeros((P, C_END), np.float32)
    r = np.arange(P)
    c[:, C_IDENT:C_IDENT + P] = np.eye(P)
    c[:, C_ONES:C_ONES + P] = 1
    c[:, C_HEADSUM:C_HEADSUM + P] = (r[:, None] // 64 == r[None] // 64)
    d = r % 64
    rot = np.zeros((P, P), np.float32)
    for m in range(P):
        if d[m] < 8:
            rot[m + 8, m] = -1
        elif d[m] < 16:
            rot[m - 8, m] = 1
    c[:, C_ROT:C_ROT + P] = rot
    pos = np.concatenate([np.arange(SEQ), PAST + np.arange(NEW) % DEC_SEQ]).astype(np.float32)
    inv = np.exp((-math.log(ROPE_THETA) * np.arange(8, dtype=np.float32) * np.float32(2.0 / 16)).astype(np.float32))
    ang = (pos[None] * inv.astype(np.float32)[:, None]).astype(np.float32).astype(np.float64)
    c[:, C_COS:C_COS + T] = np.where(d[:, None] < 16, np.cos(ang)[d % 8], 1)
    c[:, C_SIN:C_SIN + T] = np.where(d[:, None] < 16, np.sin(ang)[d % 8], 0)
    t = np.arange(T)
    c[:, C_RESET:C_RESET + T] = np.where(t < SEQ, t % CH != 0, t % DEC_SEQ != 0)
    for j in range(4):
        c[:, C_BIAS + P * j:C_BIAS + P * (j + 1)] = multiplicity((3 - j) * P + r[:, None] - r[None])
    s, u = r % CH, np.arange(CH)
    for l, h in enumerate(LEVELS):
        m = (s[:, None] == u) if h == 0 else \
            (s[:, None] // (2 * h) == u // (2 * h)) & (s[:, None] % (2 * h) < h) & (u % (2 * h) >= h)
        c[:, C_MASK + CH * l:C_MASK + CH * (l + 1)] = m
    for b in range(DEC_BATCH):
        c[:NEW, C_BATCH + b] = (r[:NEW] // DEC_SEQ == b)
    q = np.arange(48) % DEC_SEQ
    c[:48, C_SBIAS:C_SBIAS + KEYS] = multiplicity(WIN + q[:, None] - cache_order()[None, :KEYS])
    n = np.arange(NEW)
    for b in range(DEC_BATCH):
        c[:48, C_NBIAS + NEW * b:C_NBIAS + NEW * (b + 1)] = \
            np.where(n // DEC_SEQ == b, multiplicity(q[:, None] - n[None] % DEC_SEQ), NEG)
    c[:, C_SCALE] = np.where(r < 64, 32.0 ** -0.5, 1)
    c[:, C_EPS] = EPS
    return c


class Steps:

    def __init__(self, eng, sem):
        self.eng, self.sem, self.n = eng, sem, 0

    def mark(self, ins):
        self.n += 1
        ins.then_inc(self.sem, 1)
        return self.n

    def step(self, ins):
        self.eng.wait_ge(self.sem, self.mark(ins))

    def after(self, n):
        self.eng.wait_ge(self.sem, n)


def build(nc, x_t, consts, params, p_t, s0_in, w_units, ck, cv,
          y_out, kp_out, kn_out, vp_out, vn_out, ck_out, cv_out, sp_out, ss_out):
    with ExitStack() as ctx:
        def sb(name, cols):
            return ctx.enter_context(nc.sbuf_tensor(name, [P, cols], F32))

        sems = []

        def sem(name):
            sems.append(ctx.enter_context(nc.semaphore(name)))
            return sems[-1]

        h_sb = sb("h", KT * T)
        x_sb = sb("x", KT * T)
        pt_sb = sb("pt", 2 * T)
        ring_sb = sb("ring", RING * 1024)
        con = sb("con", C_END)
        par = sb("par", W_END)
        ebl_sb = sb("ebl", 4 * 16)
        small = sb("small", 64)
        arena = sb("arena", 29184)
        H = h_sb[:, :].rearrange("p (k t) -> p k t", k=KT)
        X = x_sb[:, :].rearrange("p (k t) -> p k t", k=KT)
        PT_IN = pt_sb[:, :].rearrange("p (k t) -> p k t", k=2)
        W = ring_sb[:, :].rearrange("p (s k n) -> p s k n", s=RING, k=KT)
        EBL = ebl_sb[:, :].rearrange("p (r c) -> p r c", r=4)

        def at(off, n, count=None):
            v = arena[:, off:off + n]
            return v if count is None else v.rearrange("p (a t) -> p a t", a=count)

        Q4, K4 = at(0, 4 * T, 4), at(4 * T, 4 * T, 4)
        V = at(4608, 5 * 1024, 5)
        B = at(9728, 4 * T, 4)
        LV = [at(12032, 4 * T, 4), at(14336, 4 * T, 4)]
        KDT = at(16640, 5 * 512, 5)
        AT = at(16640, HEADS * 4 * CH).rearrange("p (s c t) -> p s c t", s=HEADS, c=4)
        ATS = at(19200, HEADS * CH, HEADS)
        OI = at(19840, 5 * T, 5)
        QI = at(22720, 4 * T, 4)
        SC = at(25024, NC * 256).rearrange("p (c r v) -> p c r v", c=NC, r=4)
        S0 = at(27072, DEC_BATCH * 256).rearrange("p (b r v) -> p b r v", b=DEC_BATCH, r=4)
        VX = [LV[1][:, 0:1, 0:512], LV[1][:, 1:2, 0:512]]
        ROTQK = at(22720, 6 * T, 6)
        GATES = at(26176, 5 * T, 5)
        proj = {"hf0": K4[:, 0], "hf1": K4[:, 1], "gq1": Q4[:, 3], "hq0": Q4[:, 0], "hq1": Q4[:, 1],
                "gq0": Q4[:, 2], "gk0": K4[:, 2], "gk1": K4[:, 3]}
        for i, n in enumerate(IN2):
            proj[n] = ROTQK[:, i] if i < 6 else GATES[:, i - 6]
        ETMP = at(0, 5 * T, 5)
        SQO = at(9728, 5 * T, 5)
        RSO = [at(12608, T), at(13184, T)]
        KB = [at(0, 3 * KEYS, 3), at(9728, 3 * KEYS, 3)]
        VB = [at(13568, KC * 384, KC), at(17408, KC * 384, KC)]
        PTB = [at(21248, 528), at(21776, 528)]
        PTP = [at(21248, 512), at(21760, 512)]
        SMP = [at(26176 + 512 * i, 512) for i in range(3)]
        SMS = [at(26176 + 1344 * i, 1344) for i in range(2)]
        OS = [at(3840 + 384 * i, 384) for i in range(2)]
        ROTMP = [V[:, 2, 0:T], V[:, 3, 0:T]]

        def qbd(b):
            return V[:, b // 4, 144 * (b % 4):144 * (b % 4) + 144].rearrange("p (c n) -> p c n", c=3)

        SQA = at(0, 3 * T, 3)
        ACCA, RSA = at(3 * T, T), at(4 * T, T)
        U = at(0, FT * T, FT)
        Y = at(18432, KT * T, KT)
        PL = at(23040, KT * T, KT)
        ACC, RS = at(27648, T), at(28224, T)
        SQ = [U[:, FT - 2], U[:, FT - 1]]
        SQX, ACCX, RSX = [X[:, 0], X[:, 1]], X[:, 2], X[:, 3]
        Z = at(0, KT * T, KT)

        IDENT, ONES = con[:, C_IDENT:C_IDENT + P], con[:, C_ONES:C_ONES + P]
        HEADSUM, ROT = con[:, C_HEADSUM:C_HEADSUM + P], con[:, C_ROT:C_ROT + P]
        COS, SIN, RESET = con[:, C_COS:C_COS + T], con[:, C_SIN:C_SIN + T], con[:, C_RESET:C_RESET + T]
        EPS_C = con[:, C_EPS:C_EPS + 1]
        NMAX, SUM, REC = small[:, 0:3], small[:, 4:7], small[:, 8:11]
        NMAXS, SUMS, RECS = small[:, 12:14], small[:, 14:16], small[:, 16:18]
        LB, OMLB, LBT = small[:, 20:22], small[:, 22:24], small[:, 24:32]

        pair = [ctx.enter_context(nc.psum_tensor(f"pair{i}", [P, 2, 512], F32)) for i in range(2)]
        bank = [pair[0][:, 0], pair[0][:, 1], pair[1][:, 0], pair[1][:, 1]] + \
               [ctx.enter_context(nc.psum_tensor(f"bank{i}", [P, 512], F32))[:, :] for i in range(4, 8)]

        s_con, s_x = ctx.enter_context(nc.semaphore("s_con")), ctx.enter_context(nc.semaphore("s_x"))
        s_y = ctx.enter_context(nc.semaphore("s_y"))
        copied = ctx.enter_context(nc.semaphore("copied"))
        s_par, s_pt, s_s0 = sem("s_par"), sem("s_pt"), sem("s_s0")
        w_landed = [sem(f"w_landed{i}") for i in range(RING)]
        down_part = sem("down_part")
        lin_mm, lin_ev = sem("lin_mm"), sem("lin_ev")
        act_steps, dve_steps, pool_steps = sem("act_steps"), sem("dve_steps"), sem("pool_steps")
        sq_pre, xn_ready, rs_ready = sem("sq_pre"), sem("xn_ready"), sem("rs_ready")
        acc_ready = sem("acc_ready")
        hf_sig, f_ready, z_log, g_ready, b_ready = (sem(n) for n in ("hf_sig", "f_ready", "z_log", "g_ready", "b_ready"))
        lb_exp = sem("lb_exp")
        eb_exp, qi_ready, kd_diff, kd_exp, kd_ready = (sem(n) for n in ("eb_exp", "qi_ready", "kd_diff", "kd_exp", "kd_ready"))
        kdt_mm, kdt_ev = sem("kdt_mm"), sem("kdt_ev")
        u_mm, u_ev = sem("u_mm"), sem("u_ev")
        in_mm, in_ev = sem("in_mm"), sem("in_ev")
        vx_ready, us_mm, us_ev = sem("vx_ready"), sem("us_mm"), sem("us_ev")
        oi_zero, at_zero, qb_zero = sem("oi_zero"), sem("at_zero"), sem("qb_zero")
        st_out = sem("st_out")
        lv_diff, lv_exp, lv_ready = sem("lv_diff"), sem("lv_exp"), sem("lv_ready")
        lv_mm, lv_ev, ls_mm, ls_ev = sem("lv_mm"), sem("lv_ev"), sem("ls_mm"), sem("ls_ev")
        ia_mm, o_ready = sem("ia_mm"), sem("o_ready")
        gate_sig, gate_ready, sqo = sem("gate_sig"), sem("gate_ready"), sem("sqo")
        rot_ready, qb_ready, kv_out = sem("rot_ready"), sem("qb_ready"), sem("kv_out")
        ps_mm, ps_max, ps_exp, ps_p = sem("ps_mm"), sem("ps_max"), sem("ps_exp"), sem("ps_p")
        pt_mm, pt_ev = sem("pt_mm"), sem("pt_ev")
        k_landed, v_landed = [[sem(f"{n}_landed{i}") for i in range(2)] for n in "kv"]
        ss_mm, ss_max, ss_exp, ss_p = sem("ss_mm"), sem("ss_max"), sem("ss_exp"), sem("ss_p")
        sp_mm, sp_ev, so_mm, os_ev, st_mm, so_ev = (sem(n) for n in ("sp_mm", "sp_ev", "so_mm", "os_ev", "st_mm", "so_ev"))
        sqa, att_ready = sem("sqa"), sem("att_ready")
        sq_mix, sq_h, h_mix, xm_ready = sem("sq_mix"), sem("sq_h"), sem("h_mix"), sem("xm_ready")
        u_relu, u_ready = sem("u_relu"), sem("u_ready")
        sq_down, h_down, z_ready, h_new = sem("sq_down"), sem("h_down"), sem("z_ready"), sem("h_new")

        first, last = min(s.num for s in sems), max(s.num for s in sems)
        assert last - first + 1 == len(sems)

        def used_up(r):
            if r < R_V:
                return lin_mm, Q[IN1[r]] + 1
            if r < R_IN2:
                return lin_mm, Q[f"v{(r - R_V) // 4}{TT}"] + 1
            if r < R_OUT:
                return lin_mm, Q[IN2[r - R_IN2]] + 1
            if r < R_PLE:
                return lin_mm, Q[f"out{r - R_OUT}"] + 1
            if r < R_UP:
                return lin_mm, Q[f"ple{4 * (r - R_PLE) + 3}"] + 1
            if r < R_DOWN:
                return lin_mm, Q[f"up{r - R_UP}"] + 1
            if r < R_GATE:
                k, j = divmod(r - R_DOWN, 4)
                return (down_part, 3 * k + j + 1) if j < 3 else (lin_mm, Q[f"down{k}"] + 1)
            return lin_mm, Q[f"gate{r - R_GATE}"] + 1

        def blocks(tile, h, half):
            if 2 * h <= DEC_SEQ:
                v = tile.rearrange("p r (n w) -> p (r n) w", w=2 * h)
                n = 4 * T // (2 * h)
                return v[:, :, half * h:half * h + h], v[:, :, h - 1:h].to_broadcast([P, n, h])
            v = tile[:, :, 0:SEQ].rearrange("p r (n w) -> p r n w", w=2 * h)
            return v[:, :, :, half * h:half * h + h], v[:, :, :, h - 1:h].to_broadcast([P, 4, SEQ // (2 * h), h])

        def last_of(tile, sample):
            if sample:
                return tile[:, :, SEQ:T].rearrange("p r (n w) -> p r n w", w=DEC_SEQ)[:, :, :, DEC_SEQ - 1:DEC_SEQ]
            return tile[:, :, 0:SEQ].rearrange("p r (n w) -> p r n w", w=CH)[:, :, :, CH - 1:CH]

        def chunks_of(tile, sample):
            if sample:
                return tile[:, :, SEQ:T].rearrange("p r (n w) -> p r n w", w=DEC_SEQ)
            return tile[:, :, 0:SEQ].rearrange("p r (n w) -> p r n w", w=CH)

        def v_cols(h):
            return 64 * h

        with nc.Block() as block:
            @block.sync
            def _(sp):
                sp.dma_start(con[:, :], consts).then_inc(s_con, 16)
                sp.dma_start(h_sb[:, :], x_t).then_inc(s_x, 16)
                sp.wait_ge(s_con, 16)
                sp.wait_ge(s_x, 16)

        with nc.Fori(0, DEPTH) as layer:
            with nc.Block() as block:
                def of_layer(dram, *rest):
                    names = "abcde"[:len(dram.shape) - 1]
                    s = " ".join(names)
                    flat = dram[bass.ds(layer, 1)].rearrange(f"l {s} -> (l {names[0]}) {' '.join(names[1:])}")
                    return flat

                @block.sync
                def _(sp):
                    sp.dma_start(par[:, :], of_layer(params)).then_inc(s_par, 16)

                    def unit(r):
                        if r >= RING:
                            sp.wait_ge(*used_up(r - RING))
                        sp.dma_start(ring_sb[:, (r % RING) * 1024:(r % RING + 1) * 1024],
                                     of_layer(w_units)[r * P:(r + 1) * P, :]).then_inc(w_landed[r % RING], 16)

                    for r in range(RING):
                        unit(r)
                    sp.dma_start(pt_sb[:, :], of_layer(p_t)).then_inc(s_pt, 16)
                    sp.wait_ge(xn_ready, KT)
                    sp.dma_start(at(27072, 2048), of_layer(s0_in)).then_inc(s_s0, 16)
                    for r in range(RING, R_IN2):
                        unit(r)
                    sp.wait_ge(u_ev, NC)
                    sp.dma_start(of_layer(sp_out), at(25024 + (NC - 1) * 256, 256)).then_inc(st_out, 16)
                    sp.wait_ge(us_ev, 4)
                    sp.dma_start(of_layer(ss_out), at(27072, 2048)).then_inc(st_out, 16)
                    for r in range(R_IN2, R_PLE):
                        unit(r)
                    sp.wait_ge(rot_ready, 6)
                    qk = at(22720, 6 * T, 6)
                    sp.dma_start(of_layer(kp_out).rearrange("p (c t) -> p c t", c=3), qk[:, 3:6, 0:SEQ]).then_inc(kv_out, 16)
                    sp.dma_start(of_layer(kn_out).rearrange("p (c t) -> p c t", c=3), qk[:, 3:6, SEQ:T]).then_inc(kv_out, 16)
                    sp.dma_start(of_layer(vp_out).rearrange("p (c t) -> p c t", c=TT), V[:, 0:TT, 640:1024]).then_inc(kv_out, 16)
                    sp.dma_start(of_layer(vn_out), V[0:NEW, TT, 640:1024]).then_inc(kv_out, 16)
                    for b in range(DEC_BATCH):
                        if b == 0:
                            sp.wait_ge(gate_ready, 6)
                        if b >= 2:
                            sp.wait_ge(ss_mm, b - 1)
                        sp.dma_start(KB[b % 2], of_layer(ck)[b * 384:(b + 1) * 384, 0:KEYS]
                                     .rearrange("(c p) n -> p c n", p=P)).then_inc(k_landed[b % 2], 16)
                        if b >= 2:
                            sp.wait_ge(so_mm, b - 1)
                        sp.dma_start(VB[b % 2], of_layer(cv)[b * WIN:b * WIN + KEYS, :]
                                     .rearrange("(c p) n -> p c n", p=P)).then_inc(v_landed[b % 2], 16)
                    for r in range(R_PLE, UNITS):
                        unit(r)
                    sp.wait_ge(st_out, 32)
                    sp.wait_ge(kv_out, 64)

                @block.gpsimd
                def _(pool):
                    nc.gpsimd.memset(OI[:, :, 0:CH], 0.0).then_inc(oi_zero, 1)

                    def copy_cache(b):
                        pool.dma_start(of_layer(ck_out)[b * 384:(b + 1) * 384, :],
                                       of_layer(ck)[b * 384:(b + 1) * 384, DEC_SEQ:WIN]).then_inc(copied, 16)
                        pool.dma_start(of_layer(cv_out)[b * KEPT:(b + 1) * KEPT, :],
                                       of_layer(cv)[b * WIN + DEC_SEQ:(b + 1) * WIN, :]).then_inc(copied, 16)

                    pool.wait_ge(lin_mm, 2)
                    copy_cache(0)
                    for h in range(HEADS):
                        if h == 0:
                            pool.wait_ge(lin_ev, Q["v14"] + 1)
                            pool.wait_ge(qi_ready, 1)
                        if h >= 2:
                            pool.wait_ge(us_mm, h - 1)
                        vx = VX[h % 2][0:NEW].rearrange("p a (b v) -> p (a b) v", v=64)
                        nc.gpsimd.tensor_tensor(
                            vx, V[0:NEW, TT, v_cols(h):v_cols(h) + 64].rearrange("p (a v) -> p a v", a=1).to_broadcast([NEW, DEC_BATCH, 64]),
                            con[0:NEW, C_BATCH:C_BATCH + DEC_BATCH].rearrange("p (b a) -> p b a", a=1).to_broadcast([NEW, DEC_BATCH, 64]),
                            ALU.mult).then_inc(vx_ready, 1)
                    pool.wait_ge(us_mm, HEADS)
                    nc.gpsimd.memset(at(16640, 3200), 0.0).then_inc(at_zero, 1)
                    copy_cache(1)
                    pool.wait_ge(ia_mm, 5)
                    nc.gpsimd.memset(V[:, 0, 0:T], 0.0).then_inc(qb_zero, 1)
                    nc.gpsimd.memset(V[:, 1, 0:T], 0.0).then_inc(qb_zero, 1)
                    for b in range(2, DEC_BATCH):
                        pool.wait_ge(*used_up(R_OUT + (b - 2) * 10))
                        copy_cache(b)

                @block.tensor
                def _(pe):
                    def claim(name):
                        q = Q[name]
                        if q >= 2:
                            pe.wait_ge(lin_ev, q - 1)
                        return pair[q % 2]

                    def land(r):
                        pe.wait_ge(w_landed[r % RING], 16 * (r // RING + 1))

                    def linear(name, units, src, kts, blocks_of=None, m=P):
                        ps = claim(name)
                        n = 0
                        for i, r in enumerate(units):
                            land(r)
                            for half in range(2):
                                for k in range(len(kts)):
                                    kk = i * len(kts) + k
                                    mm = nc.tensor.matmul(ps[:, half, 0:HALF], W[:, r % RING, kts[k], :],
                                                          src[:, kk, half * HALF:(half + 1) * HALF],
                                                          start=kk == 0, stop=kk == len(kts) * len(units) - 1)
                            if i < len(units) - 1:
                                mm.then_inc(down_part, 1)
                        return mm

                    def total(name, lhsT, tiles, ready):
                        ps = claim(name)
                        pe.wait_ge(*ready)
                        for half in range(2):
                            for i, t in enumerate(tiles):
                                mm = nc.tensor.matmul(ps[:, half, 0:HALF], lhsT, t[:, half * HALF:(half + 1) * HALF],
                                                      start=i == 0, stop=i == len(tiles) - 1)
                        mm.then_inc(lin_mm, 1)

                    def project(name, r, src, kts=range(KT)):
                        linear(name, [r], src, list(kts)).then_inc(lin_mm, 1)

                    total("sum_pre", ONES, [ACC], (acc_ready, 1))
                    for i, name in enumerate(IN1):
                        if i == 0:
                            pe.wait_ge(xn_ready, KT)
                        project(name, R_IN1 + i, X)
                        if name == "gq1":
                            pe.wait_ge(s_par, 16)
                            pe.wait_ge(lin_ev, Q["gq1"] + 1)
                            for z in range(2):
                                ps = claim(f"z{z}")
                                for half in range(2):
                                    mm = nc.tensor.matmul(ps[:, half, 0:HALF], par[64:80, W_G2 + P * z:W_G2 + P * (z + 1)],
                                                          Q4[64:80, 3, half * HALF:(half + 1) * HALF], start=True, stop=True)
                                mm.then_inc(lin_mm, 1)
                    for g in range(2):
                        for j in range(4):
                            land(R_V + 4 * g + j)
                        for tt in range(TT + 1):
                            m = P if tt < TT else NEW
                            ps = claim(f"v{g}{tt}")
                            for k in range(KT):
                                r = R_V + 4 * g + k // 2
                                mm = nc.tensor.matmul(ps[0:m, 0, :], X[:, k, tt * P:tt * P + m],
                                                      ring_sb[:, (r % RING) * 1024 + (k % 2) * 512:(r % RING) * 1024 + (k % 2) * 512 + 512],
                                                      start=k == 0, stop=k == KT - 1)
                            mm.then_inc(lin_mm, 1)

                    pe.wait_ge(kd_ready, 1)
                    for tt in range(TT + 1):
                        m = P if tt < TT else NEW
                        if tt >= 2:
                            pe.wait_ge(kdt_ev, tt - 1)
                        for r in range(4):
                            mm = nc.tensor.transpose(bank[4 + tt % 2][0:m, r * P:(r + 1) * P],
                                                     LV[0][:, r, tt * P:tt * P + m], IDENT)
                        mm.then_inc(kdt_mm, 1)
                    pe.wait_ge(lin_ev, Q[f"v1{TT}"] + 1)
                    for c in range(NC):
                        par_, tt = c % 2, c // 2
                        if c < 4:
                            pe.wait_ge(kdt_ev, TT + 1)
                        else:
                            pe.wait_ge(u_ev, c - 3)
                        rows = slice(64 * par_, 64 * par_ + 64)
                        for h in range(HEADS + 2):
                            r, row, n = HEAD_AT[h] if h < HEADS else (3, 64 + 32 * (h - HEADS), 32)
                            mm = nc.tensor.matmul(bank[4 + c % 4][row:row + n, r * 64:(r + 1) * 64],
                                                  KDT[rows, tt, r * P + row:r * P + row + n],
                                                  V[rows, tt, v_cols(h % HEADS):v_cols(h % HEADS) + 64],
                                                  start=True, stop=True)
                        mm.then_inc(u_mm, 1)
                    pe.wait_ge(qi_ready, 1)
                    pe.wait_ge(s_s0, 16)
                    for h in range(HEADS):
                        r, row, n = HEAD_AT[h]
                        o = 64 * (h % 2)
                        b_ = bank[4 + h % 2]
                        if h == 0:
                            pe.wait_ge(u_ev, NC)
                        if h >= 2:
                            pe.wait_ge(in_ev, h - 1)
                        for b in range(DEC_BATCH):
                            nc.tensor.matmul(b_[o:o + 64, b * DEC_SEQ:(b + 1) * DEC_SEQ], S0[row:row + n, b, r, :],
                                             QI[row:row + n, r, SEQ + b * DEC_SEQ:SEQ + (b + 1) * DEC_SEQ],
                                             start=True, stop=True)
                        for c in range(1, NC):
                            mm = nc.tensor.matmul(b_[o:o + 64, c * CH:(c + 1) * CH], SC[row:row + n, c - 1, r, :],
                                                  QI[row:row + n, r, c * CH:(c + 1) * CH], start=True, stop=True)
                        mm.then_inc(in_mm, 1)
                    for h in range(HEADS):
                        r, row, n = HEAD_AT[h]
                        if r >= 2 and row == 0:
                            pe.wait_ge(us_ev, r - 1)
                        pe.wait_ge(vx_ready, h + 1)
                        nc.tensor.matmul(bank[6 + r % 2][row:row + n, :], KDT[0:NEW, TT, r * P + row:r * P + row + n],
                                         VX[h % 2][0:NEW, 0, :], start=True, stop=True).then_inc(us_mm, 1)

                    in2 = list(enumerate(IN2))
                    gi = si = 0
                    for l in range(len(LEVELS)):
                        if l == 0:
                            pe.wait_ge(in_ev, HEADS)
                            pe.wait_ge(us_ev, 4)
                            kq = (K4, Q4)
                        else:
                            pe.wait_ge(lv_ready, l)
                            kq = (LV[l % 2], LV[l % 2])
                        for g, heads in enumerate(GROUPS):
                            b_ = bank[4 + gi % 2]
                            if gi >= 2:
                                pe.wait_ge(lv_ev, gi - 1)
                            for i, h in enumerate(heads):
                                r, row, n = HEAD_AT[h]
                                for c in range(NC):
                                    o = 64 * (c % 2)
                                    col = (4 * i + c // 2) * CH
                                    mm = nc.tensor.matmul(b_[o:o + 64, col:col + CH],
                                                          kq[0][row:row + n, r, c * CH:(c + 1) * CH],
                                                          kq[1][row:row + n, r, c * CH:(c + 1) * CH], start=True, stop=True)
                            mm.then_inc(lv_mm, 1)
                            gi += 1
                            if l in SMALL:
                                b_ = bank[6 + si % 2]
                                if si >= 2:
                                    pe.wait_ge(ls_ev, si - 1)
                                for i, h in enumerate(heads):
                                    r, row, n = HEAD_AT[h]
                                    mm = nc.tensor.matmul(b_[0:NEW, i * CH:(i + 1) * CH], kq[0][row:row + n, r, SEQ:T],
                                                          kq[1][row:row + n, r, SEQ:T], start=True, stop=True)
                                mm.then_inc(ls_mm, 1)
                                si += 1
                        for _ in range(2 if l < 5 else 1):
                            if in2:
                                i, name = in2.pop(0)
                                project(name, R_IN2 + i, X)
                    assert not in2
                    for t in range(5):
                        ev, od = bank[4 + 2 * (t % 2)], bank[5 + 2 * (t % 2)]
                        if t == 0:
                            pe.wait_ge(lv_ev, gi)
                            pe.wait_ge(ls_ev, si)
                        if t >= 2:
                            pe.wait_ge(o_ready, t - 1)
                        for par_, b_ in ((0, ev), (1, od)):
                            rows = slice(64 * par_, 64 * par_ + 64)
                            for h in (2 * t, 2 * t + 1):
                                o = 64 * (h % 2)
                                for c in range(TT):
                                    mm = nc.tensor.matmul(b_[o:o + 64, c * CH:(c + 1) * CH],
                                                          V[rows, c, v_cols(h):v_cols(h) + 64], AT[rows, SLOT[h], c, :],
                                                          start=True, stop=True)
                                if par_ == 0:
                                    nc.tensor.matmul(b_[o:o + 64, TT * CH:(TT + 1) * CH],
                                                     V[0:NEW, TT, v_cols(h):v_cols(h) + 64], ATS[0:NEW, SLOT[h], :],
                                                     start=True, stop=True)
                        mm.then_inc(ia_mm, 1)
                    for i in range(5):
                        total(f"sum_o{i}", HEADSUM, [SQO[:, i]], (sqo, i + 1))
                    for i in range(6):
                        ps = claim(f"rot{i}")
                        for half in range(2):
                            mm = nc.tensor.matmul(ps[:, half, 0:HALF], ROT, ROTQK[:, i, half * HALF:(half + 1) * HALF],
                                                  start=True, stop=True)
                        mm.then_inc(lin_mm, 1)

                    pe.wait_ge(rot_ready, 6)
                    units = [(h, qt) for h in range(6) for qt in range(TT)]

                    def scores(i):
                        h, qt = units[i]
                        rows = slice(64 * (h % 2), 64 * (h % 2) + 64)
                        if i >= 2:
                            pe.wait_ge(ps_max, i - 1)
                        nc.tensor.matmul(bank[4 + i % 2][:, 0:(qt + 1) * P], ROTQK[rows, h // 2, qt * P:(qt + 1) * P],
                                         ROTQK[rows, 3 + h // 2, 0:(qt + 1) * P], start=True, stop=True).then_inc(ps_mm, 1)

                    def turn(i):
                        h, qt = units[i]
                        pe.wait_ge(ps_p, i + 1)
                        if i >= 2:
                            pe.wait_ge(pt_ev, i - 1)
                        for kt in range(qt + 1):
                            mm = nc.tensor.transpose(bank[6 + i % 2][:, kt * P:(kt + 1) * P],
                                                     SMP[i % 3][:, kt * P:(kt + 1) * P], IDENT)
                        mm.then_inc(pt_mm, 1)

                    def weigh(i):
                        h, qt = units[i]
                        name = f"pv{h // 2}"
                        if h % 2 == 0 and qt == 0:
                            claim(name)
                        ps = pair[Q[name] % 2]
                        o = 64 * (h % 2)
                        pe.wait_ge(pt_ev, i + 1)
                        for kt in range(qt + 1):
                            mm = nc.tensor.matmul(ps[o:o + 64, 0, qt * P:(qt + 1) * P],
                                                  V[:, kt, 640 + 64 * h:704 + 64 * h], PTP[i % 2][:, kt * P:(kt + 1) * P],
                                                  start=kt == 0, stop=kt == qt)
                        if h % 2 == 1 and qt == TT - 1:
                            mm.then_inc(lin_mm, 1)

                    n = len(units)
                    scores(0)
                    scores(1)
                    for i in range(n + 1):
                        if i + 2 < n:
                            scores(i + 2)
                        if i < n:
                            turn(i)
                        if i >= 1:
                            weigh(i - 1)

                    def s_scores(b):
                        kb = KB[b % 2]
                        if b == 0:
                            pe.wait_ge(qb_ready, 1)
                            pe.wait_ge(lin_ev, Q["pv2"] + 1)
                        else:
                            pe.wait_ge(ss_max, b)
                        pe.wait_ge(k_landed[b % 2], 16 * (b // 2 + 1))
                        for j, (lo, w) in enumerate(((0, 512), (512, 512), (1024, 256))):
                            for c in range(3):
                                mm = nc.tensor.matmul(bank[j][0:48, 0:w], qbd(b)[:, c, :], kb[:, c, lo:lo + w],
                                                      start=c == 0, stop=c == 2)
                        for c in range(3):
                            mm = nc.tensor.matmul(bank[3][0:48, 0:NEW], qbd(b)[:, c, :], ROTQK[:, 3 + c, SEQ:T],
                                                  start=c == 0, stop=c == 2)
                        mm.then_inc(ss_mm, 1)

                    def s_turn(b):
                        pe.wait_ge(ss_p, b + 1)
                        if b >= 1:
                            pe.wait_ge(sp_ev, b)
                        else:
                            pe.wait_ge(pt_ev, n)
                        for c in range(KC):
                            nc.tensor.transpose(bank[6][:, 48 * c:48 * c + 48], SMS[b % 2][0:48, c * P:(c + 1) * P],
                                                IDENT[0:48, 0:48])
                        nc.tensor.transpose(bank[5][0:NEW, 0:48], SMS[b % 2][0:48, KEYS:KEYS + NEW],
                                            IDENT[0:48, 0:48]).then_inc(sp_mm, 1)

                    def s_weigh(b):
                        pe.wait_ge(sp_ev, b + 1)
                        pe.wait_ge(v_landed[b % 2], 16 * (b // 2 + 1))
                        if b >= 1:
                            pe.wait_ge(os_ev, b)
                        for k in range(KC):
                            nc.tensor.matmul(bank[7][0:48, 0:384], PTB[b % 2][:, 48 * k:48 * k + 48],
                                             VB[b % 2][:, k, :], start=k == 0, stop=False)
                        nc.tensor.matmul(bank[7][0:48, 0:384], PTB[b % 2][0:NEW, 480:528], V[0:NEW, TT, 640:1024],
                                         start=False, stop=True).then_inc(so_mm, 1)

                    def s_back(b):
                        pe.wait_ge(os_ev, b + 1)
                        if b >= 1:
                            pe.wait_ge(so_ev, b)
                        for c in range(3):
                            mm = nc.tensor.transpose(bank[4][:, 48 * c:48 * c + 48], OS[b % 2][0:48, c * P:(c + 1) * P],
                                                     IDENT[0:48, 0:48])
                        mm.then_inc(st_mm, 1)

                    s_scores(0)
                    for b in range(DEC_BATCH):
                        if b + 1 < DEC_BATCH:
                            s_scores(b + 1)
                        if b >= 1:
                            s_back(b - 1)
                        s_turn(b)
                        s_weigh(b)
                    s_back(DEC_BATCH - 1)
                    total("sum_att", ONES, [SQA[:, i] for i in range(3)], (sqa, 3))

                    for k in range(KT):
                        if k == 0:
                            pe.wait_ge(att_ready, 1)
                        project(f"out{k}", R_OUT + k, X)
                    pe.wait_ge(s_pt, 16)

                    def ple(k):
                        r = R_PLE + k // 4
                        project(f"ple{k}", r, PT_IN, kts=[2 * (k % 4), 2 * (k % 4) + 1])

                    ple(0)
                    ple(1)
                    total("sum_mix", ONES, [ACC], (acc_ready, 2))
                    for k in range(2, KT):
                        ple(k)
                    total("sum_mlp", ONES, [ACC], (acc_ready, 3))
                    for k in range(FT):
                        if k == 0:
                            pe.wait_ge(xm_ready, KT)
                        project(f"up{k}", R_UP + k, X)
                    for k in range(KT):
                        if k == 0:
                            pe.wait_ge(u_ready, FT)
                        linear(f"down{k}", [R_DOWN + 4 * k + j for j in range(4)], U, list(range(KT))).then_inc(lin_mm, 1)
                    total("sum_down", ONES, [ACCX], (acc_ready, 4))
                    for k in range(KT):
                        if k == 0:
                            pe.wait_ge(h_down, KT)
                        project(f"gate{k}", R_GATE + k, H)

                @block.scalar
                def _(act):
                    st = Steps(act, act_steps)
                    A = nc.scalar.activation

                    def two(ap):
                        return ap.rearrange("p (a t) -> p a t", a=2)

                    def evac(name, dst, func=ACT.Copy, also=None, **kw):
                        act.wait_ge(lin_mm, Q[name] + 1)
                        ps = pair[Q[name] % 2][:, :, 0:HALF]
                        if also is not None:
                            A(two(also), ps, ACT.Square)
                        A(two(dst), ps, func, **kw).then_inc(lin_ev, 1)

                    def rstd(name, dst, scale):
                        act.wait_ge(lin_mm, Q[name] + 1)
                        A(two(dst), pair[Q[name] % 2][:, :, 0:HALF], ACT.Ln, scale=scale, bias=EPS_C).then_inc(lin_ev, 1)
                        act.wait_ge(lin_ev, Q[name] + 1)
                        A(dst, dst, ACT.Exp, scale=-0.5).then_inc(rs_ready, 1)

                    for k in range(KT):
                        dst = ACC if k == 0 else U[:, FT - 8 + k]
                        A(dst, H[:, k], ACT.Square).then_inc(sq_pre, 1)
                    rstd("sum_pre", RS, 1.0 / D_MODEL)
                    act.wait_ge(lb_exp, 1)
                    A(LBT[:, 2:6], LBT[:, 2:6], ACT.Exp).then_inc(lb_exp, 1)
                    evac("hf0", proj["hf0"])
                    evac("hf1", proj["hf1"])
                    act.wait_ge(lin_ev, Q["hf1"] + 1)
                    A(LV[0][:, 0:2], K4[:, 0:2], ACT.Sigmoid).then_inc(hf_sig, 1)
                    evac("gq1", proj["gq1"], scale=con[:, C_SCALE:C_SCALE + 1])
                    evac("z0", LV[1][:, 0], ACT.Identity, bias=par[:, W_B:W_B + 1])
                    evac("z1", LV[1][:, 1], ACT.Identity, bias=par[:, W_B + 1:W_B + 2])
                    evac("hq0", proj["hq0"])
                    evac("hq1", proj["hq1"])
                    act.wait_ge(lin_ev, Q["z1"] + 1)
                    st.step(A(LV[1][:, 2:4], LV[1][:, 0:2], ACT.Abs))
                    st.step(A(LV[1][:, 2:4], LV[1][:, 2:4], ACT.Exp, scale=-1.0))
                    A(LV[1][:, 2:4], LV[1][:, 2:4], ACT.Ln, bias=1.0).then_inc(z_log, 1)
                    act.wait_ge(f_ready, 1)
                    A(LV[0][:, 0:2], LV[0][:, 0:2], ACT.Ln).then_inc(g_ready, 1)
                    evac("gq0", proj["gq0"], scale=32.0 ** -0.5)
                    evac("gk0", proj["gk0"])
                    evac("gk1", proj["gk1"])

                    def values(g, tt):
                        name, m = f"v{g}{tt}", P if tt < TT else NEW
                        act.wait_ge(lin_mm, Q[name] + 1)
                        A(V[0:m, tt, 512 * g:512 * g + 512], pair[Q[name] % 2][0:m, 0, :], ACT.Copy).then_inc(lin_ev, 1)

                    for tt in range(TT + 1):
                        values(0, tt)
                    act.wait_ge(b_ready, 4)
                    A(LV[1], B, ACT.Exp).then_inc(eb_exp, 1)
                    act.wait_ge(kd_diff, 2)
                    A(LV[0], LV[0], ACT.Exp).then_inc(kd_exp, 1)
                    for tt in range(TT + 1):
                        values(1, tt)
                    for tt in range(TT + 1):
                        m = P if tt < TT else NEW
                        act.wait_ge(kdt_mm, tt + 1)
                        A(KDT[0:m, tt], bank[4 + tt % 2][0:m, :], ACT.Copy).then_inc(kdt_ev, 1)
                    for h in range(HEADS):
                        o, t = 64 * (h % 2), h // 2
                        act.wait_ge(in_mm, h + 1)
                        A(OI[o:o + 64, t, CH:SEQ], bank[4 + h % 2][o:o + 64, CH:SEQ], ACT.Copy)
                        A(OI[o:o + 64, t, SEQ:T], bank[4 + h % 2][o:o + 64, 0:NEW], ACT.Copy).then_inc(in_ev, 1)
                    in2 = list(IN2)
                    act.wait_ge(st_out, 32)
                    for l in range(len(LEVELS)):
                        if l + 1 < len(LEVELS):
                            act.wait_ge(lv_diff, l + 1)
                            v = LV[(l + 1) % 2]
                            v = v if (l + 1) in SMALL else v[:, :, 0:SEQ]
                            A(v, v, ACT.Exp).then_inc(lv_exp, 1)
                        for _ in range(2 if l < 5 else 1):
                            if in2:
                                name = in2.pop(0)
                                evac(name, proj[name])
                    act.wait_ge(lin_ev, Q["gr2"] + 1)
                    act.wait_ge(lv_mm, 6 * len(LEVELS))
                    A(ETMP, GATES, ACT.Sigmoid).then_inc(gate_sig, 1)
                    xo = [0, 1, 5, 6, 7]
                    for i in range(5):
                        act.wait_ge(o_ready, i + 1)
                        A(SQO[:, i], X[:, xo[i]], ACT.Square).then_inc(sqo, 1)
                    for i in range(5):
                        if i >= 2:
                            act.wait_ge(gate_ready, 1 + i - 1)
                        rstd(f"sum_o{i}", RSO[i % 2], 1.0 / 64)
                    for i in range(6):
                        if i >= 2:
                            act.wait_ge(rot_ready, i - 1)
                        evac(f"rot{i}", ROTMP[i % 2])

                    units = [(h, qt) for h in range(6) for qt in range(TT)]
                    n = len(units)

                    def p_exp(i):
                        w = (units[i][1] + 1) * P
                        act.wait_ge(ps_max, i + 1)
                        A(SMP[i % 3][:, 0:w], SMP[i % 3][:, 0:w], ACT.Exp, bias=NMAX[:, i % 3:i % 3 + 1],
                          accum_out=SUM[:, i % 3:i % 3 + 1]).then_inc(ps_exp, 1)

                    def p_turned(i):
                        w = (units[i][1] + 1) * P
                        act.wait_ge(pt_mm, i + 1)
                        A(PTP[i % 2][:, 0:w], bank[6 + i % 2][:, 0:w], ACT.Copy).then_inc(pt_ev, 1)

                    def p_out(t):
                        name = f"pv{t}"
                        act.wait_ge(lin_mm, Q[name] + 1)
                        A(X[:, 2 + t, 0:SEQ], pair[Q[name] % 2][:, 0, :], ACT.Copy).then_inc(lin_ev, 1)

                    for i in range(n + 1):
                        if i < n:
                            p_exp(i)
                        if i >= 1:
                            p_turned(i - 1)
                        if i >= 3 and (i - 3) % 8 == 7:
                            p_out((i - 3) // 8)
                    p_out(2)

                    def s_exp(b):
                        act.wait_ge(ss_max, b + 1)
                        A(SMS[b % 2][0:48, :], SMS[b % 2][0:48, :], ACT.Exp, bias=NMAXS[0:48, b % 2:b % 2 + 1],
                          accum_out=SUMS[0:48, b % 2:b % 2 + 1]).then_inc(ss_exp, 1)

                    def s_turned(b):
                        act.wait_ge(sp_mm, b + 1)
                        A(PTB[b % 2][:, 0:480], bank[6][:, 0:480], ACT.Copy)
                        A(PTB[b % 2][0:NEW, 480:528], bank[5][0:NEW, 0:48], ACT.Copy).then_inc(sp_ev, 1)

                    def s_outputs(b):
                        act.wait_ge(so_mm, b + 1)
                        A(OS[b % 2][0:48, :], bank[7][0:48, 0:384], ACT.Copy).then_inc(os_ev, 1)

                    s_exp(0)
                    for b in range(DEC_BATCH):
                        if b >= 1:
                            s_outputs(b - 1)
                        if b + 1 < DEC_BATCH:
                            s_exp(b + 1)
                        s_turned(b)
                    s_outputs(DEC_BATCH - 1)
                    for i in range(3):
                        act.wait_ge(so_ev, DEC_BATCH)
                        A(SQA[:, i], X[:, 2 + i], ACT.Square).then_inc(sqa, 1)
                    rstd("sum_att", RSA, 1.0 / 384)

                    act.wait_ge(kv_out, 64)
                    for k in range(KT):
                        evac(f"out{k}", Y[:, k], also=ACC if k == 0 else U[:, FT - 8 + k])
                    evac("ple0", PL[:, 0])
                    evac("ple1", PL[:, 1])
                    rstd("sum_mix", RS, 1.0 / D_MODEL)
                    order = [2, 3, 4, 5, 6, 7]
                    for k in range(KT):
                        if k < 6:
                            evac(f"ple{order[k]}", PL[:, order[k]])
                        act.wait_ge(h_mix, k + 1)
                        A(ACC if k == 0 else U[:, FT - 8 + k], H[:, k], ACT.Square).then_inc(sq_h, 1)
                    rstd("sum_mlp", RS, 1.0 / D_MODEL)
                    for k in range(FT):
                        evac(f"up{k}", U[:, k], ACT.Relu)
                    for k in range(KT):
                        evac(f"down{k}", Y[:, k], also=ACCX if k == 0 else SQX[k % 2])
                        if k >= 1 and k + 2 <= KT:
                            act.wait_ge(sq_down, k)
                    rstd("sum_down", RSX, 1.0 / D_MODEL)
                    for k in range(KT):
                        act.wait_ge(lin_mm, Q[f"gate{k}"] + 1)
                        A(two(Z[:, k]), pair[Q[f"gate{k}"] % 2][:, :, 0:HALF], ACT.Sigmoid).then_inc(lin_ev, 1)

                @block.vector
                def _(dve):
                    st = Steps(dve, dve_steps)
                    tt_, ts_, stt = nc.vector.tensor_tensor, nc.vector.tensor_scalar, nc.vector.scalar_tensor_tensor

                    dve.wait_ge(s_par, 16)
                    st.step(tt_(LBT[:, 0:2], par[:, W_LB:W_LB + 2], par[:, W_LB + 2:W_LB + 4], ALU.max))
                    st.mark(tt_(LBT[:, 2:4], par[:, W_LB:W_LB + 2], LBT[:, 0:2], ALU.subtract))
                    tt_(LBT[:, 4:6], par[:, W_LB + 2:W_LB + 4], LBT[:, 0:2], ALU.subtract).then_inc(lb_exp, 1)
                    dve.wait_ge(dve_steps, st.n)

                    def accumulate(acc, sqs, sem_, base=0):
                        for k in range(1, KT):
                            dve.wait_ge(sem_, base + k + 1)
                            ins = tt_(acc, acc, sqs(k), ALU.add)
                            if k < KT - 1:
                                st.step(ins)
                        ins.then_inc(acc_ready, 1)

                    def rstd(name):
                        dve.wait_ge(rs_ready, [n for n in LIN if n.startswith("sum")].index(name) + 1)

                    def spare(k):
                        return U[:, FT - 8 + k]

                    accumulate(ACC, spare, sq_pre)
                    rstd("sum_pre")
                    for k in range(KT):
                        stt(X[:, k], H[:, k], par[:, W_PRE + k:W_PRE + k + 1], RS, ALU.mult, ALU.mult).then_inc(xn_ready, 1)
                    dve.wait_ge(lb_exp, 2)
                    st.step(tt_(LBT[:, 6:8], LBT[:, 2:4], LBT[:, 4:6], ALU.add))
                    st.step(nc.vector.reciprocal(LBT[:, 6:8], LBT[:, 6:8]))
                    st.step(tt_(LBT[:, 6:8], LBT[:, 6:8], LBT[:, 4:6], ALU.mult))
                    st.step(ts_(LB, LBT[:, 6:8], par[:, W_FLAG:W_FLAG + 1], None, ALU.mult))
                    st.step(ts_(OMLB, LB, -1.0, 1.0, ALU.mult, ALU.add))
                    dve.wait_ge(hf_sig, 1)
                    f = LV[0][:, 0:2]
                    for i in range(2):
                        n = st.mark(ts_(f[:, i], f[:, i], OMLB[:, i:i + 1], LB[:, i:i + 1], ALU.mult, ALU.add))
                    st.after(n)
                    ts_(K4[:, 0:2], f, -1.0, 1.0, ALU.mult, ALU.add).then_inc(f_ready, 1)
                    dve.wait_ge(z_log, 1)
                    st.step(stt(LV[0][:, 2:4], LV[1][:, 0:2], 0.0, LV[1][:, 2:4], ALU.min, ALU.subtract))
                    st.step(ts_(LV[0][:, 2:4], LV[0][:, 2:4], 1.0 / 16, None, ALU.mult))
                    dve.wait_ge(g_ready, 1)
                    for r in range(4):
                        nc.vector.tensor_tensor_scan(B[:, r], RESET, LV[0][:, r], 0.0, ALU.mult, ALU.add).then_inc(b_ready, 1)
                    dve.wait_ge(b_ready, 4)
                    for s in range(2):
                        shape = [P, 4, NC, CH] if s == 0 else [P, 4, DEC_BATCH, DEC_SEQ]
                        tt_(chunks_of(LV[0], s), last_of(B, s).to_broadcast(shape), chunks_of(B, s),
                            ALU.subtract).then_inc(kd_diff, 1)
                    dve.wait_ge(eb_exp, 1)
                    dve.wait_ge(lin_ev, Q["gk1"] + 1)
                    n = st.mark(nc.vector.tensor_copy(EBL[:, :, 0:8], LV[1][:, :, CH - 1:SEQ:CH]))
                    n = st.mark(nc.vector.tensor_copy(EBL[:, :, 8:16], LV[1][:, :, SEQ + DEC_SEQ - 1:T:DEC_SEQ]))
                    st.after(n)
                    tt_(QI, Q4, LV[1], ALU.mult).then_inc(qi_ready, 1)
                    dve.wait_ge(kd_exp, 1)
                    tt_(LV[0], LV[0], K4, ALU.mult).then_inc(kd_ready, 1)
                    for c in range(NC):
                        add = bank[4 + c % 4][:, 0:256].rearrange("p (r v) -> p r v", r=4)
                        if c > 0:
                            st.step(tt_(SC[:, c], SC[:, c - 1],
                                        EBL[:, :, c:c + 1].to_broadcast([P, 4, 64]), ALU.mult))
                        dve.wait_ge(u_mm, c + 1)
                        ins = tt_(SC[:, c], SC[:, c], add, ALU.add) if c > 0 else nc.vector.tensor_copy(SC[:, c], add)
                        ins.then_inc(u_ev, 1)
                        dve.wait_ge(u_ev, c + 1)
                    dve.wait_ge(in_mm, HEADS)
                    for r in range(4):
                        n = P if r < 3 else 64
                        s = S0[0:n, :, r, :]
                        st.step(tt_(s, s, EBL[0:n, r, 8:16].rearrange("p (b a) -> p b a", a=1).to_broadcast([n, DEC_BATCH, 64]), ALU.mult))
                        dve.wait_ge(us_mm, [2, 4, 8, 10][r])
                        tt_(s, s, bank[6 + r % 2][0:n, :].rearrange("p (b v) -> p b v", v=64), ALU.add).then_inc(us_ev, 1)

                    def diff(l):
                        h, v = LEVELS[l], LV[l % 2]
                        (d0, _), (d1, _) = blocks(v, h, 0), blocks(v, h, 1)
                        (b0, mid), (b1, _) = blocks(B, h, 0), blocks(B, h, 1)
                        st.mark(tt_(d0, mid, b0, ALU.subtract))
                        tt_(d1, b1, mid, ALU.subtract).then_inc(lv_diff, 1)

                    def scale(l):
                        h, v = LEVELS[l], LV[l % 2]
                        dve.wait_ge(lv_exp, l)
                        d0, d1 = blocks(v, h, 0)[0], blocks(v, h, 1)[0]
                        n = st.mark(tt_(d0, d0, blocks(K4, h, 0)[0], ALU.mult))
                        st.after(n)
                        tt_(d1, d1, blocks(Q4, h, 1)[0], ALU.mult).then_inc(lv_ready, 1)

                    gi = si = 0

                    def pick(l):
                        nonlocal gi, si
                        mask = con[:, C_MASK + CH * l:C_MASK + CH * (l + 1)].bitcast(U32).rearrange("p (a t) -> p a t", a=1)
                        for g, heads in enumerate(GROUPS):
                            n, s = len(heads), FIRST_SLOT[g]
                            dve.wait_ge(lv_mm, gi + 1)
                            nc.vector.copy_predicated(
                                AT[:, s:s + n].rearrange("p s c t -> p (s c) t"), mask.to_broadcast([P, 4 * n, CH]),
                                bank[4 + gi % 2][:, 0:4 * n * CH].rearrange("p (a t) -> p a t", t=CH)).then_inc(lv_ev, 1)
                            gi += 1
                            if l in SMALL:
                                dve.wait_ge(ls_mm, si + 1)
                                nc.vector.copy_predicated(
                                    ATS[0:NEW, s:s + n], mask[0:NEW].to_broadcast([NEW, n, CH]),
                                    bank[6 + si % 2][0:NEW, 0:n * CH].rearrange("p (a t) -> p a t", t=CH)).then_inc(ls_ev, 1)
                                si += 1

                    dve.wait_ge(kdt_mm, TT + 1)
                    dve.wait_ge(us_mm, HEADS)
                    diff(1)
                    dve.wait_ge(at_zero, 1)
                    for l in range(1, len(LEVELS)):
                        pick(l - 1)
                        scale(l)
                        if l + 1 < len(LEVELS):
                            diff(l + 1)
                    pick(len(LEVELS) - 1)
                    xo = [0, 1, 5, 6, 7]
                    dve.wait_ge(in_ev, HEADS)
                    dve.wait_ge(oi_zero, 1)
                    for t in range(5):
                        dve.wait_ge(ia_mm, t + 1)
                        x = X[:, xo[t]]
                        for par_ in range(2):
                            o3 = x[:, 0:SEQ].rearrange("p (c a s) -> p a c s", a=2, s=CH)[:, par_]
                            i3 = OI[:, t, 0:SEQ].rearrange("p (c a s) -> p a c s", a=2, s=CH)[:, par_]
                            n = st.mark(tt_(o3, i3, bank[4 + 2 * (t % 2) + par_][:, 0:4 * CH].rearrange("p (c s) -> p c s", s=CH), ALU.add))
                        tt_(x[:, SEQ:T], OI[:, t, SEQ:T], bank[4 + 2 * (t % 2)][:, 4 * CH:5 * CH], ALU.add).then_inc(o_ready, 1)
                    dve.wait_ge(gate_sig, 1)
                    tt_(GATES, GATES, ETMP, ALU.mult).then_inc(gate_ready, 1)
                    dve.wait_ge(gate_ready, 1)
                    for i in range(5):
                        x, rs = X[:, xo[i]], RSO[i % 2]
                        rstd(f"sum_o{i}")
                        st.step(stt(x, x, par[:, W_O + xo[i]:W_O + xo[i] + 1], rs, ALU.mult, ALU.mult))
                        tt_(x, x, GATES[:, i], ALU.mult).then_inc(gate_ready, 1)
                    dve.wait_ge(gate_ready, 6)
                    for i in range(6):
                        dve.wait_ge(lin_ev, Q[f"rot{i}"] + 1)
                        n = st.mark(tt_(ROTMP[i % 2], ROTMP[i % 2], SIN, ALU.mult))
                        n = st.mark(tt_(ROTQK[:, i], ROTQK[:, i], COS, ALU.mult))
                        st.after(n)
                        tt_(ROTQK[:, i], ROTQK[:, i], ROTMP[i % 2], ALU.add).then_inc(rot_ready, 1)
                    dve.wait_ge(rot_ready, 6)
                    dve.wait_ge(qb_zero, 2)
                    for g in range(2):
                        for h in range(6):
                            c, hp = h // 2, h % 2
                            rows = slice(64 * hp, 64 * hp + 64)
                            dst = V[rows, g, 0:T].rearrange("p (b c n) -> p b c n", b=4, c=3)[:, :, c, 8 * h:8 * h + 8]
                            src = ROTQK[rows, c, SEQ + 32 * g:SEQ + 32 * g + 32].rearrange("p (b t) -> p b t", b=4)
                            n = st.mark(nc.vector.tensor_copy(dst, src))
                    st.after(n)
                    dve.sem_inc(qb_ready, 1)

                    units = [(h, qt) for h in range(6) for qt in range(TT)]
                    n_u = len(units)

                    def p_max(i):
                        h, qt = units[i]
                        w = (qt + 1) * P
                        dve.wait_ge(ps_mm, i + 1)
                        if i >= 3:
                            dve.wait_ge(pt_mm, i - 2)
                        st.step(stt(SMP[i % 3][:, 0:w], bank[4 + i % 2][:, 0:w], 0.125,
                                    con[:, C_BIAS + (3 - qt) * P:C_BIAS + 4 * P], ALU.mult, ALU.add))
                        nc.vector.tensor_reduce(NMAX[:, i % 3:i % 3 + 1], SMP[i % 3][:, 0:w], AX_X, ALU.max,
                                                negate=True).then_inc(ps_max, 1)

                    def p_norm(i):
                        w = (units[i][1] + 1) * P
                        dve.wait_ge(ps_exp, i + 1)
                        st.step(nc.vector.reciprocal(REC[:, i % 3:i % 3 + 1], SUM[:, i % 3:i % 3 + 1]))
                        ts_(SMP[i % 3][:, 0:w], SMP[i % 3][:, 0:w], REC[:, i % 3:i % 3 + 1], None, ALU.mult).then_inc(ps_p, 1)

                    for i in range(n_u + 1):
                        if i < n_u:
                            p_max(i)
                        if i >= 1:
                            p_norm(i - 1)

                    def s_max(b):
                        sm = SMS[b % 2]
                        dve.wait_ge(ss_mm, b + 1)
                        if b >= 2:
                            dve.wait_ge(sp_mm, b - 1)
                        for j, (lo, w) in enumerate(((0, 512), (512, 512), (1024, 256))):
                            n = st.mark(stt(sm[0:48, lo:lo + w], bank[j][0:48, 0:w], 0.125,
                                            con[0:48, C_SBIAS + lo:C_SBIAS + lo + w], ALU.mult, ALU.add))
                        st.step(stt(sm[0:48, KEYS:KEYS + NEW], bank[3][0:48, 0:NEW], 0.125,
                                    con[0:48, C_NBIAS + NEW * b:C_NBIAS + NEW * (b + 1)], ALU.mult, ALU.add))
                        nc.vector.tensor_reduce(NMAXS[0:48, b % 2:b % 2 + 1], sm[0:48, :], AX_X, ALU.max,
                                                negate=True).then_inc(ss_max, 1)

                    def s_norm(b):
                        sm = SMS[b % 2]
                        dve.wait_ge(ss_exp, b + 1)
                        st.step(nc.vector.reciprocal(RECS[0:48, b % 2:b % 2 + 1], SUMS[0:48, b % 2:b % 2 + 1]))
                        ts_(sm[0:48, :], sm[0:48, :], RECS[0:48, b % 2:b % 2 + 1], None, ALU.mult).then_inc(ss_p, 1)

                    def s_out(b):
                        dve.wait_ge(st_mm, b + 1)
                        for hp in range(2):
                            rows = slice(64 * hp, 64 * hp + 64)
                            src = bank[4][rows, 0:192].rearrange("p (c n) -> p c n", c=3)[:, :, 8 * hp:8 * hp + 8]
                            ins = nc.vector.tensor_copy(X[rows, 2:5, SEQ + 8 * b:SEQ + 8 * b + 8], src)
                            if hp == 0:
                                st.mark(ins)
                        ins.then_inc(so_ev, 1)

                    dve.wait_ge(pt_mm, n_u)
                    for b in range(DEC_BATCH + 1):
                        if b < DEC_BATCH:
                            s_max(b)
                        if b >= 2:
                            s_out(b - 2)
                        if b >= 1:
                            s_norm(b - 1)
                    s_out(DEC_BATCH - 1)
                    rstd("sum_att")
                    for i in range(3):
                        n = st.mark(stt(X[:, 2 + i], X[:, 2 + i], par[:, W_O + 2 + i:W_O + 3 + i], RSA, ALU.mult, ALU.mult))
                    st.after(n)
                    dve.sem_inc(att_ready, 1)

                    accumulate(ACC, spare, lin_ev, base=Q["out0"])
                    rstd("sum_mix")

                    def add_normed(k, w, rs, ready):
                        st.step(stt(Y[:, k], Y[:, k], par[:, w + k:w + k + 1], rs, ALU.mult, ALU.mult))
                        tt_(H[:, k], H[:, k], Y[:, k], ALU.add).then_inc(ready, 1)

                    for k in range(KT):
                        add_normed(k, W_MIX, RS, h_mix)
                        if k >= 2:
                            dve.wait_ge(sq_h, k)
                            st.step(tt_(ACC, ACC, spare(k - 1), ALU.add))
                    dve.wait_ge(sq_h, KT)
                    tt_(ACC, ACC, spare(KT - 1), ALU.add).then_inc(acc_ready, 1)
                    rstd("sum_mlp")
                    for k in range(KT):
                        stt(X[:, k], H[:, k], par[:, W_MLP + k:W_MLP + k + 1], RS, ALU.mult, ALU.mult).then_inc(xm_ready, 1)
                    for k in range(FT):
                        dve.wait_ge(lin_ev, Q[f"up{k}"] + 1)
                        tt_(U[:, k], U[:, k], U[:, k], ALU.mult).then_inc(u_ready, 1)
                    for k in range(1, KT):
                        dve.wait_ge(lin_ev, Q[f"down{k}"] + 1)
                        ins = tt_(ACCX, ACCX, SQX[k % 2], ALU.add)
                        if k < KT - 1:
                            ins.then_inc(sq_down, 1)
                            dve.wait_ge(sq_down, k)
                    ins.then_inc(acc_ready, 1)
                    rstd("sum_down")
                    for k in range(KT):
                        add_normed(k, W_DOWN, RSX, h_down)
                    for k in range(KT):
                        dve.wait_ge(lin_ev, Q[f"gate{k}"] + 1)
                        n = st.mark(tt_(Z[:, k], Z[:, k], PL[:, k], ALU.mult))
                    st.after(n)
                    for k in range(KT):
                        n = st.mark(tt_(H[:, k], H[:, k], Z[:, k], ALU.add))
                    st.after(n)

            nc.gpsimd.sem_clear(range(first, last + 1))
            nc.all_engine_barrier()

        with nc.Block() as block:
            @block.sync
            def _(sp):
                sp.dma_start(y_out, h_sb[:, :]).then_inc(s_y, 16)
                sp.wait_ge(s_y, 16)
                sp.wait_ge(copied, 16 * 2 * DEC_BATCH * DEPTH)


IN_SPLITS = (256, 256, 256, 256, 384, 384, 384, 192, 192, 384, 16, 384)
IN_NAMES = ("hq", "hf", "hi", "hg", "aq", "ak", "av", "gq", "gk", "gv", "lr", "gr")


def kernel(**inputs):
    import concourse.bacc as bacc
    from concourse.bass_utils import run_bass_kernel_spmd

    a = {k: np.asarray(v) for k, v in inputs.items()}
    f = np.float32

    def feature_major(x):
        n, d = x.shape
        return x.T.reshape(d // P, P, n).transpose(1, 0, 2).reshape(P, -1)

    def both(prompt, sample, d):
        return feature_major(np.concatenate([prompt.reshape(SEQ, d), sample.reshape(NEW, d)], 0))

    def units(w):
        k, n = w.shape
        return w.reshape(k // 1024, KT, P, n // P, P).transpose(3, 0, 2, 1, 4).reshape(-1, P, 1024)

    w_units = np.zeros((DEPTH, UNITS * P, 1024), f)
    par = np.zeros((DEPTH, P, W_END), f)
    s0 = np.zeros((DEPTH, P, DEC_BATCH, 4, 64), f)
    cols = dict(zip(IN_NAMES, np.split(np.arange(sum(IN_SPLITS)), np.cumsum(IN_SPLITS)[:-1])))
    for l in range(DEPTH):
        w = a["w_in"][l]
        tile_cols = {}
        for n in ("hf", "hq", "aq", "ak", "hg", "gr"):
            for i in range(len(cols[n]) // P):
                tile_cols[f"{n}{i}"] = cols[n][i * P:(i + 1) * P]
        tile_cols["gq0"], tile_cols["gk0"] = cols["gq"][:P], cols["gk"][:P]
        tile_cols["gq1"] = np.concatenate([cols["gq"][P:], cols["lr"]])
        tile_cols["gk1"] = cols["gk"][P:]
        u = []

        def in_unit(n):
            t = np.zeros((D_MODEL, P), f)
            t[:, :len(tile_cols[n])] = w[:, tile_cols[n]]
            u.append(units(t)[0])

        for n in IN1:
            in_unit(n)
        wv = w[:, np.concatenate([cols["hi"], cols["gv"], cols["av"]])]
        for g in range(2):
            for j in range(4):
                blk = wv[256 * j:256 * (j + 1), 512 * g:512 * (g + 1)]
                u.append(blk.reshape(2, P, 512).transpose(1, 0, 2).reshape(P, 1024))
        for n in IN2:
            in_unit(n)
        u.extend(units(a["w_out"][l]))
        wp = a["w_ple"][l].reshape(2, P, 2, 4, P).transpose(2, 1, 3, 0, 4).reshape(2, P, 1024)
        u.extend(wp)
        u.extend(units(a["w_up"][l]))
        u.extend(units(a["w_down"][l]))
        u.extend(units(a["w_ple_gate"][l]))
        assert len(u) == UNITS
        w_units[l] = np.concatenate(u, 0)

        def col(v):
            return v.reshape(-1, P).T

        par[l, :, W_PRE:W_PRE + 8] = col(a["norm_pre_mix"][l])
        par[l, :, W_MIX:W_MIX + 8] = col(a["norm_post_mix"][l])
        par[l, :, W_MLP:W_MLP + 8] = col(a["norm_pre_mlp"][l])
        par[l, :, W_DOWN:W_DOWN + 8] = col(a["norm_post_mlp"][l])
        par[l, :, W_O:W_O + 8] = col(np.concatenate([a["hgrn_norm"][l], a["attn_norm"][l], a["gla_norm"][l]]))
        par[l, :, W_B] = a["gla_b_gate"][l][:P]
        par[l, :64, W_B + 1] = a["gla_b_gate"][l][P:]
        for i in range(DEPTH):
            par[l, :, W_LB + 2 * i:W_LB + 2 * i + 2] = col(a["hgrn_lb"][i])
        par[l, :, W_FLAG] = l
        par[l, 64:80, W_G2:W_G2 + 192] = a["gla_w_gate2"][l]
        for h in range(4):
            r, row, n = HEAD_AT[h]
            s0[l, row:row + n, :, r] = a["state_hgrn"][l][:, h].transpose(1, 0, 2)
        for h in range(6):
            r, row, n = HEAD_AT[4 + h]
            s0[l, row:row + n, :, r] = a["state_gla"][l][:, h].transpose(1, 0, 2)
    order = cache_order()
    ck = a["cache_k"].reshape(DEPTH, DEC_BATCH, WIN, 384)[:, :, order].transpose(0, 1, 3, 2)
    cv = a["cache_v"].reshape(DEPTH, DEC_BATCH, WIN, 384)[:, :, order]
    arrays = {
        "x_t": both(a["x_prompt"], a["x_sample"], D_MODEL),
        "consts": constants(),
        "params": par,
        "p_t": np.stack([both(a["p_prompt"][l], a["p_sample"][l], 256) for l in range(DEPTH)]),
        "s0_in": s0.reshape(DEPTH, P, -1),
        "w_units": w_units,
        "ck": ck.reshape(DEPTH, DEC_BATCH * 384, WIN),
        "cv": cv.reshape(DEPTH, DEC_BATCH * WIN, 384),
    }
    arrays = {k: np.ascontiguousarray(v) for k, v in arrays.items()}
    outs = {
        "y_out": (P, KT * T), "kp_out": (DEPTH, P, 3 * SEQ), "kn_out": (DEPTH, P, 3 * NEW),
        "vp_out": (DEPTH, P, TT * 384), "vn_out": (DEPTH, NEW, 384),
        "ck_out": (DEPTH, DEC_BATCH * 384, KEPT), "cv_out": (DEPTH, DEC_BATCH * KEPT, 384),
        "sp_out": (DEPTH, P, 256), "ss_out": (DEPTH, P, 2048),
    }
    nc = bacc.Bacc("TRN2", target_bir_lowering=False, num_devices=1)
    args = {k: nc.dram_tensor(k, v.shape, F32, kind="ExternalInput").ap() for k, v in arrays.items()}
    args.update({k: nc.dram_tensor(k, s, F32, kind="ExternalOutput").ap() for k, s in outs.items()})
    build(nc, **args)
    r = run_bass_kernel_spmd(nc, [arrays], core_ids=[0]).results[0]

    y = r["y_out"].reshape(P, KT, T).transpose(2, 1, 0).reshape(T, D_MODEL)
    y_p = y[:SEQ].reshape(1, SEQ, D_MODEL)
    y_s = y[SEQ:].reshape(DEC_BATCH, DEC_SEQ, D_MODEL)

    def keys(x, n):
        return x.reshape(DEPTH, P, 3, n).transpose(0, 3, 2, 1).reshape(DEPTH, n, 6, 64)

    k_p = keys(r["kp_out"], SEQ)[:, None]
    v_p = r["vp_out"].reshape(DEPTH, P, TT, 384).transpose(0, 2, 1, 3).reshape(DEPTH, 1, SEQ, 6, 64)
    sp = r["sp_out"].reshape(DEPTH, P, 1, 4, 64)
    ss = r["ss_out"].reshape(DEPTH, P, DEC_BATCH, 4, 64)

    def states(s, heads):
        return np.stack([s[:, row:row + n, :, t].transpose(0, 2, 1, 3) for t, row, n in heads], 2)

    back = np.empty(KEPT, np.int64)
    back[order[DEC_SEQ:] - DEC_SEQ] = np.arange(KEPT)
    ck_n = r["ck_out"].reshape(DEPTH, DEC_BATCH, 384, KEPT)[:, :, :, back].transpose(0, 1, 3, 2)
    cv_n = r["cv_out"].reshape(DEPTH, DEC_BATCH, KEPT, 384)[:, :, back]
    kn = keys(r["kn_out"], NEW).reshape(DEPTH, DEC_BATCH, DEC_SEQ, 6, 64)
    vn = r["vn_out"].reshape(DEPTH, DEC_BATCH, DEC_SEQ, 6, 64)
    k_s = np.concatenate([ck_n.reshape(DEPTH, DEC_BATCH, KEPT, 6, 64), kn], 2)
    v_s = np.concatenate([cv_n.reshape(DEPTH, DEC_BATCH, KEPT, 6, 64), vn], 2)
    hg, gl = HEAD_AT[:4], HEAD_AT[4:]
    got = (y_p, y_s, states(sp, hg), states(sp, gl), k_p, v_p, states(ss, hg), states(ss, gl), k_s, v_s)
    return tuple(np.ascontiguousarray(x) for x in got)
```

```python
import math
from contextlib import ExitStack

import numpy as np

import concourse.bass as bass
from concourse import mybir
from concourse.alu_op_type import AluOpType as ALU

F32 = mybir.dt.float32
F32R = mybir.dt.float32r
U32 = mybir.dt.uint32
ACT = mybir.ActivationFunctionType
AX_X = mybir.AxisListType.X

P = 128
D_MODEL, DEPTH = 1024, 2
SEQ, DEC_BATCH, DEC_SEQ = 512, 8, 8
NEW = DEC_BATCH * DEC_SEQ
T = SEQ + NEW
HALF = T // 2
KT = D_MODEL // P
D_FF = 4 * D_MODEL
FT = D_FF // P
PAST, WIN = 4096, 2048
CH = 64
NC = SEQ // CH
TT = SEQ // P
EPS = 1e-6
ROPE_THETA = 500000.0
PATTERNS = ((128, 1), (512, 4), (2048, 16))
NEG = -1e30
KEYS = 1280
KC = KEYS // P
KEPT = WIN - DEC_SEQ

IN1 = ["hf0", "hf1", "gq1", "hq0", "hq1", "gq0", "gk0", "gk1"]
IN2 = ["aq0", "aq1", "aq2", "ak0", "ak1", "ak2", "hg0", "hg1", "gr0", "gr1", "gr2"]
R_IN1, R_V = 0, 8
R_IN2 = R_V + 8
R_OUT = R_IN2 + len(IN2)
R_PLE = R_OUT + KT
R_UP = R_PLE + 2
R_GATE = R_UP + 2 * FT
UNITS = R_GATE + KT
CHUNKS = FT // KT
RING = 8
RAW = 4
SPLITS = 3
SPLIT = list(range(R_OUT, R_PLE)) + list(range(R_UP, UNITS))

HEADS = 10
HEAD_AT = [(0, 0, 64), (0, 64, 64), (1, 0, 64), (1, 64, 64)] + \
          [(2, 32 * j, 32) for j in range(4)] + [(3, 0, 32), (3, 32, 32)]
GROUPS = [(0, 2), (1, 3), (4, 8), (5, 9), (6,), (7,)]
SLOT = {h: i for i, h in enumerate([h for g in GROUPS for h in g])}
FIRST_SLOT = [sum(len(g) for g in GROUPS[:i]) for i in range(len(GROUPS))]
LEVELS = [0, 1, 2, 4, 8, 16, 32]
SMALL = [l for l, h in enumerate(LEVELS) if 2 * h <= DEC_SEQ]

LIN = (["sum_pre", "hf0", "hf1", "gq1", "z0", "z1", "hq0", "hq1", "gq0", "gk0", "gk1"]
       + [f"v{g}{tt}" for g in range(2) for tt in range(TT + 1)]
       + IN2 + [f"sum_o{i}" for i in range(5)] + [f"rot{i}" for i in range(6)]
       + [f"pv{i}" for i in range(3)] + ["sum_att"]
       + [f"out{n}" for n in range(KT)] + ["sum_mix", "sum_mlp"] + [f"up{n}" for n in range(FT)]
       + ["sum_down"] + [f"gate{n}" for n in range(KT)])
Q = {name: i for i, name in enumerate(LIN)}
assert len(Q) == len(LIN)
SIDE = [f"ple{n}" for n in range(KT)] + [f"down{c}{n}" for c in range(CHUNKS) for n in range(KT)]
D = {name: i for i, name in enumerate(SIDE)}


def slot_of(r):
    return r % RING if r < R_OUT else (r - R_OUT) % RAW


def former(r):
    return max((q for q in range(r) if slot_of(q) == slot_of(r)), default=None)


def loads(r):
    return sum(slot_of(q) == slot_of(r) for q in range(r + 1))

C_IDENT, C_ONES, C_HEADSUM, C_ROT = 0, P, 2 * P, 3 * P
C_COS = 4 * P
C_SIN = C_COS + T
C_RESET = C_SIN + T
C_BIAS = C_RESET + T
C_MASK = C_BIAS + 4 * P
C_BATCH = C_MASK + len(LEVELS) * CH
C_SBIAS = C_BATCH + DEC_BATCH
C_NBIAS = C_SBIAS + KEYS
C_SCALE = C_NBIAS + DEC_BATCH * NEW
C_EPS = C_SCALE + 1
C_END = C_EPS + 1
W_PRE, W_MIX, W_MLP, W_DOWN, W_O = 0, 8, 16, 24, 32
W_B = 40
W_LB = 42
W_FLAG = 46
W_G2 = 47
W_END = W_G2 + 2 * P


def multiplicity(delta):
    m = np.zeros(delta.shape)
    for w, d in PATTERNS:
        m += (delta >= 0) & (delta <= w) & (delta % d == 0)
    return np.where(m > 0, np.log(np.maximum(m, 1)), NEG).astype(np.float32)


def cache_order():
    j = np.arange(WIN)
    wide = (j < WIN - 512) & (j % 16 < DEC_SEQ)
    read = np.concatenate([j[wide], j[j >= WIN - 512]])
    assert len(read) == KEYS and (read[:DEC_SEQ] == np.arange(DEC_SEQ)).all()
    return np.concatenate([read, j[(j < WIN - 512) & ~wide]])


def constants():
    c = np.zeros((P, C_END), np.float32)
    r = np.arange(P)
    c[:, C_IDENT:C_IDENT + P] = np.eye(P)
    c[:, C_ONES:C_ONES + P] = 1
    c[:, C_HEADSUM:C_HEADSUM + P] = (r[:, None] // 64 == r[None] // 64)
    d = r % 64
    rot = np.zeros((P, P), np.float32)
    for m in range(P):
        if d[m] < 8:
            rot[m + 8, m] = -1
        elif d[m] < 16:
            rot[m - 8, m] = 1
    c[:, C_ROT:C_ROT + P] = rot
    pos = np.concatenate([np.arange(SEQ), PAST + np.arange(NEW) % DEC_SEQ]).astype(np.float32)
    inv = np.exp((-math.log(ROPE_THETA) * np.arange(8, dtype=np.float32) * np.float32(2.0 / 16)).astype(np.float32))
    ang = (pos[None] * inv.astype(np.float32)[:, None]).astype(np.float32).astype(np.float64)
    c[:, C_COS:C_COS + T] = np.where(d[:, None] < 16, np.cos(ang)[d % 8], 1)
    c[:, C_SIN:C_SIN + T] = np.where(d[:, None] < 16, np.sin(ang)[d % 8], 0)
    t = np.arange(T)
    c[:, C_RESET:C_RESET + T] = np.where(t < SEQ, t % CH != 0, t % DEC_SEQ != 0)
    for j in range(4):
        c[:, C_BIAS + P * j:C_BIAS + P * (j + 1)] = multiplicity((3 - j) * P + r[:, None] - r[None])
    s, u = r % CH, np.arange(CH)
    for l, h in enumerate(LEVELS):
        m = (s[:, None] == u) if h == 0 else \
            (s[:, None] // (2 * h) == u // (2 * h)) & (s[:, None] % (2 * h) < h) & (u % (2 * h) >= h)
        c[:, C_MASK + CH * l:C_MASK + CH * (l + 1)] = m
    for b in range(DEC_BATCH):
        c[:NEW, C_BATCH + b] = (r[:NEW] // DEC_SEQ == b)
    q = np.arange(48) % DEC_SEQ
    c[:48, C_SBIAS:C_SBIAS + KEYS] = multiplicity(WIN + q[:, None] - cache_order()[None, :KEYS])
    n = np.arange(NEW)
    for b in range(DEC_BATCH):
        c[:48, C_NBIAS + NEW * b:C_NBIAS + NEW * (b + 1)] = \
            np.where(n // DEC_SEQ == b, multiplicity(q[:, None] - n[None] % DEC_SEQ), NEG)
    c[:, C_SCALE] = np.where(r < 64, 32.0 ** -0.5, 1)
    c[:, C_EPS] = EPS
    return c


class Steps:

    def __init__(self, eng, sem):
        self.eng, self.sem, self.n = eng, sem, 0

    def mark(self, ins):
        self.n += 1
        ins.then_inc(self.sem, 1)
        return self.n

    def step(self, ins):
        self.eng.wait_ge(self.sem, self.mark(ins))

    def after(self, n):
        self.eng.wait_ge(self.sem, n)


def build(nc, x_t, consts, params, p_t, s0_in, w_units, ck, cv,
          y_out, kp_out, kn_out, vp_out, vn_out, ck_out, cv_out, sp_out, ss_out):
    with ExitStack() as ctx:
        def sb(name, cols):
            return ctx.enter_context(nc.sbuf_tensor(name, [P, cols], F32))

        sems = []

        def sem(name):
            sems.append(ctx.enter_context(nc.semaphore(name)))
            return sems[-1]

        h_sb = sb("h", KT * T)
        x_sb = sb("x", KT * T)
        pt_sb = sb("pt", 2 * T)
        raw_sb = sb("raw", RAW * 1024)
        con = sb("con", C_END)
        par = sb("par", W_END)
        ebl_sb = sb("ebl", 4 * 16)
        small = sb("small", 64)
        H = h_sb[:, :].rearrange("p (k t) -> p k t", k=KT)
        X = x_sb[:, :].rearrange("p (k t) -> p k t", k=KT)
        PT_IN = pt_sb[:, :].rearrange("p (k t) -> p k t", k=2)
        EBL = ebl_sb[:, :].rearrange("p (r c) -> p r c", r=4)

        IDENT, ONES = con[:, C_IDENT:C_IDENT + P], con[:, C_ONES:C_ONES + P]
        HEADSUM, ROT = con[:, C_HEADSUM:C_HEADSUM + P], con[:, C_ROT:C_ROT + P]
        COS, SIN, RESET = con[:, C_COS:C_COS + T], con[:, C_SIN:C_SIN + T], con[:, C_RESET:C_RESET + T]
        EPS_C = con[:, C_EPS:C_EPS + 1]
        NMAX, SUM, REC = small[:, 0:3], small[:, 4:7], small[:, 8:11]
        NMAXS, SUMS, RECS = small[:, 12:14], small[:, 14:16], small[:, 16:19]
        LB, OMLB, LBT = small[:, 20:22], small[:, 22:24], small[:, 24:32]

        pair = [ctx.enter_context(nc.psum_tensor(f"pair{i}", [P, 2, 512], F32)) for i in range(4)]
        bank = [pair[i // 2][:, i % 2] for i in range(8)]

        s_con, s_x = ctx.enter_context(nc.semaphore("s_con")), ctx.enter_context(nc.semaphore("s_x"))
        s_y = ctx.enter_context(nc.semaphore("s_y"))
        copied = ctx.enter_context(nc.semaphore("copied"))
        s_par, s_pt, s_s0 = sem("s_par"), sem("s_pt"), sem("s_s0")
        w_landed = [sem(f"w_landed{i}") for i in range(RING)]
        w_hi, w_split = sem("w_hi"), sem("w_split")
        x_hi, x_split, u_sq, u_hi, u_split = (sem(n) for n in ("x_hi", "x_split", "u_sq", "u_hi", "u_split"))
        side_mm, side_ev = sem("side_mm"), sem("side_ev")
        act_steps_b, dve_steps_b = sem("act_steps_b"), sem("dve_steps_b")
        lin_mm, lin_ev = sem("lin_mm"), sem("lin_ev")
        act_steps, dve_steps, pool_steps = sem("act_steps"), sem("dve_steps"), sem("pool_steps")
        sq_pre, xn_ready, rs_ready = sem("sq_pre"), sem("xn_ready"), sem("rs_ready")
        acc_ready = sem("acc_ready")
        hf_sig, f_ready, z_log, g_ready, b_ready = (sem(n) for n in ("hf_sig", "f_ready", "z_log", "g_ready", "b_ready"))
        lb_exp = sem("lb_exp")
        eb_exp, qi_ready, kd_diff, kd_exp, kd_ready = (sem(n) for n in ("eb_exp", "qi_ready", "kd_diff", "kd_exp", "kd_ready"))
        kdt_mm, kdt_ev = sem("kdt_mm"), sem("kdt_ev")
        u_mm, u_ev = sem("u_mm"), sem("u_ev")
        in_mm, in_ev = sem("in_mm"), sem("in_ev")
        vx_ready, us_mm, us_ev = sem("vx_ready"), sem("us_mm"), sem("us_ev")
        oi_zero, at_zero, qb_zero = sem("oi_zero"), sem("at_zero"), sem("qb_zero")
        st_out = sem("st_out")
        lv_diff, lv_exp, lv_ready = sem("lv_diff"), sem("lv_exp"), sem("lv_ready")
        lv_mm, lv_ev, ls_mm, ls_ev = sem("lv_mm"), sem("lv_ev"), sem("ls_mm"), sem("ls_ev")
        ia_mm, o_ready = sem("ia_mm"), sem("o_ready")
        gate_sig, gate_ready, sqo = sem("gate_sig"), sem("gate_ready"), sem("sqo")
        rot_ready, qb_ready, kv_out = sem("rot_ready"), sem("qb_ready"), sem("kv_out")
        ps_mm, ps_max, ps_exp, ps_p = sem("ps_mm"), sem("ps_max"), sem("ps_exp"), sem("ps_p")
        pt_mm, pt_ev = sem("pt_mm"), sem("pt_ev")
        k_landed, v_landed = [[sem(f"{n}_landed{i}") for i in range(2)] for n in "kv"]
        ss_mm, ss_read, ss_max, ss_exp, ss_p = sem("ss_mm"), sem("ss_read"), sem("ss_max"), sem("ss_exp"), sem("ss_p")
        sp_mm, sp_ev, so_mm, os_ev, st_mm, so_ev = (sem(n) for n in ("sp_mm", "sp_ev", "so_mm", "os_ev", "st_mm", "so_ev"))
        sqa, att_ready = sem("sqa"), sem("att_ready")
        sq_mix, sq_h, h_mix = sem("sq_mix"), sem("sq_h"), sem("h_mix")
        acc_mix, acc_h, xm_ready = sem("acc_mix"), sem("acc_h"), sem("xm_ready")
        sq_down, acc_down, h_down, z_used = sem("sq_down"), sem("acc_down"), sem("h_down"), sem("z_used")

        first, last = min(s.num for s in sems), max(s.num for s in sems)
        assert last - first + 1 == len(sems)

        def used_up(r):
            if r < R_V:
                return lin_mm, Q[IN1[r]] + 1
            if r < R_IN2:
                return lin_mm, Q[f"v{(r - R_V) // 4}{TT}"] + 1
            if r < R_OUT:
                return lin_mm, Q[IN2[r - R_IN2]] + 1
            if r < R_PLE:
                return lin_mm, Q[f"out{r - R_OUT}"] + 1
            if r < R_UP:
                return side_mm, D[f"ple{4 * (r - R_PLE) + 3}"] + 1
            if r < R_GATE:
                c, j = divmod(r - R_UP, 2 * KT)
                return (lin_mm, Q[f"up{c * KT + j}"] + 1) if j < KT else (side_mm, D[f"down{c}{j - KT}"] + 1)
            return lin_mm, Q[f"gate{r - R_GATE}"] + 1

        def freed(r):
            return (w_split, SPLIT.index(r) + 1) if r in SPLIT else used_up(r)

        def blocks(tile, h, half):
            if 2 * h <= DEC_SEQ:
                v = tile.rearrange("p r (n w) -> p (r n) w", w=2 * h)
                n = 4 * T // (2 * h)
                return v[:, :, half * h:half * h + h], v[:, :, h - 1:h].to_broadcast([P, n, h])
            v = tile[:, :, 0:SEQ].rearrange("p r (n w) -> p r n w", w=2 * h)
            return v[:, :, :, half * h:half * h + h], v[:, :, :, h - 1:h].to_broadcast([P, 4, SEQ // (2 * h), h])

        def last_of(tile, sample):
            if sample:
                return tile[:, :, SEQ:T].rearrange("p r (n w) -> p r n w", w=DEC_SEQ)[:, :, :, DEC_SEQ - 1:DEC_SEQ]
            return tile[:, :, 0:SEQ].rearrange("p r (n w) -> p r n w", w=CH)[:, :, :, CH - 1:CH]

        def chunks_of(tile, sample):
            if sample:
                return tile[:, :, SEQ:T].rearrange("p r (n w) -> p r n w", w=DEC_SEQ)
            return tile[:, :, 0:SEQ].rearrange("p r (n w) -> p r n w", w=CH)

        def v_cols(h):
            return 64 * h

        with nc.Block() as block:
            @block.sync
            def _(sp):
                sp.dma_start(con[:, :], consts).then_inc(s_con, 16)
                sp.dma_start(h_sb[:, :], x_t).then_inc(s_x, 16)
                sp.wait_ge(s_con, 16)
                sp.wait_ge(s_x, 16)

        with nc.Fori(0, DEPTH) as layer:
            def of_layer(dram, *rest):
                names = "abcde"[:len(dram.shape) - 1]
                return dram[bass.ds(layer, 1)].rearrange(f"l {' '.join(names)} -> (l {names[0]}) {' '.join(names[1:])}")

            def copy_cache(pool, b):
                pool.dma_start(of_layer(ck_out)[b * 384:(b + 1) * 384, :],
                               of_layer(ck)[b * 384:(b + 1) * 384, DEC_SEQ:WIN]).then_inc(copied, 16)
                pool.dma_start(of_layer(cv_out)[b * KEPT:(b + 1) * KEPT, :],
                               of_layer(cv)[b * WIN + DEC_SEQ:(b + 1) * WIN, :]).then_inc(copied, 16)

            with nc.sbuf_tensor("arena", [P, 29184], F32) as arena, \
                    nc.sbuf_tensor("more", [P, (RING - RAW) * 1024], F32) as more_sb, nc.Block() as block:
                def at(off, n, count=None):
                    v = arena[:, off:off + n]
                    return v if count is None else v.rearrange("p (a t) -> p a t", a=count)

                Q4, K4 = at(0, 4 * T, 4), at(4 * T, 4 * T, 4)
                V = at(4608, 5 * 1024, 5)
                B = at(9728, 4 * T, 4)
                LV = [at(12032, 4 * T, 4), at(14336, 4 * T, 4)]
                KDT = at(16640, 5 * 512, 5)
                AT = at(16640, HEADS * 4 * CH).rearrange("p (s c t) -> p s c t", s=HEADS, c=4)
                ATS = at(19200, HEADS * CH, HEADS)
                OI = at(19840, 5 * T, 5)
                QI = at(22720, 4 * T, 4)
                SC = at(25024, NC * 256).rearrange("p (c r v) -> p c r v", c=NC, r=4)
                S0 = at(27072, DEC_BATCH * 256).rearrange("p (b r v) -> p b r v", b=DEC_BATCH, r=4)
                VX = [LV[1][:, 0:1, 0:512], LV[1][:, 1:2, 0:512]]
                ROTQK = at(22720, 6 * T, 6)
                GATES = at(26176, 5 * T, 5)
                proj = {"hf0": K4[:, 0], "hf1": K4[:, 1], "gq1": Q4[:, 3], "hq0": Q4[:, 0], "hq1": Q4[:, 1],
                        "gq0": Q4[:, 2], "gk0": K4[:, 2], "gk1": K4[:, 3]}
                for i, n in enumerate(IN2):
                    proj[n] = ROTQK[:, i] if i < 6 else GATES[:, i - 6]
                ETMP = at(0, 5 * T, 5)
                SQO = at(9728, 5 * T, 5)
                RSO = [at(12608, T), at(13184, T)]
                KB = [at(0, 3 * KEYS, 3), at(9728, 3 * KEYS, 3)]
                VB = [at(13568, KC * 384, KC), at(17408, KC * 384, KC)]
                PTB = [at(21248, 528), at(21776, 528)]
                PTP = [at(21248, 512), at(21760, 512)]
                SMP = [at(26176 + 512 * i, 512) for i in range(3)]
                SMS = [at(26176 + 1344 * i, 1344) for i in range(2)]
                OS = [at(3840 + 384 * i, 384) for i in range(2)]
                ROTMP = [V[:, 2, 0:T], V[:, 3, 0:T]]

                def qbd(b):
                    return V[:, b // 4, 144 * (b % 4):144 * (b % 4) + 144].rearrange("p (c n) -> p c n", c=3)

                SQA = at(0, 3 * T, 3)
                ACCA, RSA = at(3 * T, T), at(4 * T, T)
                ACC, RS = at(27648, T), at(28224, T)
                SQ = at(13824, KT * T, KT)

                def wslot(r):
                    i = slot_of(r)
                    return raw_sb[:, i * 1024:(i + 1) * 1024] if i < RAW else more_sb[:, (i - RAW) * 1024:(i - RAW + 1) * 1024]

                def load(sp, r):
                    if former(r) is not None:
                        sp.wait_ge(*freed(former(r)))
                    sp.dma_start(wslot(r), of_layer(w_units)[r * P:(r + 1) * P, :]).then_inc(w_landed[slot_of(r)], 16)

                @block.sync
                def _(sp):
                    sp.dma_start(par[:, :], of_layer(params)).then_inc(s_par, 16)

                    for r in range(RING):
                        load(sp, r)
                    sp.dma_start(pt_sb[:, :], of_layer(p_t)).then_inc(s_pt, 16)
                    sp.wait_ge(xn_ready, KT)
                    sp.dma_start(at(27072, 2048), of_layer(s0_in)).then_inc(s_s0, 16)
                    for r in range(RING, R_IN2):
                        load(sp, r)
                    sp.wait_ge(u_ev, NC)
                    sp.dma_start(of_layer(sp_out), at(25024 + (NC - 1) * 256, 256)).then_inc(st_out, 16)
                    sp.wait_ge(us_ev, 4)
                    sp.dma_start(of_layer(ss_out), at(27072, 2048)).then_inc(st_out, 16)
                    for r in range(R_IN2, R_OUT):
                        load(sp, r)
                    sp.wait_ge(rot_ready, 6)
                    qk = at(22720, 6 * T, 6)
                    sp.dma_start(of_layer(kp_out).rearrange("p (c t) -> p c t", c=3), qk[:, 3:6, 0:SEQ]).then_inc(kv_out, 16)
                    sp.dma_start(of_layer(kn_out).rearrange("p (c t) -> p c t", c=3), qk[:, 3:6, SEQ:T]).then_inc(kv_out, 16)
                    sp.dma_start(of_layer(vp_out).rearrange("p (c t) -> p c t", c=TT), V[:, 0:TT, 640:1024]).then_inc(kv_out, 16)
                    sp.dma_start(of_layer(vn_out), V[0:NEW, TT, 640:1024]).then_inc(kv_out, 16)
                    def load_keys(b):
                        if b >= 2:
                            sp.wait_ge(ss_mm, b - 1)
                        sp.dma_start(KB[b % 2], of_layer(ck)[b * 384:(b + 1) * 384, 0:KEYS]
                                     .rearrange("(c p) n -> p c n", p=P)).then_inc(k_landed[b % 2], 16)

                    def load_values(b):
                        if b >= 2:
                            sp.wait_ge(so_mm, b - 1)
                        sp.dma_start(VB[b % 2], of_layer(cv)[b * WIN:b * WIN + KEYS, :]
                                     .rearrange("(c p) n -> p c n", p=P)).then_inc(v_landed[b % 2], 16)

                    sp.wait_ge(gate_ready, 6)
                    load_keys(0)
                    load_keys(1)
                    load_values(0)
                    for b in range(2, DEC_BATCH):
                        load_keys(b)
                        load_values(b - 1)
                    load_values(DEC_BATCH - 1)
                    for r in range(R_OUT, R_OUT + RAW):
                        load(sp, r)
                    sp.wait_ge(st_out, 32)
                    sp.wait_ge(kv_out, 64)

                @block.gpsimd
                def _(pool):
                    nc.gpsimd.memset(OI[:, :, 0:CH], 0.0).then_inc(oi_zero, 1)

                    pool.wait_ge(lin_mm, 2)
                    copy_cache(pool, 0)
                    for h in range(HEADS):
                        if h == 0:
                            pool.wait_ge(lin_ev, Q["v14"] + 1)
                            pool.wait_ge(qi_ready, 1)
                        if h >= 2:
                            pool.wait_ge(us_mm, h - 1)
                        vx = VX[h % 2][0:NEW].rearrange("p a (b v) -> p (a b) v", v=64)
                        nc.gpsimd.tensor_tensor(
                            vx, V[0:NEW, TT, v_cols(h):v_cols(h) + 64].rearrange("p (a v) -> p a v", a=1).to_broadcast([NEW, DEC_BATCH, 64]),
                            con[0:NEW, C_BATCH:C_BATCH + DEC_BATCH].rearrange("p (b a) -> p b a", a=1).to_broadcast([NEW, DEC_BATCH, 64]),
                            ALU.mult).then_inc(vx_ready, 1)
                    pool.wait_ge(us_mm, HEADS)
                    nc.gpsimd.memset(at(16640, 3200), 0.0).then_inc(at_zero, 1)
                    copy_cache(pool, 1)
                    pool.wait_ge(ia_mm, 5)
                    nc.gpsimd.memset(V[:, 0, 0:T], 0.0).then_inc(qb_zero, 1)
                    nc.gpsimd.memset(V[:, 1, 0:T], 0.0).then_inc(qb_zero, 1)
                    pool.wait_ge(ss_mm, 8)
                    copy_cache(pool, 2)

                @block.tensor
                def _(pe):
                    def claim(name):
                        q = Q[name]
                        if q >= 2:
                            pe.wait_ge(lin_ev, q - 1)
                        return pair[q % 2]

                    def land(r):
                        pe.wait_ge(w_landed[slot_of(r)], 16 * loads(r))

                    def project(name, r):
                        ps = claim(name)
                        land(r)
                        for half in range(2):
                            for k in range(KT):
                                mm = nc.tensor.matmul(ps[:, half, 0:HALF], wslot(r)[:, k * P:(k + 1) * P],
                                                      X[:, k, half * HALF:(half + 1) * HALF], start=k == 0, stop=k == KT - 1)
                        mm.then_inc(lin_mm, 1)

                    def total(name, lhsT, tiles, ready):
                        ps = claim(name)
                        pe.wait_ge(*ready)
                        for half in range(2):
                            for i, t in enumerate(tiles):
                                mm = nc.tensor.matmul(ps[:, half, 0:HALF], lhsT, t[:, half * HALF:(half + 1) * HALF],
                                                      start=i == 0, stop=i == len(tiles) - 1)
                        mm.then_inc(lin_mm, 1)

                    total("sum_pre", ONES, [ACC], (acc_ready, 1))
                    for i, name in enumerate(IN1):
                        if i == 0:
                            pe.wait_ge(xn_ready, KT)
                        project(name, R_IN1 + i)
                        if name == "gq1":
                            pe.wait_ge(s_par, 16)
                            pe.wait_ge(lin_ev, Q["gq1"] + 1)
                            for z in range(2):
                                ps = claim(f"z{z}")
                                for half in range(2):
                                    mm = nc.tensor.matmul(ps[:, half, 0:HALF], par[64:80, W_G2 + P * z:W_G2 + P * (z + 1)],
                                                          Q4[64:80, 3, half * HALF:(half + 1) * HALF], start=True, stop=True)
                                mm.then_inc(lin_mm, 1)
                    for g in range(2):
                        for j in range(4):
                            land(R_V + 4 * g + j)
                        for tt in range(TT + 1):
                            m = P if tt < TT else NEW
                            ps = claim(f"v{g}{tt}")
                            for k in range(KT):
                                r = R_V + 4 * g + k // 2
                                mm = nc.tensor.matmul(ps[0:m, 0, :], X[:, k, tt * P:tt * P + m],
                                                      wslot(r)[:, (k % 2) * 512:(k % 2) * 512 + 512],
                                                      start=k == 0, stop=k == KT - 1)
                            mm.then_inc(lin_mm, 1)

                    pe.wait_ge(kd_ready, 1)
                    for tt in range(TT + 1):
                        m = P if tt < TT else NEW
                        if tt >= 2:
                            pe.wait_ge(kdt_ev, tt - 1)
                        for r in range(4):
                            mm = nc.tensor.transpose(bank[4 + tt % 2][0:m, r * P:(r + 1) * P],
                                                     LV[0][:, r, tt * P:tt * P + m], IDENT)
                        mm.then_inc(kdt_mm, 1)
                    pe.wait_ge(lin_ev, Q[f"v1{TT}"] + 1)
                    for c in range(NC):
                        par_, tt = c % 2, c // 2
                        if c < 4:
                            pe.wait_ge(kdt_ev, TT + 1)
                        else:
                            pe.wait_ge(u_ev, c - 3)
                        rows = slice(64 * par_, 64 * par_ + 64)
                        for h in range(HEADS + 2):
                            r, row, n = HEAD_AT[h] if h < HEADS else (3, 64 + 32 * (h - HEADS), 32)
                            mm = nc.tensor.matmul(bank[4 + c % 4][row:row + n, r * 64:(r + 1) * 64],
                                                  KDT[rows, tt, r * P + row:r * P + row + n],
                                                  V[rows, tt, v_cols(h % HEADS):v_cols(h % HEADS) + 64],
                                                  start=True, stop=True)
                        mm.then_inc(u_mm, 1)
                    pe.wait_ge(qi_ready, 1)
                    pe.wait_ge(s_s0, 16)
                    for h in range(HEADS):
                        r, row, n = HEAD_AT[h]
                        o = 64 * (h % 2)
                        b_ = bank[4 + h % 2]
                        if h == 0:
                            pe.wait_ge(u_ev, NC)
                        if h >= 2:
                            pe.wait_ge(in_ev, h - 1)
                        for b in range(DEC_BATCH):
                            nc.tensor.matmul(b_[o:o + 64, b * DEC_SEQ:(b + 1) * DEC_SEQ], S0[row:row + n, b, r, :],
                                             QI[row:row + n, r, SEQ + b * DEC_SEQ:SEQ + (b + 1) * DEC_SEQ],
                                             start=True, stop=True)
                        for c in range(1, NC):
                            mm = nc.tensor.matmul(b_[o:o + 64, c * CH:(c + 1) * CH], SC[row:row + n, c - 1, r, :],
                                                  QI[row:row + n, r, c * CH:(c + 1) * CH], start=True, stop=True)
                        mm.then_inc(in_mm, 1)
                    for h in range(HEADS):
                        r, row, n = HEAD_AT[h]
                        if r >= 2 and row == 0:
                            pe.wait_ge(us_ev, r - 1)
                        pe.wait_ge(vx_ready, h + 1)
                        nc.tensor.matmul(bank[6 + r % 2][row:row + n, :], KDT[0:NEW, TT, r * P + row:r * P + row + n],
                                         VX[h % 2][0:NEW, 0, :], start=True, stop=True).then_inc(us_mm, 1)

                    in2 = list(enumerate(IN2))
                    gi = si = 0
                    for l in range(len(LEVELS)):
                        if l == 0:
                            pe.wait_ge(in_ev, HEADS)
                            pe.wait_ge(us_ev, 4)
                            kq = (K4, Q4)
                        else:
                            pe.wait_ge(lv_ready, l)
                            kq = (LV[l % 2], LV[l % 2])
                        for g, heads in enumerate(GROUPS):
                            b_ = bank[4 + gi % 2]
                            if gi >= 2:
                                pe.wait_ge(lv_ev, gi - 1)
                            for i, h in enumerate(heads):
                                r, row, n = HEAD_AT[h]
                                for c in range(NC):
                                    o = 64 * (c % 2)
                                    col = (4 * i + c // 2) * CH
                                    mm = nc.tensor.matmul(b_[o:o + 64, col:col + CH],
                                                          kq[0][row:row + n, r, c * CH:(c + 1) * CH],
                                                          kq[1][row:row + n, r, c * CH:(c + 1) * CH], start=True, stop=True)
                            mm.then_inc(lv_mm, 1)
                            gi += 1
                            if l in SMALL:
                                b_ = bank[6 + si % 2]
                                if si >= 2:
                                    pe.wait_ge(ls_ev, si - 1)
                                for i, h in enumerate(heads):
                                    r, row, n = HEAD_AT[h]
                                    mm = nc.tensor.matmul(b_[0:NEW, i * CH:(i + 1) * CH], kq[0][row:row + n, r, SEQ:T],
                                                          kq[1][row:row + n, r, SEQ:T], start=True, stop=True)
                                mm.then_inc(ls_mm, 1)
                                si += 1
                        for _ in range(2 if l < 5 else 1):
                            if in2:
                                i, name = in2.pop(0)
                                project(name, R_IN2 + i)
                    assert not in2
                    for t in range(5):
                        ev, od = bank[4 + 2 * (t % 2)], bank[5 + 2 * (t % 2)]
                        if t == 0:
                            pe.wait_ge(lv_ev, gi)
                            pe.wait_ge(ls_ev, si)
                        if t >= 2:
                            pe.wait_ge(o_ready, t - 1)
                        for par_, b_ in ((0, ev), (1, od)):
                            rows = slice(64 * par_, 64 * par_ + 64)
                            for h in (2 * t, 2 * t + 1):
                                o = 64 * (h % 2)
                                for c in range(TT):
                                    mm = nc.tensor.matmul(b_[o:o + 64, c * CH:(c + 1) * CH],
                                                          V[rows, c, v_cols(h):v_cols(h) + 64], AT[rows, SLOT[h], c, :],
                                                          start=True, stop=True)
                                if par_ == 0:
                                    nc.tensor.matmul(b_[o:o + 64, TT * CH:(TT + 1) * CH],
                                                     V[0:NEW, TT, v_cols(h):v_cols(h) + 64], ATS[0:NEW, SLOT[h], :],
                                                     start=True, stop=True)
                        mm.then_inc(ia_mm, 1)
                    for i in range(5):
                        total(f"sum_o{i}", HEADSUM, [SQO[:, i]], (sqo, i + 1))
                    for i in range(6):
                        ps = claim(f"rot{i}")
                        for half in range(2):
                            mm = nc.tensor.matmul(ps[:, half, 0:HALF], ROT, ROTQK[:, i, half * HALF:(half + 1) * HALF],
                                                  start=True, stop=True)
                        mm.then_inc(lin_mm, 1)

                    pe.wait_ge(rot_ready, 6)
                    units = [(h, qt) for h in range(6) for qt in range(TT)]

                    def scores(i):
                        h, qt = units[i]
                        rows = slice(64 * (h % 2), 64 * (h % 2) + 64)
                        if i >= 2:
                            pe.wait_ge(ps_max, i - 1)
                        nc.tensor.matmul(bank[4 + i % 2][:, 0:(qt + 1) * P], ROTQK[rows, h // 2, qt * P:(qt + 1) * P],
                                         ROTQK[rows, 3 + h // 2, 0:(qt + 1) * P], start=True, stop=True).then_inc(ps_mm, 1)

                    def turn(i):
                        h, qt = units[i]
                        pe.wait_ge(ps_p, i + 1)
                        if i >= 2:
                            pe.wait_ge(pt_ev, i - 1)
                        for kt in range(qt + 1):
                            mm = nc.tensor.transpose(bank[6 + i % 2][:, kt * P:(kt + 1) * P],
                                                     SMP[i % 3][:, kt * P:(kt + 1) * P], IDENT)
                        mm.then_inc(pt_mm, 1)

                    def weigh(i):
                        h, qt = units[i]
                        name = f"pv{h // 2}"
                        if h % 2 == 0 and qt == 0:
                            claim(name)
                        ps = pair[Q[name] % 2]
                        o = 64 * (h % 2)
                        pe.wait_ge(pt_ev, i + 1)
                        for kt in range(qt + 1):
                            mm = nc.tensor.matmul(ps[o:o + 64, 0, qt * P:(qt + 1) * P],
                                                  V[:, kt, 640 + 64 * h:704 + 64 * h], PTP[i % 2][:, kt * P:(kt + 1) * P],
                                                  start=kt == 0, stop=kt == qt)
                        if h % 2 == 1 and qt == TT - 1:
                            mm.then_inc(lin_mm, 1)

                    n = len(units)
                    scores(0)
                    scores(1)
                    for i in range(n + 1):
                        if i + 2 < n:
                            scores(i + 2)
                        if i < n:
                            turn(i)
                        if i >= 1:
                            weigh(i - 1)

                    def s_scores(b):
                        kb = KB[b % 2]
                        if b == 0:
                            pe.wait_ge(qb_ready, 1)
                            pe.wait_ge(lin_ev, Q["pv2"] + 1)
                        else:
                            pe.wait_ge(ss_read, b)
                        pe.wait_ge(k_landed[b % 2], 16 * (b // 2 + 1))
                        for j, (lo, w) in enumerate(((0, 512), (512, 512), (1024, 256))):
                            for c in range(3):
                                mm = nc.tensor.matmul(bank[j][0:48, 0:w], qbd(b)[:, c, :], kb[:, c, lo:lo + w],
                                                      start=c == 0, stop=c == 2)
                        for c in range(3):
                            mm = nc.tensor.matmul(bank[3][0:48, 0:NEW], qbd(b)[:, c, :], ROTQK[:, 3 + c, SEQ:T],
                                                  start=c == 0, stop=c == 2)
                        mm.then_inc(ss_mm, 1)

                    def s_turn(b):
                        pe.wait_ge(ss_exp, b + 1)
                        if b >= 1:
                            pe.wait_ge(sp_ev, b)
                        else:
                            pe.wait_ge(pt_ev, n)
                        for c in range(KC):
                            nc.tensor.transpose(bank[6][:, 48 * c:48 * c + 48], SMS[b % 2][0:48, c * P:(c + 1) * P],
                                                IDENT[0:48, 0:48])
                        nc.tensor.transpose(bank[5][0:NEW, 0:48], SMS[b % 2][0:48, KEYS:KEYS + NEW],
                                            IDENT[0:48, 0:48]).then_inc(sp_mm, 1)

                    def s_weigh(b):
                        pe.wait_ge(sp_ev, b + 1)
                        pe.wait_ge(v_landed[b % 2], 16 * (b // 2 + 1))
                        if b >= 1:
                            pe.wait_ge(os_ev, b)
                        for k in range(KC):
                            nc.tensor.matmul(bank[7][0:48, 0:384], PTB[b % 2][:, 48 * k:48 * k + 48],
                                             VB[b % 2][:, k, :], start=k == 0, stop=False)
                        nc.tensor.matmul(bank[7][0:48, 0:384], PTB[b % 2][0:NEW, 480:528], V[0:NEW, TT, 640:1024],
                                         start=False, stop=True).then_inc(so_mm, 1)

                    def s_back(b):
                        pe.wait_ge(os_ev, b + 1)
                        if b >= 1:
                            pe.wait_ge(so_ev, b)
                        for c in range(3):
                            mm = nc.tensor.transpose(bank[4][:, 48 * c:48 * c + 48], OS[b % 2][0:48, c * P:(c + 1) * P],
                                                     IDENT[0:48, 0:48])
                        mm.then_inc(st_mm, 1)

                    s_scores(0)
                    for b in range(DEC_BATCH):
                        if b + 1 < DEC_BATCH:
                            s_scores(b + 1)
                        if b >= 1:
                            s_weigh(b - 1)
                        if b >= 2:
                            s_back(b - 2)
                        s_turn(b)
                    s_weigh(DEC_BATCH - 1)
                    s_back(DEC_BATCH - 2)
                    s_back(DEC_BATCH - 1)
                    total("sum_att", ONES, [SQA[:, i] for i in range(3)], (sqa, 3))

                @block.scalar
                def _(act):
                    st = Steps(act, act_steps)
                    A = nc.scalar.activation

                    def two(ap):
                        return ap.rearrange("p (a t) -> p a t", a=2)

                    def evac(name, dst, func=ACT.Copy, also=None, **kw):
                        act.wait_ge(lin_mm, Q[name] + 1)
                        ps = pair[Q[name] % 2][:, :, 0:HALF]
                        if also is not None:
                            A(two(also), ps, ACT.Square)
                        A(two(dst), ps, func, **kw).then_inc(lin_ev, 1)

                    def rstd(name, dst, scale):
                        act.wait_ge(lin_mm, Q[name] + 1)
                        A(two(dst), pair[Q[name] % 2][:, :, 0:HALF], ACT.Ln, scale=scale, bias=EPS_C).then_inc(lin_ev, 1)
                        act.wait_ge(lin_ev, Q[name] + 1)
                        A(dst, dst, ACT.Exp, scale=-0.5).then_inc(rs_ready, 1)

                    for k in range(KT):
                        dst = ACC if k == 0 else SQ[:, k]
                        A(dst, H[:, k], ACT.Square).then_inc(sq_pre, 1)
                    rstd("sum_pre", RS, 1.0 / D_MODEL)
                    act.wait_ge(lb_exp, 1)
                    A(LBT[:, 2:6], LBT[:, 2:6], ACT.Exp).then_inc(lb_exp, 1)
                    evac("hf0", proj["hf0"])
                    evac("hf1", proj["hf1"])
                    act.wait_ge(lin_ev, Q["hf1"] + 1)
                    A(LV[0][:, 0:2], K4[:, 0:2], ACT.Sigmoid).then_inc(hf_sig, 1)
                    evac("gq1", proj["gq1"], scale=con[:, C_SCALE:C_SCALE + 1])
                    evac("z0", LV[1][:, 0], ACT.Identity, bias=par[:, W_B:W_B + 1])
                    evac("z1", LV[1][:, 1], ACT.Identity, bias=par[:, W_B + 1:W_B + 2])
                    evac("hq0", proj["hq0"])
                    evac("hq1", proj["hq1"])
                    act.wait_ge(lin_ev, Q["z1"] + 1)
                    st.step(A(LV[1][:, 2:4], LV[1][:, 0:2], ACT.Abs))
                    st.step(A(LV[1][:, 2:4], LV[1][:, 2:4], ACT.Exp, scale=-1.0))
                    A(LV[1][:, 2:4], LV[1][:, 2:4], ACT.Ln, bias=1.0).then_inc(z_log, 1)
                    act.wait_ge(f_ready, 1)
                    A(LV[0][:, 0:2], LV[0][:, 0:2], ACT.Ln).then_inc(g_ready, 1)
                    evac("gq0", proj["gq0"], scale=32.0 ** -0.5)
                    evac("gk0", proj["gk0"])
                    evac("gk1", proj["gk1"])

                    def values(g, tt):
                        name, m = f"v{g}{tt}", P if tt < TT else NEW
                        act.wait_ge(lin_mm, Q[name] + 1)
                        A(V[0:m, tt, 512 * g:512 * g + 512], pair[Q[name] % 2][0:m, 0, :], ACT.Copy).then_inc(lin_ev, 1)

                    for tt in range(TT + 1):
                        values(0, tt)
                    act.wait_ge(b_ready, 4)
                    A(LV[1], B, ACT.Exp).then_inc(eb_exp, 1)
                    act.wait_ge(kd_diff, 2)
                    A(LV[0], LV[0], ACT.Exp).then_inc(kd_exp, 1)
                    for tt in range(TT + 1):
                        values(1, tt)
                    for tt in range(TT + 1):
                        m = P if tt < TT else NEW
                        act.wait_ge(kdt_mm, tt + 1)
                        A(KDT[0:m, tt], bank[4 + tt % 2][0:m, :], ACT.Copy).then_inc(kdt_ev, 1)
                    for h in range(HEADS):
                        o, t = 64 * (h % 2), h // 2
                        act.wait_ge(in_mm, h + 1)
                        A(OI[o:o + 64, t, CH:SEQ], bank[4 + h % 2][o:o + 64, CH:SEQ], ACT.Copy)
                        A(OI[o:o + 64, t, SEQ:T], bank[4 + h % 2][o:o + 64, 0:NEW], ACT.Copy).then_inc(in_ev, 1)
                    in2 = list(IN2)
                    act.wait_ge(st_out, 32)
                    for l in range(len(LEVELS)):
                        if l + 1 < len(LEVELS):
                            act.wait_ge(lv_diff, l + 1)
                            v = LV[(l + 1) % 2]
                            v = v if (l + 1) in SMALL else v[:, :, 0:SEQ]
                            A(v, v, ACT.Exp).then_inc(lv_exp, 1)
                        for _ in range(2 if l < 5 else 1):
                            if in2:
                                name = in2.pop(0)
                                evac(name, proj[name])
                    act.wait_ge(lin_ev, Q["gr2"] + 1)
                    act.wait_ge(lv_mm, 6 * len(LEVELS))
                    A(ETMP, GATES, ACT.Sigmoid).then_inc(gate_sig, 1)
                    xo = [0, 1, 5, 6, 7]
                    for i in range(5):
                        act.wait_ge(o_ready, i + 1)
                        A(SQO[:, i], X[:, xo[i]], ACT.Square).then_inc(sqo, 1)
                    for i in range(5):
                        if i >= 2:
                            act.wait_ge(gate_ready, 1 + i - 1)
                        rstd(f"sum_o{i}", RSO[i % 2], 1.0 / 64)
                    for i in range(6):
                        if i >= 2:
                            act.wait_ge(rot_ready, i - 1)
                        evac(f"rot{i}", ROTMP[i % 2])

                    units = [(h, qt) for h in range(6) for qt in range(TT)]
                    n = len(units)

                    def p_exp(i):
                        w = (units[i][1] + 1) * P
                        act.wait_ge(ps_max, i + 1)
                        A(SMP[i % 3][:, 0:w], SMP[i % 3][:, 0:w], ACT.Exp, bias=NMAX[:, i % 3:i % 3 + 1],
                          accum_out=SUM[:, i % 3:i % 3 + 1]).then_inc(ps_exp, 1)

                    def p_turned(i):
                        w = (units[i][1] + 1) * P
                        act.wait_ge(pt_mm, i + 1)
                        A(PTP[i % 2][:, 0:w], bank[6 + i % 2][:, 0:w], ACT.Copy).then_inc(pt_ev, 1)

                    def p_out(t):
                        name = f"pv{t}"
                        act.wait_ge(lin_mm, Q[name] + 1)
                        A(X[:, 2 + t, 0:SEQ], pair[Q[name] % 2][:, 0, :], ACT.Copy).then_inc(lin_ev, 1)

                    for i in range(n + 1):
                        if i < n:
                            p_exp(i)
                        if i >= 1:
                            p_turned(i - 1)
                        if i >= 3 and (i - 3) % 8 == 7:
                            p_out((i - 3) // 8)
                    p_out(2)

                    def s_exp(b):
                        act.wait_ge(ss_max, b + 1)
                        A(SMS[b % 2][0:48, :], SMS[b % 2][0:48, :], ACT.Exp, bias=NMAXS[0:48, b % 2:b % 2 + 1],
                          accum_out=SUMS[0:48, b % 2:b % 2 + 1]).then_inc(ss_exp, 1)

                    def s_turned(b):
                        act.wait_ge(sp_mm, b + 1)
                        A(PTB[b % 2][:, 0:480], bank[6][:, 0:480], ACT.Copy)
                        A(PTB[b % 2][0:NEW, 480:528], bank[5][0:NEW, 0:48], ACT.Copy).then_inc(sp_ev, 1)

                    def s_outputs(b):
                        act.wait_ge(so_mm, b + 1)
                        act.wait_ge(ss_p, b + 1)
                        A(OS[b % 2][0:48, :], bank[7][0:48, 0:384], ACT.Copy,
                          scale=RECS[0:48, b % 3:b % 3 + 1]).then_inc(os_ev, 1)

                    s_exp(0)
                    for b in range(DEC_BATCH):
                        if b + 1 < DEC_BATCH:
                            s_exp(b + 1)
                        if b >= 1:
                            s_outputs(b - 1)
                        s_turned(b)
                    s_outputs(DEC_BATCH - 1)
                    for i in range(3):
                        act.wait_ge(so_ev, DEC_BATCH)
                        A(SQA[:, i], X[:, 2 + i], ACT.Square).then_inc(sqa, 1)
                    rstd("sum_att", RSA, 1.0 / 384)

                @block.vector
                def _(dve):
                    st = Steps(dve, dve_steps)
                    tt_, ts_, stt = nc.vector.tensor_tensor, nc.vector.tensor_scalar, nc.vector.scalar_tensor_tensor

                    dve.wait_ge(s_par, 16)
                    st.step(tt_(LBT[:, 0:2], par[:, W_LB:W_LB + 2], par[:, W_LB + 2:W_LB + 4], ALU.max))
                    st.mark(tt_(LBT[:, 2:4], par[:, W_LB:W_LB + 2], LBT[:, 0:2], ALU.subtract))
                    tt_(LBT[:, 4:6], par[:, W_LB + 2:W_LB + 4], LBT[:, 0:2], ALU.subtract).then_inc(lb_exp, 1)
                    dve.wait_ge(dve_steps, st.n)

                    def accumulate(acc, sqs, sem_, base=0):
                        for k in range(1, KT):
                            dve.wait_ge(sem_, base + k + 1)
                            ins = tt_(acc, acc, sqs(k), ALU.add)
                            if k < KT - 1:
                                st.step(ins)
                        ins.then_inc(acc_ready, 1)

                    def rstd(name):
                        dve.wait_ge(rs_ready, [n for n in LIN if n.startswith("sum")].index(name) + 1)

                    def spare(k):
                        return SQ[:, k]

                    accumulate(ACC, spare, sq_pre)
                    rstd("sum_pre")
                    for k in range(KT):
                        stt(X[:, k], H[:, k], par[:, W_PRE + k:W_PRE + k + 1], RS, ALU.mult, ALU.mult).then_inc(xn_ready, 1)
                    dve.wait_ge(lb_exp, 2)
                    st.step(tt_(LBT[:, 6:8], LBT[:, 2:4], LBT[:, 4:6], ALU.add))
                    st.step(nc.vector.reciprocal(LBT[:, 6:8], LBT[:, 6:8]))
                    st.step(tt_(LBT[:, 6:8], LBT[:, 6:8], LBT[:, 4:6], ALU.mult))
                    st.step(ts_(LB, LBT[:, 6:8], par[:, W_FLAG:W_FLAG + 1], None, ALU.mult))
                    st.step(ts_(OMLB, LB, -1.0, 1.0, ALU.mult, ALU.add))
                    dve.wait_ge(hf_sig, 1)
                    f = LV[0][:, 0:2]
                    for i in range(2):
                        n = st.mark(ts_(f[:, i], f[:, i], OMLB[:, i:i + 1], LB[:, i:i + 1], ALU.mult, ALU.add))
                    st.after(n)
                    ts_(K4[:, 0:2], f, -1.0, 1.0, ALU.mult, ALU.add).then_inc(f_ready, 1)
                    dve.wait_ge(z_log, 1)
                    st.step(stt(LV[0][:, 2:4], LV[1][:, 0:2], 0.0, LV[1][:, 2:4], ALU.min, ALU.subtract))
                    st.step(ts_(LV[0][:, 2:4], LV[0][:, 2:4], 1.0 / 16, None, ALU.mult))
                    dve.wait_ge(g_ready, 1)
                    for r in range(4):
                        nc.vector.tensor_tensor_scan(B[:, r], RESET, LV[0][:, r], 0.0, ALU.mult, ALU.add).then_inc(b_ready, 1)
                    dve.wait_ge(b_ready, 4)
                    for s in range(2):
                        shape = [P, 4, NC, CH] if s == 0 else [P, 4, DEC_BATCH, DEC_SEQ]
                        tt_(chunks_of(LV[0], s), last_of(B, s).to_broadcast(shape), chunks_of(B, s),
                            ALU.subtract).then_inc(kd_diff, 1)
                    dve.wait_ge(eb_exp, 1)
                    dve.wait_ge(lin_ev, Q["gk1"] + 1)
                    n = st.mark(nc.vector.tensor_copy(EBL[:, :, 0:8], LV[1][:, :, CH - 1:SEQ:CH]))
                    n = st.mark(nc.vector.tensor_copy(EBL[:, :, 8:16], LV[1][:, :, SEQ + DEC_SEQ - 1:T:DEC_SEQ]))
                    st.after(n)
                    tt_(QI, Q4, LV[1], ALU.mult).then_inc(qi_ready, 1)
                    dve.wait_ge(kd_exp, 1)
                    tt_(LV[0], LV[0], K4, ALU.mult).then_inc(kd_ready, 1)
                    for c in range(NC):
                        add = bank[4 + c % 4][:, 0:256].rearrange("p (r v) -> p r v", r=4)
                        if c > 0:
                            st.step(tt_(SC[:, c], SC[:, c - 1],
                                        EBL[:, :, c:c + 1].to_broadcast([P, 4, 64]), ALU.mult))
                        dve.wait_ge(u_mm, c + 1)
                        ins = tt_(SC[:, c], SC[:, c], add, ALU.add) if c > 0 else nc.vector.tensor_copy(SC[:, c], add)
                        ins.then_inc(u_ev, 1)
                        dve.wait_ge(u_ev, c + 1)
                    dve.wait_ge(in_mm, HEADS)
                    for r in range(4):
                        n = P if r < 3 else 64
                        s = S0[0:n, :, r, :]
                        st.step(tt_(s, s, EBL[0:n, r, 8:16].rearrange("p (b a) -> p b a", a=1).to_broadcast([n, DEC_BATCH, 64]), ALU.mult))
                        dve.wait_ge(us_mm, [2, 4, 8, 10][r])
                        tt_(s, s, bank[6 + r % 2][0:n, :].rearrange("p (b v) -> p b v", v=64), ALU.add).then_inc(us_ev, 1)

                    def diff(l):
                        h, v = LEVELS[l], LV[l % 2]
                        (d0, _), (d1, _) = blocks(v, h, 0), blocks(v, h, 1)
                        (b0, mid), (b1, _) = blocks(B, h, 0), blocks(B, h, 1)
                        st.mark(tt_(d0, mid, b0, ALU.subtract))
                        tt_(d1, b1, mid, ALU.subtract).then_inc(lv_diff, 1)

                    def scale(l):
                        h, v = LEVELS[l], LV[l % 2]
                        dve.wait_ge(lv_exp, l)
                        d0, d1 = blocks(v, h, 0)[0], blocks(v, h, 1)[0]
                        n = st.mark(tt_(d0, d0, blocks(K4, h, 0)[0], ALU.mult))
                        st.after(n)
                        tt_(d1, d1, blocks(Q4, h, 1)[0], ALU.mult).then_inc(lv_ready, 1)

                    gi = si = 0

                    def pick(l):
                        nonlocal gi, si
                        mask = con[:, C_MASK + CH * l:C_MASK + CH * (l + 1)].bitcast(U32).rearrange("p (a t) -> p a t", a=1)
                        for g, heads in enumerate(GROUPS):
                            n, s = len(heads), FIRST_SLOT[g]
                            dve.wait_ge(lv_mm, gi + 1)
                            nc.vector.copy_predicated(
                                AT[:, s:s + n].rearrange("p s c t -> p (s c) t"), mask.to_broadcast([P, 4 * n, CH]),
                                bank[4 + gi % 2][:, 0:4 * n * CH].rearrange("p (a t) -> p a t", t=CH)).then_inc(lv_ev, 1)
                            gi += 1
                            if l in SMALL:
                                dve.wait_ge(ls_mm, si + 1)
                                nc.vector.copy_predicated(
                                    ATS[0:NEW, s:s + n], mask[0:NEW].to_broadcast([NEW, n, CH]),
                                    bank[6 + si % 2][0:NEW, 0:n * CH].rearrange("p (a t) -> p a t", t=CH)).then_inc(ls_ev, 1)
                                si += 1

                    dve.wait_ge(kdt_mm, TT + 1)
                    dve.wait_ge(us_mm, HEADS)
                    diff(1)
                    dve.wait_ge(at_zero, 1)
                    for l in range(1, len(LEVELS)):
                        pick(l - 1)
                        scale(l)
                        if l + 1 < len(LEVELS):
                            diff(l + 1)
                    pick(len(LEVELS) - 1)
                    xo = [0, 1, 5, 6, 7]
                    dve.wait_ge(in_ev, HEADS)
                    dve.wait_ge(oi_zero, 1)
                    for t in range(5):
                        dve.wait_ge(ia_mm, t + 1)
                        x = X[:, xo[t]]
                        for par_ in range(2):
                            o3 = x[:, 0:SEQ].rearrange("p (c a s) -> p a c s", a=2, s=CH)[:, par_]
                            i3 = OI[:, t, 0:SEQ].rearrange("p (c a s) -> p a c s", a=2, s=CH)[:, par_]
                            n = st.mark(tt_(o3, i3, bank[4 + 2 * (t % 2) + par_][:, 0:4 * CH].rearrange("p (c s) -> p c s", s=CH), ALU.add))
                        tt_(x[:, SEQ:T], OI[:, t, SEQ:T], bank[4 + 2 * (t % 2)][:, 4 * CH:5 * CH], ALU.add).then_inc(o_ready, 1)
                    dve.wait_ge(gate_sig, 1)
                    tt_(GATES, GATES, ETMP, ALU.mult).then_inc(gate_ready, 1)
                    dve.wait_ge(gate_ready, 1)
                    for i in range(5):
                        x, rs = X[:, xo[i]], RSO[i % 2]
                        rstd(f"sum_o{i}")
                        st.step(stt(x, x, par[:, W_O + xo[i]:W_O + xo[i] + 1], rs, ALU.mult, ALU.mult))
                        tt_(x, x, GATES[:, i], ALU.mult).then_inc(gate_ready, 1)
                    dve.wait_ge(gate_ready, 6)
                    for i in range(6):
                        dve.wait_ge(lin_ev, Q[f"rot{i}"] + 1)
                        n = st.mark(tt_(ROTMP[i % 2], ROTMP[i % 2], SIN, ALU.mult))
                        n = st.mark(tt_(ROTQK[:, i], ROTQK[:, i], COS, ALU.mult))
                        st.after(n)
                        tt_(ROTQK[:, i], ROTQK[:, i], ROTMP[i % 2], ALU.add).then_inc(rot_ready, 1)
                    dve.wait_ge(rot_ready, 6)
                    dve.wait_ge(qb_zero, 2)
                    for g in range(2):
                        for h in range(6):
                            c, hp = h // 2, h % 2
                            rows = slice(64 * hp, 64 * hp + 64)
                            dst = V[rows, g, 0:T].rearrange("p (b c n) -> p b c n", b=4, c=3)[:, :, c, 8 * h:8 * h + 8]
                            src = ROTQK[rows, c, SEQ + 32 * g:SEQ + 32 * g + 32].rearrange("p (b t) -> p b t", b=4)
                            n = st.mark(nc.vector.tensor_copy(dst, src))
                    st.after(n)
                    dve.sem_inc(qb_ready, 1)

                    units = [(h, qt) for h in range(6) for qt in range(TT)]
                    n_u = len(units)

                    def p_max(i):
                        h, qt = units[i]
                        w = (qt + 1) * P
                        dve.wait_ge(ps_mm, i + 1)
                        if i >= 3:
                            dve.wait_ge(pt_mm, i - 2)
                        st.step(stt(SMP[i % 3][:, 0:w], bank[4 + i % 2][:, 0:w], 0.125,
                                    con[:, C_BIAS + (3 - qt) * P:C_BIAS + 4 * P], ALU.mult, ALU.add))
                        nc.vector.tensor_reduce(NMAX[:, i % 3:i % 3 + 1], SMP[i % 3][:, 0:w], AX_X, ALU.max,
                                                negate=True).then_inc(ps_max, 1)

                    def p_norm(i):
                        w = (units[i][1] + 1) * P
                        dve.wait_ge(ps_exp, i + 1)
                        st.step(nc.vector.reciprocal(REC[:, i % 3:i % 3 + 1], SUM[:, i % 3:i % 3 + 1]))
                        ts_(SMP[i % 3][:, 0:w], SMP[i % 3][:, 0:w], REC[:, i % 3:i % 3 + 1], None, ALU.mult).then_inc(ps_p, 1)

                    for i in range(n_u + 1):
                        if i < n_u:
                            p_max(i)
                        if i >= 1:
                            p_norm(i - 1)

                    def s_max(b):
                        sm = SMS[b % 2]
                        dve.wait_ge(ss_mm, b + 1)
                        if b >= 2:
                            dve.wait_ge(sp_mm, b - 1)
                        for j, (lo, w) in enumerate(((0, 512), (512, 512), (1024, 256))):
                            n = st.mark(stt(sm[0:48, lo:lo + w], bank[j][0:48, 0:w], 0.125,
                                            con[0:48, C_SBIAS + lo:C_SBIAS + lo + w], ALU.mult, ALU.add))
                        stt(sm[0:48, KEYS:KEYS + NEW], bank[3][0:48, 0:NEW], 0.125,
                            con[0:48, C_NBIAS + NEW * b:C_NBIAS + NEW * (b + 1)], ALU.mult, ALU.add).then_inc(ss_read, 1)
                        st.after(n)
                        dve.wait_ge(ss_read, b + 1)
                        nc.vector.tensor_reduce(NMAXS[0:48, b % 2:b % 2 + 1], sm[0:48, :], AX_X, ALU.max,
                                                negate=True).then_inc(ss_max, 1)

                    def s_norm(b):
                        dve.wait_ge(ss_exp, b + 1)
                        if b >= 3:
                            dve.wait_ge(os_ev, b - 2)
                        nc.vector.reciprocal(RECS[0:48, b % 3:b % 3 + 1], SUMS[0:48, b % 2:b % 2 + 1]).then_inc(ss_p, 1)

                    def s_out(b):
                        dve.wait_ge(st_mm, b + 1)
                        for hp in range(2):
                            rows = slice(64 * hp, 64 * hp + 64)
                            src = bank[4][rows, 0:192].rearrange("p (c n) -> p c n", c=3)[:, :, 8 * hp:8 * hp + 8]
                            ins = nc.vector.tensor_copy(X[rows, 2:5, SEQ + 8 * b:SEQ + 8 * b + 8], src)
                            if hp == 0:
                                st.mark(ins)
                        ins.then_inc(so_ev, 1)

                    dve.wait_ge(pt_mm, n_u)
                    for b in range(DEC_BATCH + 3):
                        if b < DEC_BATCH:
                            s_max(b)
                        if 1 <= b <= DEC_BATCH:
                            s_norm(b - 1)
                        if b >= 3:
                            s_out(b - 3)
                    rstd("sum_att")
                    for i in range(3):
                        n = st.mark(stt(X[:, 2 + i], X[:, 2 + i], par[:, W_O + 2 + i:W_O + 3 + i], RSA, ALU.mult, ALU.mult))
                    st.after(n)
                    dve.sem_inc(att_ready, 1)

            with nc.sbuf_tensor("x_hi_part", [P, KT * T], F32R) as xh_sb, \
                    nc.sbuf_tensor("x_lo_part", [P, KT * T], F32R) as xl_sb, \
                    nc.sbuf_tensor("u_hi_part", [P, KT * T], F32R) as uh_sb, \
                    nc.sbuf_tensor("u_lo_part", [P, KT * T], F32R) as ul_sb, \
                    nc.sbuf_tensor("w_hi_part", [P, SPLITS * 1024], F32R) as wh_sb, \
                    nc.sbuf_tensor("w_lo_part", [P, SPLITS * 1024], F32R) as wl_sb, \
                    nc.sbuf_tensor("y", [P, KT * T], F32) as y_sb, \
                    nc.sbuf_tensor("tmp", [P, 6 * T], F32) as tmp_sb, nc.Block() as block:
                XH, XL, UH, UL, Y = (v[:, :].rearrange("p (k t) -> p k t", k=KT) for v in (xh_sb, xl_sb, uh_sb, ul_sb, y_sb))
                tmp = tmp_sb[:, :].rearrange("p (k t) -> p k t", k=6)
                TMP, ACC, RS = [tmp[:, 0], tmp[:, 1]], tmp[:, 2], tmp[:, 3]
                XT = [X[:, 0], X[:, 1]]
                PL = [X[:, 2 + k] for k in range(6)] + [tmp[:, 4], tmp[:, 5]]
                XORDER = [0, 1, 5, 6, 7, 2, 3, 4]

                def raw(r):
                    return raw_sb[:, slot_of(r) * 1024:(slot_of(r) + 1) * 1024]

                def w_part(sb_, i):
                    return sb_[:, (i % SPLITS) * 1024:(i % SPLITS + 1) * 1024]

                I_UP, I_GATE = KT, KT + 2 * FT

                @block.sync
                def _(sp):
                    for r in range(R_OUT + RAW, UNITS):
                        sp.wait_ge(*freed(former(r)))
                        sp.dma_start(raw(r), of_layer(w_units)[r * P:(r + 1) * P, :]).then_inc(w_landed[slot_of(r)], 16)

                @block.gpsimd
                def _(pool):
                    for b in range(3, DEC_BATCH):
                        pool.wait_ge(lin_mm, Q[f"up{6 * (b - 3)}"] + 1)
                        copy_cache(pool, b)

                @block.tensor
                def _(pe):
                    def split_product(ps, i, xh, xl, done, ready=None, order=range(KT)):
                        pe.wait_ge(w_split, i + 1)
                        wh, wl = w_part(wh_sb, i), w_part(wl_sb, i)
                        for n, k in enumerate(order):
                            if ready is not None:
                                pe.wait_ge(ready[0], ready[1] + n + 1)
                            cols = slice(k * P, (k + 1) * P)
                            for half in range(2):
                                out, t = ps[:, half, 0:HALF], slice(half * HALF, (half + 1) * HALF)
                                nc.tensor.matmul(out, wh[:, cols], xh[:, k, t], start=n == 0, stop=False)
                                nc.tensor.matmul(out, wh[:, cols], xl[:, k, t], start=False, stop=False)
                                mm = nc.tensor.matmul(out, wl[:, cols], xh[:, k, t], start=False, stop=n == KT - 1)
                        mm.then_inc(done, 1)

                    def claim(name):
                        q = Q[name]
                        pe.wait_ge(lin_ev, q - 1)
                        return pair[q % 2]

                    def claim_side(name):
                        q = D[name]
                        if q >= 2:
                            pe.wait_ge(side_ev, q - 1)
                        return pair[2 + q % 2]

                    def total(name, ready):
                        ps = claim(name)
                        pe.wait_ge(acc_ready, ready)
                        for half in range(2):
                            mm = nc.tensor.matmul(ps[:, half, 0:HALF], ONES, ACC[:, half * HALF:(half + 1) * HALF],
                                                  start=True, stop=True)
                        mm.then_inc(lin_mm, 1)

                    for k in range(KT):
                        split_product(claim(f"out{k}"), k, XH, XL, lin_mm, (x_split, 0) if k == 0 else None, XORDER)

                    def ple(n):
                        r = R_PLE + n // 4
                        if n % 4 == 0:
                            pe.wait_ge(w_landed[slot_of(r)], 16 * loads(r))
                        ps = claim_side(f"ple{n}")
                        for half in range(2):
                            for k in range(2):
                                o = (2 * (n % 4) + k) * P
                                mm = nc.tensor.matmul(ps[:, half, 0:HALF], raw(r)[:, o:o + P],
                                                      PT_IN[:, k, half * HALF:(half + 1) * HALF], start=k == 0, stop=k == 1)
                        mm.then_inc(side_mm, 1)

                    pe.wait_ge(s_pt, 16)
                    ple(0)
                    ple(1)
                    total("sum_mix", 2)
                    for n in range(2, KT):
                        ple(n)
                    total("sum_mlp", 3)
                    for c in range(CHUNKS):
                        i = I_UP + 2 * KT * c
                        for j in range(KT):
                            first_ = c == 0 and j == 0
                            split_product(claim(f"up{c * KT + j}"), i + j, XH, XL, lin_mm, (x_split, KT) if first_ else None)
                        for n in range(KT):
                            split_product(claim_side(f"down{c}{n}"), i + KT + n, UH, UL, side_mm,
                                          (u_split, c * KT) if n == 0 else None)
                    total("sum_down", 4)
                    for k in range(KT):
                        split_product(claim(f"gate{k}"), I_GATE + k, XH, XL, lin_mm, (x_split, 2 * KT) if k == 0 else None)

                @block.scalar
                def _(act):
                    A = nc.scalar.activation

                    def two(ap):
                        return ap.rearrange("p (a t) -> p a t", a=2)

                    def leading(dst, src, done):
                        return A(dst, src, ACT.Copy).then_inc(done, 1)

                    def split_w(i):
                        if i < len(SPLIT):
                            r = SPLIT[i]
                            act.wait_ge(w_landed[slot_of(r)], 16 * loads(r))
                            if i >= SPLITS:
                                act.wait_ge(*used_up(SPLIT[i - SPLITS]))
                            leading(w_part(wh_sb, i), raw(r), w_hi)

                    def rstd(name):
                        act.wait_ge(lin_mm, Q[name] + 1)
                        A(two(RS), pair[Q[name] % 2][:, :, 0:HALF], ACT.Ln, scale=1.0 / D_MODEL, bias=EPS_C).then_inc(lin_ev, 1)
                        act.wait_ge(lin_ev, Q[name] + 1)
                        A(RS, RS, ACT.Exp, scale=-0.5).then_inc(rs_ready, 1)

                    def square(k, src, done, used):
                        if k >= 3:
                            act.wait_ge(used, k - 2)
                        A(two(ACC if k == 0 else TMP[k % 2]), src, ACT.Square).then_inc(done, 1)

                    split_w(0)
                    for n, k in enumerate(XORDER):
                        leading(XH[:, k], X[:, k], x_hi)
                        if n in (0, 1):
                            split_w(n + 1)
                    for k in range(KT):
                        name = f"out{k}"
                        act.wait_ge(lin_mm, Q[name] + 1)
                        ps = pair[Q[name] % 2][:, :, 0:HALF]
                        square(k, ps, sq_mix, acc_mix)
                        A(two(Y[:, k]), ps, ACT.Copy).then_inc(lin_ev, 1)
                        if k < KT - 1:
                            split_w(k + SPLITS)

                    def ple(n):
                        act.wait_ge(side_mm, n + 1)
                        A(two(PL[n]), pair[2 + n % 2][:, :, 0:HALF], ACT.Copy).then_inc(side_ev, 1)

                    act.wait_ge(x_split, KT)
                    ple(0)
                    ple(1)
                    rstd("sum_mix")
                    for k in range(KT):
                        if k + 2 < KT:
                            ple(k + 2)
                        act.wait_ge(h_mix, k + 1)
                        square(k, two(H[:, k]), sq_h, acc_h)
                    split_w(KT - 1 + SPLITS)
                    rstd("sum_mlp")
                    for k in range(KT):
                        act.wait_ge(xm_ready, k + 1)
                        leading(XH[:, k], XT[k % 2], x_hi)
                    for c in range(CHUNKS):
                        for j in range(KT):
                            g, i = c * KT + j, I_UP + 2 * KT * c + j
                            if g >= 2:
                                act.wait_ge(u_split, g - 1)
                            act.wait_ge(lin_mm, Q[f"up{g}"] + 1)
                            A(two(TMP[g % 2]), pair[Q[f"up{g}"] % 2][:, :, 0:HALF], ACT.Relu).then_inc(lin_ev, 1)
                            split_w(i + SPLITS)
                            act.wait_ge(u_sq, g + 1)
                            leading(UH[:, j], TMP[g % 2], u_hi)
                        for n in range(KT):
                            i, q = I_UP + 2 * KT * c + KT + n, D[f"down{c}{n}"]
                            if c == 0:
                                act.wait_ge(side_mm, q + 1)
                                A(two(Y[:, n]), pair[2 + q % 2][:, :, 0:HALF], ACT.Copy).then_inc(side_ev, 1)
                            split_w(i + SPLITS)
                            if c == CHUNKS - 1:
                                act.wait_ge(side_ev, q + 1)
                                if n == 0:
                                    act.wait_ge(u_split, FT)
                                square(n, two(Y[:, n]), sq_down, acc_down)
                    rstd("sum_down")
                    for k in range(KT):
                        act.wait_ge(h_down, k + 1)
                        leading(XH[:, k], H[:, k], x_hi)
                    for k in range(KT):
                        name = f"gate{k}"
                        if k >= 2:
                            act.wait_ge(z_used, k - 1)
                        act.wait_ge(lin_mm, Q[name] + 1)
                        A(two(TMP[k % 2]), pair[Q[name] % 2][:, :, 0:HALF], ACT.Sigmoid).then_inc(lin_ev, 1)
                        split_w(I_GATE + k + SPLITS)

                @block.vector
                def _(dve):
                    st = Steps(dve, dve_steps_b)
                    tt_, stt = nc.vector.tensor_tensor, nc.vector.scalar_tensor_tensor

                    def remainder(dst, src, hi, done):
                        return tt_(dst, src, hi.bitcast(F32), ALU.subtract).then_inc(done, 1)

                    def split_w(i):
                        if i < len(SPLIT):
                            dve.wait_ge(w_hi, i + 1)
                            remainder(w_part(wl_sb, i), raw(SPLIT[i]), w_part(wh_sb, i), w_split)

                    def rstd(name):
                        dve.wait_ge(rs_ready, [n for n in LIN if n.startswith("sum")].index(name) + 1)

                    def accumulate(k, squared, done):
                        dve.wait_ge(squared, k + 1)
                        if k >= 2:
                            dve.wait_ge(done, k - 1)
                        ins = tt_(ACC, ACC, TMP[k % 2], ALU.add)
                        ins.then_inc(acc_ready if k == KT - 1 else done, 1)

                    def two(ap):
                        return ap.rearrange("p (a t) -> p a t", a=2)

                    split_w(0)
                    for n, k in enumerate(XORDER):
                        dve.wait_ge(x_hi, n + 1)
                        remainder(XL[:, k], X[:, k], XH[:, k], x_split)
                        if n in (0, 1):
                            split_w(n + 1)
                    for k in range(KT):
                        if k >= 1:
                            accumulate(k, sq_mix, acc_mix)
                        if k < KT - 1:
                            split_w(k + SPLITS)
                    rstd("sum_mix")

                    def add_normed(k, w, ready):
                        st.step(stt(Y[:, k], Y[:, k], par[:, w + k:w + k + 1], RS, ALU.mult, ALU.mult))
                        tt_(H[:, k], H[:, k], Y[:, k], ALU.add).then_inc(ready, 1)

                    for k in range(KT):
                        add_normed(k, W_MIX, h_mix)
                        if k >= 2:
                            accumulate(k - 1, sq_h, acc_h)
                    accumulate(KT - 1, sq_h, acc_h)
                    split_w(KT - 1 + SPLITS)
                    rstd("sum_mlp")
                    for k in range(KT + 1):
                        if k < KT:
                            if k >= 2:
                                dve.wait_ge(x_split, KT + k - 1)
                            stt(XT[k % 2], H[:, k], par[:, W_MLP + k:W_MLP + k + 1], RS, ALU.mult, ALU.mult).then_inc(xm_ready, 1)
                        if k >= 1:
                            dve.wait_ge(x_hi, KT + k)
                            remainder(XL[:, k - 1], XT[(k - 1) % 2], XH[:, k - 1], x_split)
                    for c in range(CHUNKS):
                        for j in range(KT):
                            g, i = c * KT + j, I_UP + 2 * KT * c + j
                            t = TMP[g % 2]
                            dve.wait_ge(lin_ev, Q[f"up{g}"] + 1)
                            tt_(t, t, t, ALU.mult).then_inc(u_sq, 1)
                            split_w(i + SPLITS)
                            dve.wait_ge(u_hi, g + 1)
                            remainder(UL[:, j], t, UH[:, j], u_split)
                        for n in range(KT):
                            i, q = I_UP + 2 * KT * c + KT + n, D[f"down{c}{n}"]
                            if c > 0:
                                dve.wait_ge(side_ev, D[f"down{c - 1}{n}"] + 1)
                                dve.wait_ge(side_mm, q + 1)
                                tt_(two(Y[:, n]), two(Y[:, n]), pair[2 + q % 2][:, :, 0:HALF], ALU.add).then_inc(side_ev, 1)
                            split_w(i + SPLITS)
                            if c == CHUNKS - 1 and n >= 2:
                                accumulate(n - 1, sq_down, acc_down)
                    accumulate(KT - 1, sq_down, acc_down)
                    rstd("sum_down")
                    for k in range(KT + 1):
                        if k < KT:
                            add_normed(k, W_DOWN, h_down)
                        if k >= 1:
                            dve.wait_ge(x_hi, 2 * KT + k)
                            remainder(XL[:, k - 1], H[:, k - 1], XH[:, k - 1], x_split)
                    for k in range(KT):
                        split_w(I_GATE + k + SPLITS)
                        dve.wait_ge(lin_ev, Q[f"gate{k}"] + 1)
                        if k == 0:
                            dve.wait_ge(x_split, 3 * KT)
                        st.step(tt_(TMP[k % 2], TMP[k % 2], PL[k], ALU.mult))
                        tt_(H[:, k], H[:, k], TMP[k % 2], ALU.add).then_inc(z_used, 1)

            nc.gpsimd.sem_clear(range(first, last + 1))
            nc.all_engine_barrier()

        with nc.Block() as block:
            @block.sync
            def _(sp):
                sp.dma_start(y_out, h_sb[:, :]).then_inc(s_y, 16)
                sp.wait_ge(s_y, 16)
                sp.wait_ge(copied, 16 * 2 * DEC_BATCH * DEPTH)


IN_SPLITS = (256, 256, 256, 256, 384, 384, 384, 192, 192, 384, 16, 384)
IN_NAMES = ("hq", "hf", "hi", "hg", "aq", "ak", "av", "gq", "gk", "gv", "lr", "gr")


def kernel(**inputs):
    import concourse.bacc as bacc
    from concourse.bass_utils import run_bass_kernel_spmd

    a = {k: np.asarray(v) for k, v in inputs.items()}
    f = np.float32

    def feature_major(x):
        n, d = x.shape
        return x.T.reshape(d // P, P, n).transpose(1, 0, 2).reshape(P, -1)

    def both(prompt, sample, d):
        return feature_major(np.concatenate([prompt.reshape(SEQ, d), sample.reshape(NEW, d)], 0))

    def units(w):
        k, n = w.shape
        return w.reshape(k // 1024, KT, P, n // P, P).transpose(3, 0, 2, 1, 4).reshape(-1, P, 1024)

    w_units = np.zeros((DEPTH, UNITS * P, 1024), f)
    par = np.zeros((DEPTH, P, W_END), f)
    s0 = np.zeros((DEPTH, P, DEC_BATCH, 4, 64), f)
    cols = dict(zip(IN_NAMES, np.split(np.arange(sum(IN_SPLITS)), np.cumsum(IN_SPLITS)[:-1])))
    for l in range(DEPTH):
        w = a["w_in"][l]
        tile_cols = {}
        for n in ("hf", "hq", "aq", "ak", "hg", "gr"):
            for i in range(len(cols[n]) // P):
                tile_cols[f"{n}{i}"] = cols[n][i * P:(i + 1) * P]
        tile_cols["gq0"], tile_cols["gk0"] = cols["gq"][:P], cols["gk"][:P]
        tile_cols["gq1"] = np.concatenate([cols["gq"][P:], cols["lr"]])
        tile_cols["gk1"] = cols["gk"][P:]
        u = []

        def in_unit(n):
            t = np.zeros((D_MODEL, P), f)
            t[:, :len(tile_cols[n])] = w[:, tile_cols[n]]
            u.append(units(t)[0])

        for n in IN1:
            in_unit(n)
        wv = w[:, np.concatenate([cols["hi"], cols["gv"], cols["av"]])]
        for g in range(2):
            for j in range(4):
                blk = wv[256 * j:256 * (j + 1), 512 * g:512 * (g + 1)]
                u.append(blk.reshape(2, P, 512).transpose(1, 0, 2).reshape(P, 1024))
        for n in IN2:
            in_unit(n)
        u.extend(units(a["w_out"][l]))
        wp = a["w_ple"][l].reshape(2, P, 2, 4, P).transpose(2, 1, 3, 0, 4).reshape(2, P, 1024)
        u.extend(wp)
        up, down = units(a["w_up"][l]), units(a["w_down"][l]).reshape(KT, CHUNKS, P, 1024)
        for c in range(CHUNKS):
            u.extend(up[c * KT:(c + 1) * KT])
            u.extend(down[:, c])
        u.extend(units(a["w_ple_gate"][l]))
        assert len(u) == UNITS
        w_units[l] = np.concatenate(u, 0)

        def col(v):
            return v.reshape(-1, P).T

        par[l, :, W_PRE:W_PRE + 8] = col(a["norm_pre_mix"][l])
        par[l, :, W_MIX:W_MIX + 8] = col(a["norm_post_mix"][l])
        par[l, :, W_MLP:W_MLP + 8] = col(a["norm_pre_mlp"][l])
        par[l, :, W_DOWN:W_DOWN + 8] = col(a["norm_post_mlp"][l])
        par[l, :, W_O:W_O + 8] = col(np.concatenate([a["hgrn_norm"][l], a["attn_norm"][l], a["gla_norm"][l]]))
        par[l, :, W_B] = a["gla_b_gate"][l][:P]
        par[l, :64, W_B + 1] = a["gla_b_gate"][l][P:]
        for i in range(DEPTH):
            par[l, :, W_LB + 2 * i:W_LB + 2 * i + 2] = col(a["hgrn_lb"][i])
        par[l, :, W_FLAG] = l
        par[l, 64:80, W_G2:W_G2 + 192] = a["gla_w_gate2"][l]
        for h in range(4):
            r, row, n = HEAD_AT[h]
            s0[l, row:row + n, :, r] = a["state_hgrn"][l][:, h].transpose(1, 0, 2)
        for h in range(6):
            r, row, n = HEAD_AT[4 + h]
            s0[l, row:row + n, :, r] = a["state_gla"][l][:, h].transpose(1, 0, 2)
    order = cache_order()
    ck = a["cache_k"].reshape(DEPTH, DEC_BATCH, WIN, 384)[:, :, order].transpose(0, 1, 3, 2)
    cv = a["cache_v"].reshape(DEPTH, DEC_BATCH, WIN, 384)[:, :, order]
    arrays = {
        "x_t": both(a["x_prompt"], a["x_sample"], D_MODEL),
        "consts": constants(),
        "params": par,
        "p_t": np.stack([both(a["p_prompt"][l], a["p_sample"][l], 256) for l in range(DEPTH)]),
        "s0_in": s0.reshape(DEPTH, P, -1),
        "w_units": w_units,
        "ck": ck.reshape(DEPTH, DEC_BATCH * 384, WIN),
        "cv": cv.reshape(DEPTH, DEC_BATCH * WIN, 384),
    }
    arrays = {k: np.ascontiguousarray(v) for k, v in arrays.items()}
    outs = {
        "y_out": (P, KT * T), "kp_out": (DEPTH, P, 3 * SEQ), "kn_out": (DEPTH, P, 3 * NEW),
        "vp_out": (DEPTH, P, TT * 384), "vn_out": (DEPTH, NEW, 384),
        "ck_out": (DEPTH, DEC_BATCH * 384, KEPT), "cv_out": (DEPTH, DEC_BATCH * KEPT, 384),
        "sp_out": (DEPTH, P, 256), "ss_out": (DEPTH, P, 2048),
    }
    nc = bacc.Bacc("TRN2", target_bir_lowering=False, num_devices=1)
    args = {k: nc.dram_tensor(k, v.shape, F32, kind="ExternalInput").ap() for k, v in arrays.items()}
    args.update({k: nc.dram_tensor(k, s, F32, kind="ExternalOutput").ap() for k, s in outs.items()})
    build(nc, **args)
    r = run_bass_kernel_spmd(nc, [arrays], core_ids=[0]).results[0]

    y = r["y_out"].reshape(P, KT, T).transpose(2, 1, 0).reshape(T, D_MODEL)
    y_p = y[:SEQ].reshape(1, SEQ, D_MODEL)
    y_s = y[SEQ:].reshape(DEC_BATCH, DEC_SEQ, D_MODEL)

    def keys(x, n):
        return x.reshape(DEPTH, P, 3, n).transpose(0, 3, 2, 1).reshape(DEPTH, n, 6, 64)

    k_p = keys(r["kp_out"], SEQ)[:, None]
    v_p = r["vp_out"].reshape(DEPTH, P, TT, 384).transpose(0, 2, 1, 3).reshape(DEPTH, 1, SEQ, 6, 64)
    sp = r["sp_out"].reshape(DEPTH, P, 1, 4, 64)
    ss = r["ss_out"].reshape(DEPTH, P, DEC_BATCH, 4, 64)

    def states(s, heads):
        return np.stack([s[:, row:row + n, :, t].transpose(0, 2, 1, 3) for t, row, n in heads], 2)

    back = np.empty(KEPT, np.int64)
    back[order[DEC_SEQ:] - DEC_SEQ] = np.arange(KEPT)
    ck_n = r["ck_out"].reshape(DEPTH, DEC_BATCH, 384, KEPT)[:, :, :, back].transpose(0, 1, 3, 2)
    cv_n = r["cv_out"].reshape(DEPTH, DEC_BATCH, KEPT, 384)[:, :, back]
    kn = keys(r["kn_out"], NEW).reshape(DEPTH, DEC_BATCH, DEC_SEQ, 6, 64)
    vn = r["vn_out"].reshape(DEPTH, DEC_BATCH, DEC_SEQ, 6, 64)
    k_s = np.concatenate([ck_n.reshape(DEPTH, DEC_BATCH, KEPT, 6, 64), kn], 2)
    v_s = np.concatenate([cv_n.reshape(DEPTH, DEC_BATCH, KEPT, 6, 64), vn], 2)
    hg, gl = HEAD_AT[:4], HEAD_AT[4:]
    got = (y_p, y_s, states(sp, hg), states(sp, gl), k_p, v_p, states(ss, hg), states(ss, gl), k_s, v_s)
    return tuple(np.ascontiguousarray(x) for x in got)
```

```python
import math
from contextlib import ExitStack

import numpy as np

import concourse.bass as bass
from concourse import mybir
from concourse.alu_op_type import AluOpType as ALU

F32 = mybir.dt.float32
F32R = mybir.dt.float32r
U32 = mybir.dt.uint32
ACT = mybir.ActivationFunctionType
AX_X = mybir.AxisListType.X

P = 128
D_MODEL, DEPTH = 1024, 2
SEQ, DEC_BATCH, DEC_SEQ = 512, 8, 8
NEW = DEC_BATCH * DEC_SEQ
T = SEQ + NEW
HALF = T // 2
KT = D_MODEL // P
D_FF = 4 * D_MODEL
FT = D_FF // P
PAST, WIN = 4096, 2048
CH = 64
NC = SEQ // CH
TT = SEQ // P
EPS = 1e-6
ROPE_THETA = 500000.0
PATTERNS = ((128, 1), (512, 4), (2048, 16))
NEG = -1e30
KEYS = 1280
KC = KEYS // P
KEPT = WIN - DEC_SEQ

IN1 = ["hf0", "hf1", "gq1", "hq0", "hq1", "gq0", "gk0", "gk1"]
IN2 = ["aq0", "aq1", "aq2", "ak0", "ak1", "ak2", "hg0", "hg1", "gr0", "gr1", "gr2"]
R_IN1, R_V = 0, 8
R_IN2 = R_V + 8
R_OUT = R_IN2 + len(IN2)
R_PLE = R_OUT + KT
R_UP = R_PLE + 2
R_GATE = R_UP + 2 * FT
UNITS = R_GATE + KT
CHUNKS = FT // KT
RING = 8
RAW = 4
SPLITS = 3
SPLIT = list(range(R_IN2)) + list(range(R_OUT, R_PLE)) + list(range(R_UP, UNITS))

HEADS = 10
HEAD_AT = [(0, 0, 64), (0, 64, 64), (1, 0, 64), (1, 64, 64)] + \
          [(2, 32 * j, 32) for j in range(4)] + [(3, 0, 32), (3, 32, 32)]
GROUPS = [(0, 2), (1, 3), (4, 8), (5, 9), (6,), (7,)]
SLOT = {h: i for i, h in enumerate([h for g in GROUPS for h in g])}
FIRST_SLOT = [sum(len(g) for g in GROUPS[:i]) for i in range(len(GROUPS))]
LEVELS = [0, 1, 2, 4, 8, 16, 32]
SMALL = [l for l, h in enumerate(LEVELS) if 2 * h <= DEC_SEQ]

LIN = (["sum_pre", "hf0", "hf1", "gq1", "z0", "z1", "hq0", "hq1", "gq0", "gk0", "gk1"]
       + ["vs0", "vs1"]
       + IN2 + [f"rot{i}" for i in range(6)] + [f"sum_o{i}" for i in range(5)]
       + [f"pv{i}" for i in range(3)] + ["sum_att"]
       + [f"out{n}" for n in range(KT)] + ["sum_mix", "sum_mlp"] + [f"up{n}" for n in range(FT)]
       + ["sum_down"] + [f"gate{n}" for n in range(KT)])
Q = {name: i for i, name in enumerate(LIN)}
assert len(Q) == len(LIN)
SIDE = [f"ple{n}" for n in range(KT)] + [f"down{c}{n}" for c in range(CHUNKS) for n in range(KT)]
D = {name: i for i, name in enumerate(SIDE)}


def slot_of(r):
    return r % RAW if r < R_IN2 else (r - R_IN2) % RING if r < R_OUT else (r - R_OUT) % RAW


def former(r):
    return max((q for q in range(r) if slot_of(q) == slot_of(r)), default=None)


def loads(r):
    return sum(slot_of(q) == slot_of(r) for q in range(RAW, r + 1))

C_IDENT, C_ONES, C_HEADSUM, C_ROT = 0, P, 2 * P, 3 * P
C_COS = 4 * P
C_SIN = C_COS + T
C_RESET = C_SIN + T
C_BIAS = C_RESET + T
C_MASK = C_BIAS + 4 * P
C_BATCH = C_MASK + len(LEVELS) * CH
C_SBIAS = C_BATCH + DEC_BATCH
C_NBIAS = C_SBIAS + KEYS
C_SCALE = C_NBIAS + DEC_BATCH * NEW
C_EPS = C_SCALE + 1
C_END = C_EPS + 1
W_PRE, W_MIX, W_MLP, W_DOWN, W_O = 0, 8, 16, 24, 32
W_B = 40
W_LB = 42
W_FLAG = 46
W_G2 = 47
W_END = W_G2 + 2 * P


def multiplicity(delta):
    m = np.zeros(delta.shape)
    for w, d in PATTERNS:
        m += (delta >= 0) & (delta <= w) & (delta % d == 0)
    return np.where(m > 0, np.log(np.maximum(m, 1)), NEG).astype(np.float32)


def cache_order():
    j = np.arange(WIN)
    wide = (j < WIN - 512) & (j % 16 < DEC_SEQ)
    read = np.concatenate([j[wide], j[j >= WIN - 512]])
    assert len(read) == KEYS and (read[:DEC_SEQ] == np.arange(DEC_SEQ)).all()
    return np.concatenate([read, j[(j < WIN - 512) & ~wide]])


def constants():
    c = np.zeros((P, C_END), np.float32)
    r = np.arange(P)
    c[:, C_IDENT:C_IDENT + P] = np.eye(P)
    c[:, C_ONES:C_ONES + P] = 1
    c[:, C_HEADSUM:C_HEADSUM + P] = (r[:, None] // 64 == r[None] // 64)
    d = r % 64
    rot = np.zeros((P, P), np.float32)
    for m in range(P):
        if d[m] < 8:
            rot[m + 8, m] = -1
        elif d[m] < 16:
            rot[m - 8, m] = 1
    c[:, C_ROT:C_ROT + P] = rot
    pos = np.concatenate([np.arange(SEQ), PAST + np.arange(NEW) % DEC_SEQ]).astype(np.float32)
    inv = np.exp((-math.log(ROPE_THETA) * np.arange(8, dtype=np.float32) * np.float32(2.0 / 16)).astype(np.float32))
    ang = (pos[None] * inv.astype(np.float32)[:, None]).astype(np.float32).astype(np.float64)
    c[:, C_COS:C_COS + T] = np.where(d[:, None] < 16, np.cos(ang)[d % 8], 1)
    c[:, C_SIN:C_SIN + T] = np.where(d[:, None] < 16, np.sin(ang)[d % 8], 0)
    t = np.arange(T)
    c[:, C_RESET:C_RESET + T] = np.where(t < SEQ, t % CH != 0, t % DEC_SEQ != 0)
    for j in range(4):
        c[:, C_BIAS + P * j:C_BIAS + P * (j + 1)] = multiplicity((3 - j) * P + r[:, None] - r[None])
    s, u = r % CH, np.arange(CH)
    for l, h in enumerate(LEVELS):
        m = (s[:, None] == u) if h == 0 else \
            (s[:, None] // (2 * h) == u // (2 * h)) & (s[:, None] % (2 * h) < h) & (u % (2 * h) >= h)
        c[:, C_MASK + CH * l:C_MASK + CH * (l + 1)] = m
    for b in range(DEC_BATCH):
        c[:NEW, C_BATCH + b] = (r[:NEW] // DEC_SEQ == b)
    q = np.arange(48) % DEC_SEQ
    c[:48, C_SBIAS:C_SBIAS + KEYS] = multiplicity(WIN + q[:, None] - cache_order()[None, :KEYS])
    n = np.arange(NEW)
    for b in range(DEC_BATCH):
        c[:48, C_NBIAS + NEW * b:C_NBIAS + NEW * (b + 1)] = \
            np.where(n // DEC_SEQ == b, multiplicity(q[:, None] - n[None] % DEC_SEQ), NEG)
    c[:, C_SCALE] = np.where(r < 64, 32.0 ** -0.5, 1)
    c[:, C_EPS] = EPS
    return c


class Steps:

    def __init__(self, eng, sem):
        self.eng, self.sem, self.n = eng, sem, 0

    def mark(self, ins):
        self.n += 1
        ins.then_inc(self.sem, 1)
        return self.n

    def step(self, ins):
        self.eng.wait_ge(self.sem, self.mark(ins))

    def after(self, n):
        self.eng.wait_ge(self.sem, n)


def build(nc, x_t, consts, params, w_first, p_t, s0_in, w_units, ck, cv,
          y_out, kp_out, kn_out, vp_out, vn_out, ck_out, cv_out, sp_out, ss_out):
    with ExitStack() as ctx:
        def sb(name, cols):
            return ctx.enter_context(nc.sbuf_tensor(name, [P, cols], F32))

        sems = []

        def sem(name):
            sems.append(ctx.enter_context(nc.semaphore(name)))
            return sems[-1]

        h_sb = sb("h", KT * T)
        x_sb = sb("x", KT * T)
        pt_sb = sb("pt", 2 * T)
        raw_sb = sb("raw", RAW * 1024)
        con = sb("con", C_END)
        par = sb("par", W_END)
        ebl_sb = sb("ebl", 4 * 16)
        small = sb("small", 64)
        H = h_sb[:, :].rearrange("p (k t) -> p k t", k=KT)
        X = x_sb[:, :].rearrange("p (k t) -> p k t", k=KT)
        PT_IN = pt_sb[:, :].rearrange("p (k t) -> p k t", k=2)
        EBL = ebl_sb[:, :].rearrange("p (r c) -> p r c", r=4)

        IDENT, ONES = con[:, C_IDENT:C_IDENT + P], con[:, C_ONES:C_ONES + P]
        HEADSUM, ROT = con[:, C_HEADSUM:C_HEADSUM + P], con[:, C_ROT:C_ROT + P]
        COS, SIN, RESET = con[:, C_COS:C_COS + T], con[:, C_SIN:C_SIN + T], con[:, C_RESET:C_RESET + T]
        EPS_C = con[:, C_EPS:C_EPS + 1]
        NMAX, SUM, REC = small[:, 0:3], small[:, 4:7], small[:, 8:11]
        NMAXS, SUMS, RECS = small[:, 12:14], small[:, 14:16], small[:, 16:19]
        TABLE = {f"sum_{n}": small[:, 40 + i:41 + i] for i, n in enumerate(("pre", "o", "att", "mix", "mlp", "down"))}
        LB, OMLB, LBT = small[:, 20:22], small[:, 22:24], small[:, 24:32]

        pair = [ctx.enter_context(nc.psum_tensor(f"pair{i}", [P, 2, 512], F32)) for i in range(4)]
        bank = [pair[i // 2][:, i % 2] for i in range(8)]

        s_con, s_x = ctx.enter_context(nc.semaphore("s_con")), ctx.enter_context(nc.semaphore("s_x"))
        s_sq, s_acc = ctx.enter_context(nc.semaphore("s_sq")), ctx.enter_context(nc.semaphore("s_acc"))
        s_par0 = ctx.enter_context(nc.semaphore("s_par0"))
        s_w0 = [ctx.enter_context(nc.semaphore(f"s_w0_{i}")) for i in range(RAW)]
        s_y = ctx.enter_context(nc.semaphore("s_y"))
        copied = ctx.enter_context(nc.semaphore("copied"))
        s_par, s_first, s_pt, s_s0 = sem("s_par"), sem("s_first"), sem("s_pt"), sem("s_s0")
        w_landed = [sem(f"w_landed{i}") for i in range(RING)]
        w_hi, w_split = sem("w_hi"), sem("w_split")
        x_hi, x_split, u_sq, u_hi, u_split = (sem(n) for n in ("x_hi", "x_split", "u_sq", "u_hi", "u_split"))
        v_used, v_ev = sem("v_used"), sem("v_ev")
        y_normed = sem("y_normed")
        side_mm, side_ev = sem("side_mm"), sem("side_ev")
        act_steps_m, dve_steps_m, dve_steps_b = sem("act_steps_m"), sem("dve_steps_m"), sem("dve_steps_b")
        lin_mm, lin_ev = sem("lin_mm"), sem("lin_ev")
        act_steps, dve_steps, pool_steps = sem("act_steps"), sem("dve_steps"), sem("pool_steps")
        sq_pre, acc_pre, xn_ready, rs_ready = sem("sq_pre"), sem("acc_pre"), sem("xn_ready"), sem("rs_ready")
        acc_ready = sem("acc_ready")
        hf_sig, f_ready, z_log, g_ready, b_ready = (sem(n) for n in ("hf_sig", "f_ready", "z_log", "g_ready", "b_ready"))
        lb_exp = sem("lb_exp")
        eb_exp, qi_ready, kd_diff, kd_exp, kd_ready = (sem(n) for n in ("eb_exp", "qi_ready", "kd_diff", "kd_exp", "kd_ready"))
        kdt_mm, kdt_ev = sem("kdt_mm"), sem("kdt_ev")
        u_mm, u_ev = sem("u_mm"), sem("u_ev")
        in_mm, in_ev = sem("in_mm"), sem("in_ev")
        vx_ready, us_mm, us_ev = sem("vx_ready"), sem("us_mm"), sem("us_ev")
        oi_zero, at_zero, qb_zero = sem("oi_zero"), sem("at_zero"), sem("qb_zero")
        st_out = sem("st_out")
        lv_diff, lv_exp, lv_ready = sem("lv_diff"), sem("lv_exp"), sem("lv_ready")
        lv_mm, lv_ev, ls_mm, ls_ev = sem("lv_mm"), sem("lv_ev"), sem("ls_mm"), sem("ls_ev")
        ia_mm, o_ready = sem("ia_mm"), sem("o_ready")
        gate_sig, gate_ready, sqo = sem("gate_sig"), sem("gate_ready"), sem("sqo")
        rot_ready, qb_ready, kv_out = sem("rot_ready"), sem("qb_ready"), sem("kv_out")
        ps_mm, ps_max, ps_exp, ps_p = sem("ps_mm"), sem("ps_max"), sem("ps_exp"), sem("ps_p")
        pt_mm, pt_ev = sem("pt_mm"), sem("pt_ev")
        k_landed, v_landed = [[sem(f"{n}_landed{i}") for i in range(2)] for n in "kv"]
        ss_mm, ss_read, ss_max, ss_exp, ss_p = sem("ss_mm"), sem("ss_read"), sem("ss_max"), sem("ss_exp"), sem("ss_p")
        sp_mm, sp_ev, so_mm, os_ev, st_mm, so_ev = (sem(n) for n in ("sp_mm", "sp_ev", "so_mm", "os_ev", "st_mm", "so_ev"))
        sqa, att_ready = sem("sqa"), sem("att_ready")
        sq_mix, sq_h, h_mix = sem("sq_mix"), sem("sq_h"), sem("h_mix")
        acc_mix, acc_h, xm_ready = sem("acc_mix"), sem("acc_h"), sem("xm_ready")
        sq_down, acc_down, h_down, z_used = sem("sq_down"), sem("acc_down"), sem("h_down"), sem("z_used")

        first, last = min(s.num for s in sems), max(s.num for s in sems)
        assert last - first + 1 == len(sems)

        def used_up(r):
            if r < R_V:
                return lin_mm, Q[IN1[r]] + 1
            if r < R_IN2:
                return v_used, r - R_V + 1
            if r < R_OUT:
                return lin_mm, Q[IN2[r - R_IN2]] + 1
            if r < R_PLE:
                return lin_mm, Q[f"out{r - R_OUT}"] + 1
            if r < R_UP:
                return side_mm, D[f"ple{4 * (r - R_PLE) + 3}"] + 1
            if r < R_GATE:
                c, j = divmod(r - R_UP, 2 * KT)
                return (lin_mm, Q[f"up{c * KT + j}"] + 1) if j < KT else (side_mm, D[f"down{c}{j - KT}"] + 1)
            return lin_mm, Q[f"gate{r - R_GATE}"] + 1

        def freed(r):
            return (w_split, SPLIT.index(r) + 1) if r in SPLIT else used_up(r)

        def blocks(tile, h, half):
            if 2 * h <= DEC_SEQ:
                v = tile.rearrange("p r (n w) -> p (r n) w", w=2 * h)
                n = 4 * T // (2 * h)
                return v[:, :, half * h:half * h + h], v[:, :, h - 1:h].to_broadcast([P, n, h])
            v = tile[:, :, 0:SEQ].rearrange("p r (n w) -> p r n w", w=2 * h)
            return v[:, :, :, half * h:half * h + h], v[:, :, :, h - 1:h].to_broadcast([P, 4, SEQ // (2 * h), h])

        def last_of(tile, sample):
            if sample:
                return tile[:, :, SEQ:T].rearrange("p r (n w) -> p r n w", w=DEC_SEQ)[:, :, :, DEC_SEQ - 1:DEC_SEQ]
            return tile[:, :, 0:SEQ].rearrange("p r (n w) -> p r n w", w=CH)[:, :, :, CH - 1:CH]

        def chunks_of(tile, sample):
            if sample:
                return tile[:, :, SEQ:T].rearrange("p r (n w) -> p r n w", w=DEC_SEQ)
            return tile[:, :, 0:SEQ].rearrange("p r (n w) -> p r n w", w=CH)

        def v_cols(h):
            return 64 * h

        with nc.Block() as block:
            @block.sync
            def _(sp):
                sp.dma_start(h_sb[:, :], x_t).then_inc(s_x, 16)
                sp.dma_start(con[:, :], consts).then_inc(s_con, 16)
                sp.dma_start(par[:, :], params[0]).then_inc(s_par0, 16)
                for i in range(RAW):
                    sp.dma_start(raw_sb[:, i * 1024:(i + 1) * 1024], w_first[0, i * P:(i + 1) * P, :]).then_inc(s_w0[i], 16)
                sp.wait_ge(s_con, 16)

            @block.scalar
            def _(act):
                act.wait_ge(s_x, 16)
                for k in range(KT):
                    nc.scalar.activation(X[:, k], H[:, k], ACT.Square).then_inc(s_sq, 1)

            @block.vector
            def _(dve):
                for k in range(1, KT):
                    dve.wait_ge(s_sq, k + 1)
                    if k >= 2:
                        dve.wait_ge(s_acc, k - 1)
                    nc.vector.tensor_tensor(X[:, 0], X[:, 0], X[:, k], ALU.add).then_inc(s_acc, 1)

        with nc.Fori(0, DEPTH) as layer:
            def of_layer(dram, *rest):
                names = "abcde"[:len(dram.shape) - 1]
                return dram[bass.ds(layer, 1)].rearrange(f"l {' '.join(names)} -> (l {names[0]}) {' '.join(names[1:])}")

            def copy_cache(pool, b):
                pool.dma_start(of_layer(ck_out)[b * 384:(b + 1) * 384, :],
                               of_layer(ck)[b * 384:(b + 1) * 384, DEC_SEQ:WIN]).then_inc(copied, 16)
                pool.dma_start(of_layer(cv_out)[b * KEPT:(b + 1) * KEPT, :],
                               of_layer(cv)[b * WIN + DEC_SEQ:(b + 1) * WIN, :]).then_inc(copied, 16)

            mixer = ExitStack()
            arena = mixer.enter_context(nc.sbuf_tensor("arena", [P, 16640], F32))
            Q4, K4, V = (arena[:, a:a + n * w].rearrange("p (a t) -> p a t", a=n)
                         for a, n, w in ((0, 4, T), (4 * T, 4, T), (4608, 5, 1024)))
            B, LV0, LV1 = (arena[:, a:a + 4 * T].rearrange("p (a t) -> p a t", a=4) for a in (9728, 12032, 14336))
            LV = [LV0, LV1]
            with nc.sbuf_tensor("xn_hi_part", [P, KT * T], F32R) as xh_sb, \
                    nc.sbuf_tensor("xn_lo_part", [P, KT * T], F32R) as xl_sb, \
                    nc.sbuf_tensor("win_hi_part", [P, SPLITS * 1024], F32R) as wh_sb, \
                    nc.sbuf_tensor("win_lo_part", [P, SPLITS * 1024], F32R) as wl_sb, nc.Block() as block:
                XH, XL = (v[:, :].rearrange("p (k t) -> p k t", k=KT) for v in (xh_sb, xl_sb))
                SUM_PRE = X[:, 0]
                RS = arena[:, 9728:9728 + T]
                proj = {"hf0": K4[:, 0], "hf1": K4[:, 1], "gq1": Q4[:, 3], "hq0": Q4[:, 0], "hq1": Q4[:, 1],
                        "gq0": Q4[:, 2], "gk0": K4[:, 2], "gk1": K4[:, 3]}

                def raw(r):
                    return raw_sb[:, slot_of(r) * 1024:(slot_of(r) + 1) * 1024]

                def w_part(sb_, i):
                    return sb_[:, (i % SPLITS) * 1024:(i % SPLITS + 1) * 1024]

                @block.sync
                def _(sp):
                    for r in range(RAW, R_IN2 + RAW):
                        sp.wait_ge(*freed(former(r)))
                        sp.dma_start(raw(r), of_layer(w_units)[r * P:(r + 1) * P, :]).then_inc(w_landed[slot_of(r)], 16)
                    sp.dma_start(pt_sb[:, :], of_layer(p_t)).then_inc(s_pt, 16)

                @block.gpsimd
                def _(pool):
                    pool.wait_ge(lin_mm, 2)
                    copy_cache(pool, 0)

                @block.tensor
                def _(pe):
                    def claim(name):
                        q = Q[name]
                        if q >= 2:
                            pe.wait_ge(lin_ev, q - 1)
                        return pair[q % 2]

                    ps = claim("sum_pre")
                    for half in range(2):
                        mm = nc.tensor.matmul(ps[:, half, 0:HALF], ONES, SUM_PRE[:, half * HALF:(half + 1) * HALF],
                                              start=True, stop=True)
                    mm.then_inc(lin_mm, 1)
                    for i, name in enumerate(IN1):
                        ps = claim(name)
                        pe.wait_ge(w_split, i + 1)
                        wh, wl = w_part(wh_sb, i), w_part(wl_sb, i)
                        for k in range(KT):
                            if i == 0:
                                pe.wait_ge(x_split, k + 1)
                            cols = slice(k * P, (k + 1) * P)
                            for half in range(2):
                                out, t = ps[:, half, 0:HALF], slice(half * HALF, (half + 1) * HALF)
                                nc.tensor.matmul(out, wh[:, cols], XH[:, k, t], start=k == 0, stop=False)
                                nc.tensor.matmul(out, wh[:, cols], XL[:, k, t], start=False, stop=False)
                                mm = nc.tensor.matmul(out, wl[:, cols], XH[:, k, t], start=False, stop=k == KT - 1)
                        mm.then_inc(lin_mm, 1)
                        if name == "gq1":
                            pe.wait_ge(s_par0, 16)
                            pe.wait_ge(lin_ev, Q["gq1"] + 1)
                            for z in range(2):
                                ps = claim(f"z{z}")
                                for half in range(2):
                                    mm = nc.tensor.matmul(ps[:, half, 0:HALF], par[64:80, W_G2 + P * z:W_G2 + P * (z + 1)],
                                                          Q4[64:80, 3, half * HALF:(half + 1) * HALF], start=True, stop=True)
                                mm.then_inc(lin_mm, 1)
                    for g in range(2):
                        ps = claim(f"vs{g}")
                        for j in range(4):
                            i = R_V + 4 * g + j
                            pe.wait_ge(w_split, i + 1)
                            for tt in (TT, 0, 1, 2, 3):
                                if g > 0 and j == 0 and tt < TT:
                                    pe.wait_ge(v_ev, tt + 1)
                                out = ps[:, 0, :] if tt == TT else bank[4 + tt]
                                t = slice(tt * P, (tt + 1) * P) if tt < TT else slice(T - P, T)
                                for k2 in range(2):
                                    k, w = 2 * j + k2, slice(512 * k2, 512 * k2 + 512)
                                    wh, wl = w_part(wh_sb, i)[:, w], w_part(wl_sb, i)[:, w]
                                    nc.tensor.matmul(out, XH[:, k, t], wh, start=k == 0, stop=False)
                                    nc.tensor.matmul(out, XH[:, k, t], wl, start=False, stop=False)
                                    mm = nc.tensor.matmul(out, XL[:, k, t], wh, start=False, stop=k == KT - 1)
                                if tt == TT and j == 3:
                                    mm.then_inc(lin_mm, 1)
                            mm.then_inc(v_used, 1)

                @block.scalar
                def _(act):
                    st = Steps(act, act_steps)
                    A = nc.scalar.activation

                    def two(ap):
                        return ap.rearrange("p (a t) -> p a t", a=2)

                    def evac(name, dst, func=ACT.Copy, **kw):
                        act.wait_ge(lin_mm, Q[name] + 1)
                        A(two(dst), pair[Q[name] % 2][:, :, 0:HALF], func, **kw).then_inc(lin_ev, 1)

                    def leading(dst, src, done):
                        return A(dst, src, ACT.Copy).then_inc(done, 1)

                    def split_w(i):
                        if i < RAW:
                            act.wait_ge(s_w0[i], 16)
                        else:
                            act.wait_ge(w_landed[slot_of(i)], 16 * loads(i))
                        if i >= SPLITS:
                            act.wait_ge(*used_up(i - SPLITS))
                        leading(w_part(wh_sb, i), raw(i), w_hi)

                    split_w(0)
                    A(TABLE["sum_pre"], EPS_C, ACT.Ln)
                    act.wait_ge(lin_mm, Q["sum_pre"] + 1)
                    A(two(RS), pair[Q["sum_pre"] % 2][:, :, 0:HALF], ACT.Ln, scale=1.0 / D_MODEL, bias=EPS_C).then_inc(lin_ev, 1)
                    act.wait_ge(lin_ev, Q["sum_pre"] + 1)
                    A(RS, RS, ACT.Exp, scale=-0.5).then_inc(rs_ready, 1)
                    for k in range(KT):
                        act.wait_ge(xn_ready, k + 1)
                        leading(XH[:, k], X[:, k], x_hi)
                    split_w(1)
                    split_w(2)
                    act.wait_ge(lb_exp, 1)
                    A(LBT[:, 2:6], LBT[:, 2:6], ACT.Exp).then_inc(lb_exp, 1)
                    evac("hf0", proj["hf0"])
                    split_w(3)
                    evac("hf1", proj["hf1"])
                    act.wait_ge(lin_ev, Q["hf1"] + 1)
                    A(LV[0][:, 0:2], K4[:, 0:2], ACT.Sigmoid).then_inc(hf_sig, 1)
                    split_w(4)
                    evac("gq1", proj["gq1"], scale=con[:, C_SCALE:C_SCALE + 1])
                    split_w(5)
                    act.wait_ge(s_par0, 16)
                    evac("z0", LV[1][:, 0], ACT.Identity, bias=par[:, W_B:W_B + 1])
                    evac("z1", LV[1][:, 1], ACT.Identity, bias=par[:, W_B + 1:W_B + 2])
                    evac("hq0", proj["hq0"])
                    split_w(6)
                    evac("hq1", proj["hq1"])
                    split_w(7)
                    act.wait_ge(lin_ev, Q["z1"] + 1)
                    st.step(A(LV[1][:, 2:4], LV[1][:, 0:2], ACT.Abs))
                    st.step(A(LV[1][:, 2:4], LV[1][:, 2:4], ACT.Exp, scale=-1.0))
                    A(LV[1][:, 2:4], LV[1][:, 2:4], ACT.Ln, bias=1.0).then_inc(z_log, 1)
                    act.wait_ge(f_ready, 1)
                    A(LV[0][:, 0:2], LV[0][:, 0:2], ACT.Ln).then_inc(g_ready, 1)
                    evac("gq0", proj["gq0"], scale=32.0 ** -0.5)
                    split_w(8)
                    evac("gk0", proj["gk0"])
                    split_w(9)
                    evac("gk1", proj["gk1"])
                    split_w(10)
                    act.wait_ge(b_ready, 4)
                    A(LV[1], B, ACT.Exp).then_inc(eb_exp, 1)
                    split_w(11)
                    act.wait_ge(kd_diff, 2)
                    A(LV[0], LV[0], ACT.Exp).then_inc(kd_exp, 1)
                    split_w(12)
                    split_w(13)
                    for g in range(2):
                        act.wait_ge(v_used, 4 * (g + 1))
                        A(V[0:NEW, TT, 512 * g:512 * g + 512], pair[Q[f"vs{g}"] % 2][P - NEW:P, 0, :], ACT.Copy).then_inc(lin_ev, 1)
                        for tt in range(TT):
                            A(V[:, tt, 512 * g:512 * g + 512], bank[4 + tt], ACT.Copy).then_inc(v_ev, 1)
                            if g == 0 and tt in (1, 3):
                                split_w(14 + tt // 2)

                @block.vector
                def _(dve):
                    st = Steps(dve, dve_steps)
                    tt_, ts_, stt = nc.vector.tensor_tensor, nc.vector.tensor_scalar, nc.vector.scalar_tensor_tensor

                    def remainder(dst, src, hi, done):
                        return tt_(dst, src, hi.bitcast(F32), ALU.subtract).then_inc(done, 1)

                    def split_w(i):
                        dve.wait_ge(w_hi, i + 1)
                        remainder(w_part(wl_sb, i), raw(i), w_part(wh_sb, i), w_split)

                    dve.wait_ge(s_par0, 16)
                    st.step(tt_(LBT[:, 0:2], par[:, W_LB:W_LB + 2], par[:, W_LB + 2:W_LB + 4], ALU.max))
                    st.mark(tt_(LBT[:, 2:4], par[:, W_LB:W_LB + 2], LBT[:, 0:2], ALU.subtract))
                    tt_(LBT[:, 4:6], par[:, W_LB + 2:W_LB + 4], LBT[:, 0:2], ALU.subtract).then_inc(lb_exp, 1)
                    dve.wait_ge(dve_steps, st.n)
                    split_w(0)
                    dve.wait_ge(rs_ready, 1)
                    for k in range(KT + 1):
                        if k < KT:
                            stt(X[:, k], H[:, k], par[:, W_PRE + k:W_PRE + k + 1], RS, ALU.mult, ALU.mult).then_inc(xn_ready, 1)
                        if k >= 1:
                            dve.wait_ge(x_hi, k)
                            remainder(XL[:, k - 1], X[:, k - 1], XH[:, k - 1], x_split)
                    split_w(1)
                    split_w(2)
                    dve.wait_ge(lb_exp, 2)
                    st.step(tt_(LBT[:, 6:8], LBT[:, 2:4], LBT[:, 4:6], ALU.add))
                    st.step(nc.vector.reciprocal(LBT[:, 6:8], LBT[:, 6:8]))
                    st.step(tt_(LBT[:, 6:8], LBT[:, 6:8], LBT[:, 4:6], ALU.mult))
                    st.step(ts_(LB, LBT[:, 6:8], par[:, W_FLAG:W_FLAG + 1], None, ALU.mult))
                    st.step(ts_(OMLB, LB, -1.0, 1.0, ALU.mult, ALU.add))
                    split_w(3)
                    dve.wait_ge(hf_sig, 1)
                    f = LV[0][:, 0:2]
                    for i in range(2):
                        n = st.mark(ts_(f[:, i], f[:, i], OMLB[:, i:i + 1], LB[:, i:i + 1], ALU.mult, ALU.add))
                    st.after(n)
                    ts_(K4[:, 0:2], f, -1.0, 1.0, ALU.mult, ALU.add).then_inc(f_ready, 1)
                    for i in range(4, 8):
                        split_w(i)
                    dve.wait_ge(z_log, 1)
                    st.step(stt(LV[0][:, 2:4], LV[1][:, 0:2], 0.0, LV[1][:, 2:4], ALU.min, ALU.subtract))
                    st.step(ts_(LV[0][:, 2:4], LV[0][:, 2:4], 1.0 / 16, None, ALU.mult))
                    split_w(8)
                    dve.wait_ge(g_ready, 1)
                    for r in range(4):
                        nc.vector.tensor_tensor_scan(B[:, r], RESET, LV[0][:, r], 0.0, ALU.mult, ALU.add).then_inc(b_ready, 1)
                    split_w(9)
                    dve.wait_ge(b_ready, 4)
                    for s in range(2):
                        shape = [P, 4, NC, CH] if s == 0 else [P, 4, DEC_BATCH, DEC_SEQ]
                        tt_(chunks_of(LV[0], s), last_of(B, s).to_broadcast(shape), chunks_of(B, s),
                            ALU.subtract).then_inc(kd_diff, 1)
                    split_w(10)
                    split_w(11)
                    dve.wait_ge(eb_exp, 1)
                    n = st.mark(nc.vector.tensor_copy(EBL[:, :, 0:8], LV[1][:, :, CH - 1:SEQ:CH]))
                    n = st.mark(nc.vector.tensor_copy(EBL[:, :, 8:16], LV[1][:, :, SEQ + DEC_SEQ - 1:T:DEC_SEQ]))
                    dve.wait_ge(kd_exp, 1)
                    dve.wait_ge(lin_ev, Q["gk1"] + 1)
                    tt_(LV[0], LV[0], K4, ALU.mult).then_inc(kd_ready, 1)
                    for i in range(12, 16):
                        split_w(i)

            with nc.sbuf_tensor("tail", [P, 12544], F32) as tail, \
                    nc.sbuf_tensor("more", [P, (RING - RAW) * 1024], F32) as more_sb, nc.Block() as block:
                def at(off, n, count=None):
                    assert off >= 16640 or off + n <= 16640
                    v = arena[:, off:off + n] if off < 16640 else tail[:, off - 16640:off - 16640 + n]
                    return v if count is None else v.rearrange("p (a t) -> p a t", a=count)

                Q4, K4 = at(0, 4 * T, 4), at(4 * T, 4 * T, 4)
                V = at(4608, 5 * 1024, 5)
                B = at(9728, 4 * T, 4)
                LV = [at(12032, 4 * T, 4), at(14336, 4 * T, 4)]
                KDT = at(16640, 5 * 512, 5)
                AT = at(16640, HEADS * 4 * CH).rearrange("p (s c t) -> p s c t", s=HEADS, c=4)
                ATS = at(19200, HEADS * CH, HEADS)
                OI = at(19840, 5 * T, 5)
                QI = at(22720, 4 * T, 4)
                SC = at(25024, NC * 256).rearrange("p (c r v) -> p c r v", c=NC, r=4)
                S0 = at(27072, DEC_BATCH * 256).rearrange("p (b r v) -> p b r v", b=DEC_BATCH, r=4)
                VX = [LV[1][:, 0:1, 0:512], LV[1][:, 1:2, 0:512]]
                ROTQK = at(22720, 6 * T, 6)
                GATES = at(26176, 5 * T, 5)
                proj = {}
                for i, n in enumerate(IN2):
                    proj[n] = ROTQK[:, i] if i < 6 else GATES[:, i - 6]
                ETMP = more_sb[:, 0:5 * T].rearrange("p (a t) -> p a t", a=5)
                SQO = at(9728, 5 * T, 5)
                RSO = [at(12608 + i * T, T) for i in range(5)]
                KB = [at(0, 3 * KEYS, 3), at(9728, 3 * KEYS, 3)]
                VB = [at(16640, KC * 384, KC), more_sb[:, 0:KC * 384].rearrange("p (a t) -> p a t", a=KC)]
                PTB = [at(13568, 528), at(14096, 528)]
                PTP = [at(14624, 512), at(15136, 512)]
                SMP = [at(26176 + 512 * i, 512) for i in range(3)]
                SMS = [at(26176 + 1344 * i, 1344) for i in range(2)]
                OS = [at(3840 + 384 * i, 384) for i in range(2)]
                ROTMP = [more_sb[:, (5 + i) * T:(6 + i) * T] for i in range(2)]

                def qbd(b):
                    return V[:, b // 4, 144 * (b % 4):144 * (b % 4) + 144].rearrange("p (c n) -> p c n", c=3)

                SQA = at(0, 3 * T, 3)
                ACCA, RSA = at(3 * T, T), at(4 * T, T)
                def wslot(r):
                    i = slot_of(r)
                    return raw_sb[:, i * 1024:(i + 1) * 1024] if i < RAW else more_sb[:, (i - RAW) * 1024:(i - RAW + 1) * 1024]

                def load(sp, r):
                    if former(r) is not None:
                        sp.wait_ge(*freed(former(r)))
                    sp.dma_start(wslot(r), of_layer(w_units)[r * P:(r + 1) * P, :]).then_inc(w_landed[slot_of(r)], 16)

                @block.sync
                def _(sp):
                    sp.dma_start(at(27072, 2048), of_layer(s0_in)).then_inc(s_s0, 16)
                    for r in range(R_IN2 + RAW, R_IN2 + RING):
                        load(sp, r)
                    sp.wait_ge(u_ev, NC)
                    sp.dma_start(of_layer(sp_out), at(25024 + (NC - 1) * 256, 256)).then_inc(st_out, 16)
                    sp.wait_ge(us_ev, 4)
                    sp.dma_start(of_layer(ss_out), at(27072, 2048)).then_inc(st_out, 16)
                    for r in range(R_IN2 + RING, R_OUT):
                        load(sp, r)
                    sp.wait_ge(rot_ready, 6)
                    qk = at(22720, 6 * T, 6)
                    sp.dma_start(of_layer(kp_out).rearrange("p (c t) -> p c t", c=3), qk[:, 3:6, 0:SEQ]).then_inc(kv_out, 16)
                    sp.dma_start(of_layer(kn_out).rearrange("p (c t) -> p c t", c=3), qk[:, 3:6, SEQ:T]).then_inc(kv_out, 16)
                    sp.dma_start(of_layer(vp_out).rearrange("p (c t) -> p c t", c=TT), V[:, 0:TT, 640:1024]).then_inc(kv_out, 16)
                    sp.dma_start(of_layer(vn_out), V[0:NEW, TT, 640:1024]).then_inc(kv_out, 16)
                    def load_keys(b):
                        if b >= 2:
                            sp.wait_ge(ss_mm, b - 1)
                        sp.dma_start(KB[b % 2], of_layer(ck)[b * 384:(b + 1) * 384, 0:KEYS]
                                     .rearrange("(c p) n -> p c n", p=P)).then_inc(k_landed[b % 2], 16)

                    def load_values(b):
                        if b >= 2:
                            sp.wait_ge(so_mm, b - 1)
                        sp.dma_start(VB[b % 2], of_layer(cv)[b * WIN:b * WIN + KEYS, :]
                                     .rearrange("(c p) n -> p c n", p=P)).then_inc(v_landed[b % 2], 16)

                    sp.wait_ge(gate_ready, 6)
                    load_keys(0)
                    load_keys(1)
                    load_values(0)
                    for b in range(2, DEC_BATCH):
                        load_keys(b)
                        load_values(b - 1)
                    load_values(DEC_BATCH - 1)
                    for r in range(R_OUT, R_OUT + RAW):
                        load(sp, r)
                    sp.wait_ge(st_out, 32)
                    sp.wait_ge(kv_out, 64)

                @block.gpsimd
                def _(pool):
                    nc.gpsimd.memset(OI[:, :, 0:CH], 0.0).then_inc(oi_zero, 1)

                    for h in range(HEADS):
                        if h == 0:
                            pool.wait_ge(qi_ready, 1)
                        if h >= 2:
                            pool.wait_ge(us_mm, h - 1)
                        vx = VX[h % 2][0:NEW].rearrange("p a (b v) -> p (a b) v", v=64)
                        nc.gpsimd.tensor_tensor(
                            vx, V[0:NEW, TT, v_cols(h):v_cols(h) + 64].rearrange("p (a v) -> p a v", a=1).to_broadcast([NEW, DEC_BATCH, 64]),
                            con[0:NEW, C_BATCH:C_BATCH + DEC_BATCH].rearrange("p (b a) -> p b a", a=1).to_broadcast([NEW, DEC_BATCH, 64]),
                            ALU.mult).then_inc(vx_ready, 1)
                    pool.wait_ge(us_mm, HEADS)
                    nc.gpsimd.memset(at(16640, 3200), 0.0).then_inc(at_zero, 1)
                    copy_cache(pool, 1)
                    pool.wait_ge(gate_sig, 1)
                    nc.gpsimd.tensor_tensor(GATES, GATES, ETMP, ALU.mult).then_inc(gate_ready, 1)
                    pool.wait_ge(ia_mm, 5)
                    nc.gpsimd.memset(V[:, 0, 0:T], 0.0).then_inc(qb_zero, 1)
                    nc.gpsimd.memset(V[:, 1, 0:T], 0.0).then_inc(qb_zero, 1)
                    pool.wait_ge(qb_zero, 2)
                    pool.wait_ge(rot_ready, 6)
                    for g in range(2):
                        for h in range(6):
                            c, hp = h // 2, h % 2
                            rows = slice(64 * hp, 64 * hp + 64)
                            dst = V[rows, g, 0:T].rearrange("p (b c n) -> p b c n", b=4, c=3)[:, :, c, 8 * h:8 * h + 8]
                            src = ROTQK[rows, c, SEQ + 32 * g:SEQ + 32 * g + 32].rearrange("p (b t) -> p b t", b=4)
                            nc.gpsimd.tensor_copy(dst, src).then_inc(qb_ready, 1)

                @block.tensor
                def _(pe):
                    def claim(name):
                        q = Q[name]
                        if q >= 2:
                            pe.wait_ge(lin_ev, q - 1)
                        return pair[q % 2]

                    def land(r):
                        pe.wait_ge(w_landed[slot_of(r)], 16 * loads(r))

                    def project(name, r):
                        ps = claim(name)
                        land(r)
                        for half in range(2):
                            for k in range(KT):
                                mm = nc.tensor.matmul(ps[:, half, 0:HALF], wslot(r)[:, k * P:(k + 1) * P],
                                                      X[:, k, half * HALF:(half + 1) * HALF], start=k == 0, stop=k == KT - 1)
                        mm.then_inc(lin_mm, 1)

                    def total(name, lhsT, tiles, ready):
                        ps = claim(name)
                        pe.wait_ge(*ready)
                        for half in range(2):
                            for i, t in enumerate(tiles):
                                mm = nc.tensor.matmul(ps[:, half, 0:HALF], lhsT, t[:, half * HALF:(half + 1) * HALF],
                                                      start=i == 0, stop=i == len(tiles) - 1)
                        mm.then_inc(lin_mm, 1)

                    pe.wait_ge(kd_ready, 1)
                    for tt in range(TT + 1):
                        m = P if tt < TT else NEW
                        if tt >= 2:
                            pe.wait_ge(kdt_ev, tt - 1)
                        for r in range(4):
                            mm = nc.tensor.transpose(bank[4 + tt % 2][0:m, r * P:(r + 1) * P],
                                                     LV[0][:, r, tt * P:tt * P + m], IDENT)
                        mm.then_inc(kdt_mm, 1)
                    for c in range(NC):
                        par_, tt = c % 2, c // 2
                        if c < 4:
                            pe.wait_ge(kdt_ev, TT + 1)
                        else:
                            pe.wait_ge(u_ev, c - 3)
                        rows = slice(64 * par_, 64 * par_ + 64)
                        for h in range(HEADS + 2):
                            r, row, n = HEAD_AT[h] if h < HEADS else (3, 64 + 32 * (h - HEADS), 32)
                            mm = nc.tensor.matmul(bank[4 + c % 4][row:row + n, r * 64:(r + 1) * 64],
                                                  KDT[rows, tt, r * P + row:r * P + row + n],
                                                  V[rows, tt, v_cols(h % HEADS):v_cols(h % HEADS) + 64],
                                                  start=True, stop=True)
                        mm.then_inc(u_mm, 1)
                    pe.wait_ge(qi_ready, 1)
                    pe.wait_ge(s_s0, 16)
                    for h in range(HEADS):
                        r, row, n = HEAD_AT[h]
                        o = 64 * (h % 2)
                        b_ = bank[4 + h % 2]
                        if h == 0:
                            pe.wait_ge(u_ev, NC)
                        if h >= 2:
                            pe.wait_ge(in_ev, h - 1)
                        for b in range(DEC_BATCH):
                            nc.tensor.matmul(b_[o:o + 64, b * DEC_SEQ:(b + 1) * DEC_SEQ], S0[row:row + n, b, r, :],
                                             QI[row:row + n, r, SEQ + b * DEC_SEQ:SEQ + (b + 1) * DEC_SEQ],
                                             start=True, stop=True)
                        for c in range(1, NC):
                            mm = nc.tensor.matmul(b_[o:o + 64, c * CH:(c + 1) * CH], SC[row:row + n, c - 1, r, :],
                                                  QI[row:row + n, r, c * CH:(c + 1) * CH], start=True, stop=True)
                        mm.then_inc(in_mm, 1)
                    for h in range(HEADS):
                        r, row, n = HEAD_AT[h]
                        if r >= 2 and row == 0:
                            pe.wait_ge(us_ev, r - 1)
                        pe.wait_ge(vx_ready, h + 1)
                        nc.tensor.matmul(bank[6 + r % 2][row:row + n, :], KDT[0:NEW, TT, r * P + row:r * P + row + n],
                                         VX[h % 2][0:NEW, 0, :], start=True, stop=True).then_inc(us_mm, 1)

                    def partners(i):
                        ps = claim(f"rot{i}")
                        if i == 0:
                            pe.wait_ge(lin_ev, Q["ak2"] + 1)
                        for half in range(2):
                            mm = nc.tensor.matmul(ps[:, half, 0:HALF], ROT, ROTQK[:, i, half * HALF:(half + 1) * HALF],
                                                  start=True, stop=True)
                        mm.then_inc(lin_mm, 1)

                    in2 = list(enumerate(IN2))
                    gi = si = 0
                    for l in range(len(LEVELS)):
                        if l == 0:
                            pe.wait_ge(in_ev, HEADS)
                            pe.wait_ge(us_ev, 4)
                            kq = (K4, Q4)
                        else:
                            pe.wait_ge(lv_ready, l)
                            kq = (LV[l % 2], LV[l % 2])
                        for g, heads in enumerate(GROUPS):
                            if l == len(LEVELS) - 1:
                                partners(g)
                            b_ = bank[4 + gi % 2]
                            if gi >= 2:
                                pe.wait_ge(lv_ev, gi - 1)
                            for i, h in enumerate(heads):
                                r, row, n = HEAD_AT[h]
                                for c in range(NC):
                                    o = 64 * (c % 2)
                                    col = (4 * i + c // 2) * CH
                                    mm = nc.tensor.matmul(b_[o:o + 64, col:col + CH],
                                                          kq[0][row:row + n, r, c * CH:(c + 1) * CH],
                                                          kq[1][row:row + n, r, c * CH:(c + 1) * CH], start=True, stop=True)
                            mm.then_inc(lv_mm, 1)
                            gi += 1
                            if l in SMALL:
                                b_ = bank[6 + si % 2]
                                if si >= 2:
                                    pe.wait_ge(ls_ev, si - 1)
                                for i, h in enumerate(heads):
                                    r, row, n = HEAD_AT[h]
                                    mm = nc.tensor.matmul(b_[0:NEW, i * CH:(i + 1) * CH], kq[0][row:row + n, r, SEQ:T],
                                                          kq[1][row:row + n, r, SEQ:T], start=True, stop=True)
                                mm.then_inc(ls_mm, 1)
                                si += 1
                        for _ in range(2 if l < 5 else 1):
                            if in2:
                                i, name = in2.pop(0)
                                project(name, R_IN2 + i)
                    assert not in2
                    for t in range(5):
                        ev, od = bank[4 + 2 * (t % 2)], bank[5 + 2 * (t % 2)]
                        if t == 0:
                            pe.wait_ge(lv_ev, gi)
                            pe.wait_ge(ls_ev, si)
                        if t >= 2:
                            pe.wait_ge(o_ready, t - 1)
                        for par_, b_ in ((0, ev), (1, od)):
                            rows = slice(64 * par_, 64 * par_ + 64)
                            for h in (2 * t, 2 * t + 1):
                                o = 64 * (h % 2)
                                for c in range(TT):
                                    mm = nc.tensor.matmul(b_[o:o + 64, c * CH:(c + 1) * CH],
                                                          V[rows, c, v_cols(h):v_cols(h) + 64], AT[rows, SLOT[h], c, :],
                                                          start=True, stop=True)
                                if par_ == 0:
                                    nc.tensor.matmul(b_[o:o + 64, TT * CH:(TT + 1) * CH],
                                                     V[0:NEW, TT, v_cols(h):v_cols(h) + 64], ATS[0:NEW, SLOT[h], :],
                                                     start=True, stop=True)
                        mm.then_inc(ia_mm, 1)
                    for i in range(5):
                        total(f"sum_o{i}", HEADSUM, [SQO[:, i]], (sqo, i + 1))
                    pe.wait_ge(rot_ready, 6)
                    units = [(h, qt) for h in range(6) for qt in range(TT)]

                    def scores(i):
                        h, qt = units[i]
                        rows = slice(64 * (h % 2), 64 * (h % 2) + 64)
                        if i >= 2:
                            pe.wait_ge(ps_max, i - 1)
                        nc.tensor.matmul(bank[4 + i % 2][:, 0:(qt + 1) * P], ROTQK[rows, h // 2, qt * P:(qt + 1) * P],
                                         ROTQK[rows, 3 + h // 2, 0:(qt + 1) * P], start=True, stop=True).then_inc(ps_mm, 1)

                    def turn(i):
                        h, qt = units[i]
                        pe.wait_ge(ps_p, i + 1)
                        if i >= 2:
                            pe.wait_ge(pt_ev, i - 1)
                        for kt in range(qt + 1):
                            mm = nc.tensor.transpose(bank[6 + i % 2][:, kt * P:(kt + 1) * P],
                                                     SMP[i % 3][:, kt * P:(kt + 1) * P], IDENT)
                        mm.then_inc(pt_mm, 1)

                    def weigh(i):
                        h, qt = units[i]
                        name = f"pv{h // 2}"
                        if h % 2 == 0 and qt == 0:
                            claim(name)
                        ps = pair[Q[name] % 2]
                        o = 64 * (h % 2)
                        pe.wait_ge(pt_ev, i + 1)
                        for kt in range(qt + 1):
                            mm = nc.tensor.matmul(ps[o:o + 64, 0, qt * P:(qt + 1) * P],
                                                  V[:, kt, 640 + 64 * h:704 + 64 * h], PTP[i % 2][:, kt * P:(kt + 1) * P],
                                                  start=kt == 0, stop=kt == qt)
                        if h % 2 == 1 and qt == TT - 1:
                            mm.then_inc(lin_mm, 1)

                    n = len(units)
                    scores(0)
                    scores(1)
                    for i in range(n + 1):
                        if i + 2 < n:
                            scores(i + 2)
                        if i < n:
                            turn(i)
                        if i >= 1:
                            weigh(i - 1)

                    def s_scores(b):
                        kb = KB[b % 2]
                        if b == 0:
                            pe.wait_ge(qb_ready, 12)
                            pe.wait_ge(lin_ev, Q["pv2"] + 1)
                        else:
                            pe.wait_ge(ss_read, b)
                        pe.wait_ge(k_landed[b % 2], 16 * (b // 2 + 1))
                        for j, (lo, w) in enumerate(((0, 512), (512, 512), (1024, 256))):
                            for c in range(3):
                                mm = nc.tensor.matmul(bank[j][0:48, 0:w], qbd(b)[:, c, :], kb[:, c, lo:lo + w],
                                                      start=c == 0, stop=c == 2)
                        for c in range(3):
                            mm = nc.tensor.matmul(bank[3][0:48, 0:NEW], qbd(b)[:, c, :], ROTQK[:, 3 + c, SEQ:T],
                                                  start=c == 0, stop=c == 2)
                        mm.then_inc(ss_mm, 1)

                    def s_turn(b):
                        pe.wait_ge(ss_exp, b + 1)
                        if b >= 1:
                            pe.wait_ge(sp_ev, b)
                        else:
                            pe.wait_ge(pt_ev, n)
                        for c in range(KC):
                            nc.tensor.transpose(bank[6][:, 48 * c:48 * c + 48], SMS[b % 2][0:48, c * P:(c + 1) * P],
                                                IDENT[0:48, 0:48])
                        nc.tensor.transpose(bank[5][0:NEW, 0:48], SMS[b % 2][0:48, KEYS:KEYS + NEW],
                                            IDENT[0:48, 0:48]).then_inc(sp_mm, 1)

                    def s_weigh(b):
                        pe.wait_ge(sp_ev, b + 1)
                        pe.wait_ge(v_landed[b % 2], 16 * (b // 2 + 1))
                        if b >= 1:
                            pe.wait_ge(os_ev, b)
                        for k in range(KC):
                            nc.tensor.matmul(bank[7][0:48, 0:384], PTB[b % 2][:, 48 * k:48 * k + 48],
                                             VB[b % 2][:, k, :], start=k == 0, stop=False)
                        nc.tensor.matmul(bank[7][0:48, 0:384], PTB[b % 2][0:NEW, 480:528], V[0:NEW, TT, 640:1024],
                                         start=False, stop=True).then_inc(so_mm, 1)

                    def s_back(b):
                        pe.wait_ge(os_ev, b + 1)
                        if b >= 1:
                            pe.wait_ge(so_ev, b)
                        for c in range(3):
                            mm = nc.tensor.transpose(bank[4][:, 48 * c:48 * c + 48], OS[b % 2][0:48, c * P:(c + 1) * P],
                                                     IDENT[0:48, 0:48])
                        mm.then_inc(st_mm, 1)

                    s_scores(0)
                    for b in range(DEC_BATCH):
                        if b + 1 < DEC_BATCH:
                            s_scores(b + 1)
                        if b >= 1:
                            s_weigh(b - 1)
                        if b >= 2:
                            s_back(b - 2)
                        s_turn(b)
                    s_weigh(DEC_BATCH - 1)
                    s_back(DEC_BATCH - 2)
                    s_back(DEC_BATCH - 1)
                    total("sum_att", ONES, [SQA[:, i] for i in range(3)], (sqa, 3))

                @block.scalar
                def _(act):
                    st = Steps(act, act_steps_m)
                    A = nc.scalar.activation

                    def two(ap):
                        return ap.rearrange("p (a t) -> p a t", a=2)

                    def evac(name, dst, func=ACT.Copy, also=None, **kw):
                        act.wait_ge(lin_mm, Q[name] + 1)
                        ps = pair[Q[name] % 2][:, :, 0:HALF]
                        if also is not None:
                            A(two(also), ps, ACT.Square)
                        A(two(dst), ps, func, **kw).then_inc(lin_ev, 1)

                    def rstd(name, dst, scale):
                        A(TABLE[name], EPS_C, ACT.Ln)
                        act.wait_ge(lin_mm, Q[name] + 1)
                        A(two(dst), pair[Q[name] % 2][:, :, 0:HALF], ACT.Ln, scale=scale, bias=EPS_C).then_inc(lin_ev, 1)
                        act.wait_ge(lin_ev, Q[name] + 1)
                        A(dst, dst, ACT.Exp, scale=-0.5).then_inc(rs_ready, 1)

                    for tt in range(TT + 1):
                        m = P if tt < TT else NEW
                        act.wait_ge(kdt_mm, tt + 1)
                        A(KDT[0:m, tt], bank[4 + tt % 2][0:m, :], ACT.Copy).then_inc(kdt_ev, 1)
                    for h in range(HEADS):
                        o, t = 64 * (h % 2), h // 2
                        act.wait_ge(in_mm, h + 1)
                        A(OI[o:o + 64, t, CH:SEQ], bank[4 + h % 2][o:o + 64, CH:SEQ], ACT.Copy)
                        A(OI[o:o + 64, t, SEQ:T], bank[4 + h % 2][o:o + 64, 0:NEW], ACT.Copy).then_inc(in_ev, 1)
                    in2 = list(IN2)
                    act.wait_ge(st_out, 32)
                    for l in range(len(LEVELS)):
                        if l + 1 < len(LEVELS):
                            act.wait_ge(lv_diff, l + 1)
                            v = LV[(l + 1) % 2]
                            v = v if (l + 1) in SMALL else v[:, :, 0:SEQ]
                            A(v, v, ACT.Exp).then_inc(lv_exp, 1)
                        for _ in range(2 if l < 5 else 1):
                            if in2:
                                name = in2.pop(0)
                                evac(name, proj[name])
                    act.wait_ge(lin_ev, Q["gr2"] + 1)
                    A(ETMP, GATES, ACT.Sigmoid).then_inc(gate_sig, 1)
                    for i in range(6):
                        if i >= 2:
                            act.wait_ge(rot_ready, i - 1)
                        evac(f"rot{i}", ROTMP[i % 2])
                    xo = [0, 1, 5, 6, 7]
                    for i in range(5):
                        act.wait_ge(o_ready, i + 1)
                        A(SQO[:, i], X[:, xo[i]], ACT.Square).then_inc(sqo, 1)
                    A(TABLE["sum_o"], EPS_C, ACT.Ln)
                    for i in range(5):
                        act.wait_ge(lin_mm, Q[f"sum_o{i}"] + 1)
                        A(two(RSO[i]), pair[Q[f"sum_o{i}"] % 2][:, :, 0:HALF], ACT.Ln, scale=1.0 / 64, bias=EPS_C).then_inc(lin_ev, 1)
                    act.wait_ge(lin_ev, Q["sum_o4"] + 1)
                    for i in range(5):
                        A(RSO[i], RSO[i], ACT.Exp, scale=-0.5).then_inc(rs_ready, 1)

                    units = [(h, qt) for h in range(6) for qt in range(TT)]
                    n = len(units)

                    def p_exp(i):
                        w = (units[i][1] + 1) * P
                        act.wait_ge(ps_max, i + 1)
                        A(SMP[i % 3][:, 0:w], SMP[i % 3][:, 0:w], ACT.Exp, bias=NMAX[:, i % 3:i % 3 + 1],
                          accum_out=SUM[:, i % 3:i % 3 + 1]).then_inc(ps_exp, 1)

                    def p_turned(i):
                        w = (units[i][1] + 1) * P
                        act.wait_ge(pt_mm, i + 1)
                        A(PTP[i % 2][:, 0:w], bank[6 + i % 2][:, 0:w], ACT.Copy).then_inc(pt_ev, 1)

                    def p_out(t):
                        name = f"pv{t}"
                        act.wait_ge(lin_mm, Q[name] + 1)
                        A(X[:, 2 + t, 0:SEQ], pair[Q[name] % 2][:, 0, :], ACT.Copy).then_inc(lin_ev, 1)

                    for i in range(n + 1):
                        if i < n:
                            p_exp(i)
                        if i >= 1:
                            p_turned(i - 1)
                        if i >= 3 and (i - 3) % 8 == 7:
                            p_out((i - 3) // 8)
                    p_out(2)

                    def s_exp(b):
                        act.wait_ge(ss_max, b + 1)
                        A(SMS[b % 2][0:48, :], SMS[b % 2][0:48, :], ACT.Exp, bias=NMAXS[0:48, b % 2:b % 2 + 1],
                          accum_out=SUMS[0:48, b % 2:b % 2 + 1]).then_inc(ss_exp, 1)

                    def s_turned(b):
                        act.wait_ge(sp_mm, b + 1)
                        A(PTB[b % 2][:, 0:480], bank[6][:, 0:480], ACT.Copy)
                        A(PTB[b % 2][0:NEW, 480:528], bank[5][0:NEW, 0:48], ACT.Copy).then_inc(sp_ev, 1)

                    def s_outputs(b):
                        act.wait_ge(so_mm, b + 1)
                        act.wait_ge(ss_p, b + 1)
                        A(OS[b % 2][0:48, :], bank[7][0:48, 0:384], ACT.Copy,
                          scale=RECS[0:48, b % 3:b % 3 + 1]).then_inc(os_ev, 1)

                    s_exp(0)
                    for b in range(DEC_BATCH):
                        if b + 1 < DEC_BATCH:
                            s_exp(b + 1)
                        if b >= 1:
                            s_outputs(b - 1)
                        s_turned(b)
                    s_outputs(DEC_BATCH - 1)
                    for i in range(3):
                        act.wait_ge(so_ev, DEC_BATCH)
                        A(SQA[:, i], X[:, 2 + i], ACT.Square).then_inc(sqa, 1)
                    rstd("sum_att", RSA, 1.0 / 384)

                @block.vector
                def _(dve):
                    st = Steps(dve, dve_steps_m)
                    tt_, ts_, stt = nc.vector.tensor_tensor, nc.vector.tensor_scalar, nc.vector.scalar_tensor_tensor

                    def rstd(name):
                        dve.wait_ge(rs_ready, [n for n in LIN if n.startswith("sum")].index(name) + 1)

                    tt_(QI, Q4, LV[1], ALU.mult).then_inc(qi_ready, 1)
                    for c in range(NC):
                        add = bank[4 + c % 4][:, 0:256].rearrange("p (r v) -> p r v", r=4)
                        if c > 0:
                            st.step(tt_(SC[:, c], SC[:, c - 1],
                                        EBL[:, :, c:c + 1].to_broadcast([P, 4, 64]), ALU.mult))
                        dve.wait_ge(u_mm, c + 1)
                        ins = tt_(SC[:, c], SC[:, c], add, ALU.add) if c > 0 else nc.vector.tensor_copy(SC[:, c], add)
                        ins.then_inc(u_ev, 1)
                        dve.wait_ge(u_ev, c + 1)
                    dve.wait_ge(in_mm, HEADS)
                    for r in range(4):
                        n = P if r < 3 else 64
                        s = S0[0:n, :, r, :]
                        st.step(tt_(s, s, EBL[0:n, r, 8:16].rearrange("p (b a) -> p b a", a=1).to_broadcast([n, DEC_BATCH, 64]), ALU.mult))
                        dve.wait_ge(us_mm, [2, 4, 8, 10][r])
                        tt_(s, s, bank[6 + r % 2][0:n, :].rearrange("p (b v) -> p b v", v=64), ALU.add).then_inc(us_ev, 1)

                    def diff(l):
                        h, v = LEVELS[l], LV[l % 2]
                        (d0, _), (d1, _) = blocks(v, h, 0), blocks(v, h, 1)
                        (b0, mid), (b1, _) = blocks(B, h, 0), blocks(B, h, 1)
                        st.mark(tt_(d0, mid, b0, ALU.subtract))
                        tt_(d1, b1, mid, ALU.subtract).then_inc(lv_diff, 1)

                    def scale(l):
                        h, v = LEVELS[l], LV[l % 2]
                        dve.wait_ge(lv_exp, l)
                        d0, d1 = blocks(v, h, 0)[0], blocks(v, h, 1)[0]
                        n = st.mark(tt_(d0, d0, blocks(K4, h, 0)[0], ALU.mult))
                        st.after(n)
                        tt_(d1, d1, blocks(Q4, h, 1)[0], ALU.mult).then_inc(lv_ready, 1)

                    def rotate(i):
                        dve.wait_ge(lin_ev, Q[f"rot{i}"] + 1)
                        n = st.mark(tt_(ROTMP[i % 2], ROTMP[i % 2], SIN, ALU.mult))
                        n = st.mark(tt_(ROTQK[:, i], ROTQK[:, i], COS, ALU.mult))
                        st.after(n)
                        tt_(ROTQK[:, i], ROTQK[:, i], ROTMP[i % 2], ALU.add).then_inc(rot_ready, 1)

                    gi = si = 0

                    def pick(l):
                        nonlocal gi, si
                        mask = con[:, C_MASK + CH * l:C_MASK + CH * (l + 1)].bitcast(U32).rearrange("p (a t) -> p a t", a=1)
                        for g, heads in enumerate(GROUPS):
                            n, s = len(heads), FIRST_SLOT[g]
                            dve.wait_ge(lv_mm, gi + 1)
                            nc.vector.copy_predicated(
                                AT[:, s:s + n].rearrange("p s c t -> p (s c) t"), mask.to_broadcast([P, 4 * n, CH]),
                                bank[4 + gi % 2][:, 0:4 * n * CH].rearrange("p (a t) -> p a t", t=CH)).then_inc(lv_ev, 1)
                            gi += 1
                            if l == len(LEVELS) - 1:
                                rotate(g)
                            if l in SMALL:
                                dve.wait_ge(ls_mm, si + 1)
                                nc.vector.copy_predicated(
                                    ATS[0:NEW, s:s + n], mask[0:NEW].to_broadcast([NEW, n, CH]),
                                    bank[6 + si % 2][0:NEW, 0:n * CH].rearrange("p (a t) -> p a t", t=CH)).then_inc(ls_ev, 1)
                                si += 1

                    dve.wait_ge(kdt_mm, TT + 1)
                    dve.wait_ge(us_mm, HEADS)
                    diff(1)
                    dve.wait_ge(at_zero, 1)
                    for l in range(1, len(LEVELS)):
                        pick(l - 1)
                        scale(l)
                        if l + 1 < len(LEVELS):
                            diff(l + 1)
                    pick(len(LEVELS) - 1)
                    xo = [0, 1, 5, 6, 7]
                    dve.wait_ge(in_ev, HEADS)
                    dve.wait_ge(oi_zero, 1)
                    for t in range(5):
                        dve.wait_ge(ia_mm, t + 1)
                        x = X[:, xo[t]]
                        for par_ in range(2):
                            o3 = x[:, 0:SEQ].rearrange("p (c a s) -> p a c s", a=2, s=CH)[:, par_]
                            i3 = OI[:, t, 0:SEQ].rearrange("p (c a s) -> p a c s", a=2, s=CH)[:, par_]
                            n = st.mark(tt_(o3, i3, bank[4 + 2 * (t % 2) + par_][:, 0:4 * CH].rearrange("p (c s) -> p c s", s=CH), ALU.add))
                        tt_(x[:, SEQ:T], OI[:, t, SEQ:T], bank[4 + 2 * (t % 2)][:, 4 * CH:5 * CH], ALU.add).then_inc(o_ready, 1)
                    dve.wait_ge(gate_ready, 1)
                    for i in range(5):
                        x, rs = X[:, xo[i]], RSO[i]
                        rstd(f"sum_o{i}")
                        st.step(stt(x, x, par[:, W_O + xo[i]:W_O + xo[i] + 1], rs, ALU.mult, ALU.mult))
                        tt_(x, x, GATES[:, i], ALU.mult).then_inc(gate_ready, 1)
                    units = [(h, qt) for h in range(6) for qt in range(TT)]
                    n_u = len(units)

                    def p_max(i):
                        h, qt = units[i]
                        w = (qt + 1) * P
                        dve.wait_ge(ps_mm, i + 1)
                        if i >= 3:
                            dve.wait_ge(pt_mm, i - 2)
                        st.step(stt(SMP[i % 3][:, 0:w], bank[4 + i % 2][:, 0:w], 0.125,
                                    con[:, C_BIAS + (3 - qt) * P:C_BIAS + 4 * P], ALU.mult, ALU.add))
                        nc.vector.tensor_reduce(NMAX[:, i % 3:i % 3 + 1], SMP[i % 3][:, 0:w], AX_X, ALU.max,
                                                negate=True).then_inc(ps_max, 1)

                    def p_norm(i):
                        w = (units[i][1] + 1) * P
                        dve.wait_ge(ps_exp, i + 1)
                        st.step(nc.vector.reciprocal(REC[:, i % 3:i % 3 + 1], SUM[:, i % 3:i % 3 + 1]))
                        ts_(SMP[i % 3][:, 0:w], SMP[i % 3][:, 0:w], REC[:, i % 3:i % 3 + 1], None, ALU.mult).then_inc(ps_p, 1)

                    for i in range(n_u + 1):
                        if i < n_u:
                            p_max(i)
                        if i >= 1:
                            p_norm(i - 1)

                    def s_max(b):
                        sm = SMS[b % 2]
                        dve.wait_ge(ss_mm, b + 1)
                        if b >= 2:
                            dve.wait_ge(sp_mm, b - 1)
                        for j, (lo, w) in enumerate(((0, 512), (512, 512), (1024, 256))):
                            n = st.mark(stt(sm[0:48, lo:lo + w], bank[j][0:48, 0:w], 0.125,
                                            con[0:48, C_SBIAS + lo:C_SBIAS + lo + w], ALU.mult, ALU.add))
                        stt(sm[0:48, KEYS:KEYS + NEW], bank[3][0:48, 0:NEW], 0.125,
                            con[0:48, C_NBIAS + NEW * b:C_NBIAS + NEW * (b + 1)], ALU.mult, ALU.add).then_inc(ss_read, 1)
                        st.after(n)
                        dve.wait_ge(ss_read, b + 1)
                        nc.vector.tensor_reduce(NMAXS[0:48, b % 2:b % 2 + 1], sm[0:48, :], AX_X, ALU.max,
                                                negate=True).then_inc(ss_max, 1)

                    def s_norm(b):
                        dve.wait_ge(ss_exp, b + 1)
                        if b >= 3:
                            dve.wait_ge(os_ev, b - 2)
                        nc.vector.reciprocal(RECS[0:48, b % 3:b % 3 + 1], SUMS[0:48, b % 2:b % 2 + 1]).then_inc(ss_p, 1)

                    def s_out(b):
                        dve.wait_ge(st_mm, b + 1)
                        for hp in range(2):
                            rows = slice(64 * hp, 64 * hp + 64)
                            src = bank[4][rows, 0:192].rearrange("p (c n) -> p c n", c=3)[:, :, 8 * hp:8 * hp + 8]
                            ins = nc.vector.tensor_copy(X[rows, 2:5, SEQ + 8 * b:SEQ + 8 * b + 8], src)
                            if hp == 0:
                                st.mark(ins)
                        ins.then_inc(so_ev, 1)

                    dve.wait_ge(pt_mm, n_u)
                    for b in range(DEC_BATCH + 3):
                        if b < DEC_BATCH:
                            s_max(b)
                        if 1 <= b <= DEC_BATCH:
                            s_norm(b - 1)
                        if b >= 3:
                            s_out(b - 3)
                    rstd("sum_att")
                    for i in range(3):
                        n = st.mark(stt(X[:, 2 + i], X[:, 2 + i], par[:, W_O + 2 + i:W_O + 3 + i], RSA, ALU.mult, ALU.mult))
                    st.after(n)
                    dve.sem_inc(att_ready, 1)

            mixer.close()

            with nc.sbuf_tensor("x_hi_part", [P, KT * T], F32R) as xh_sb, \
                    nc.sbuf_tensor("x_lo_part", [P, KT * T], F32R) as xl_sb, \
                    nc.sbuf_tensor("u_hi_part", [P, KT * T], F32R) as uh_sb, \
                    nc.sbuf_tensor("u_lo_part", [P, KT * T], F32R) as ul_sb, \
                    nc.sbuf_tensor("w_hi_part", [P, SPLITS * 1024], F32R) as wh_sb, \
                    nc.sbuf_tensor("w_lo_part", [P, SPLITS * 1024], F32R) as wl_sb, \
                    nc.sbuf_tensor("y", [P, KT * T], F32) as y_sb, \
                    nc.sbuf_tensor("tmp", [P, 6 * T], F32) as tmp_sb, nc.Block() as block:
                XH, XL, UH, UL, Y = (v[:, :].rearrange("p (k t) -> p k t", k=KT) for v in (xh_sb, xl_sb, uh_sb, ul_sb, y_sb))
                tmp = tmp_sb[:, :].rearrange("p (k t) -> p k t", k=6)
                TMP, ACC, RS = [tmp[:, 0], tmp[:, 1]], tmp[:, 2], tmp[:, 3]
                SQN = [ACC, RS]
                XT = [X[:, 0], X[:, 1]]
                PL = [X[:, 2 + k] for k in range(6)] + [tmp[:, 4], tmp[:, 5]]
                XORDER = [0, 1, 5, 6, 7, 2, 3, 4]

                def raw(r):
                    return raw_sb[:, slot_of(r) * 1024:(slot_of(r) + 1) * 1024]

                def w_part(sb_, i):
                    return sb_[:, (i % SPLITS) * 1024:(i % SPLITS + 1) * 1024]

                I_OUT = R_IN2
                I_UP = I_OUT + KT
                I_GATE = I_UP + 2 * FT

                @block.sync
                def _(sp):
                    for r in range(R_OUT + RAW, UNITS):
                        sp.wait_ge(*freed(former(r)))
                        sp.dma_start(raw(r), of_layer(w_units)[r * P:(r + 1) * P, :]).then_inc(w_landed[slot_of(r)], 16)
                    sp.wait_ge(y_normed, 2 * KT)
                    sp.dma_start(par[:, :], params[bass.ds(layer + 1, 1)].rearrange("l p n -> (l p) n")).then_inc(s_par, 16)
                    for i in range(RAW):
                        sp.wait_ge(*freed(max(r for r in range(UNITS) if slot_of(r) == i)))
                        sp.dma_start(raw_sb[:, i * 1024:(i + 1) * 1024],
                                     w_first[bass.ds(layer + 1, 1)].rearrange("l p n -> (l p) n")[i * P:(i + 1) * P, :]
                                     ).then_inc(s_first, 16)
                    sp.wait_ge(s_par, 16)
                    sp.wait_ge(s_first, 16 * RAW)

                @block.gpsimd
                def _(pool):
                    for b in range(2, DEC_BATCH):
                        pool.wait_ge(lin_mm, Q[f"up{5 * (b - 2)}"] + 1)
                        copy_cache(pool, b)

                @block.tensor
                def _(pe):
                    def split_product(ps, i, xh, xl, done, ready=None, order=range(KT)):
                        pe.wait_ge(w_split, i + 1)
                        wh, wl = w_part(wh_sb, i), w_part(wl_sb, i)
                        for n, k in enumerate(order):
                            if ready is not None:
                                pe.wait_ge(ready[0], ready[1] + n + 1)
                            cols = slice(k * P, (k + 1) * P)
                            for half in range(2):
                                out, t = ps[:, half, 0:HALF], slice(half * HALF, (half + 1) * HALF)
                                nc.tensor.matmul(out, wh[:, cols], xh[:, k, t], start=n == 0, stop=False)
                                nc.tensor.matmul(out, wh[:, cols], xl[:, k, t], start=False, stop=False)
                                mm = nc.tensor.matmul(out, wl[:, cols], xh[:, k, t], start=False, stop=n == KT - 1)
                        mm.then_inc(done, 1)

                    def claim(name):
                        q = Q[name]
                        pe.wait_ge(lin_ev, q - 1)
                        return pair[q % 2]

                    def claim_side(name):
                        q = D[name]
                        if q >= 2:
                            pe.wait_ge(side_ev, q - 1)
                        return pair[2 + q % 2]

                    def total(name, ready):
                        ps = claim(name)
                        pe.wait_ge(acc_ready, ready)
                        for half in range(2):
                            mm = nc.tensor.matmul(ps[:, half, 0:HALF], ONES, ACC[:, half * HALF:(half + 1) * HALF],
                                                  start=True, stop=True)
                        mm.then_inc(lin_mm, 1)

                    for k in range(KT):
                        split_product(claim(f"out{k}"), I_OUT + k, XH, XL, lin_mm, (x_split, KT) if k == 0 else None, XORDER)

                    def ple(n):
                        r = R_PLE + n // 4
                        if n % 4 == 0:
                            pe.wait_ge(w_landed[slot_of(r)], 16 * loads(r))
                        ps = claim_side(f"ple{n}")
                        for half in range(2):
                            for k in range(2):
                                o = (2 * (n % 4) + k) * P
                                mm = nc.tensor.matmul(ps[:, half, 0:HALF], raw(r)[:, o:o + P],
                                                      PT_IN[:, k, half * HALF:(half + 1) * HALF], start=k == 0, stop=k == 1)
                        mm.then_inc(side_mm, 1)

                    pe.wait_ge(s_pt, 16)
                    ple(0)
                    ple(1)
                    total("sum_mix", 1)
                    for n in range(2, KT):
                        ple(n)
                    total("sum_mlp", 2)
                    for c in range(CHUNKS):
                        i = I_UP + 2 * KT * c
                        for j in range(KT):
                            first_ = c == 0 and j == 0
                            split_product(claim(f"up{c * KT + j}"), i + j, XH, XL, lin_mm, (x_split, 2 * KT) if first_ else None)
                        for n in range(KT):
                            split_product(claim_side(f"down{c}{n}"), i + KT + n, UH, UL, side_mm,
                                          (u_split, c * KT) if n == 0 else None)
                    total("sum_down", 3)
                    for k in range(KT):
                        split_product(claim(f"gate{k}"), I_GATE + k, XH, XL, lin_mm, (x_split, 3 * KT) if k == 0 else None)

                @block.scalar
                def _(act):
                    A = nc.scalar.activation

                    def two(ap):
                        return ap.rearrange("p (a t) -> p a t", a=2)

                    def leading(dst, src, done):
                        return A(dst, src, ACT.Copy).then_inc(done, 1)

                    def split_w(i):
                        if i < len(SPLIT):
                            r = SPLIT[i]
                            act.wait_ge(w_landed[slot_of(r)], 16 * loads(r))
                            if i >= SPLITS:
                                act.wait_ge(*used_up(SPLIT[i - SPLITS]))
                            leading(w_part(wh_sb, i), raw(r), w_hi)

                    def rstd(name):
                        A(TABLE[name], EPS_C, ACT.Ln)
                        act.wait_ge(lin_mm, Q[name] + 1)
                        A(two(RS), pair[Q[name] % 2][:, :, 0:HALF], ACT.Ln, scale=1.0 / D_MODEL, bias=EPS_C).then_inc(lin_ev, 1)
                        act.wait_ge(lin_ev, Q[name] + 1)
                        A(RS, RS, ACT.Exp, scale=-0.5).then_inc(rs_ready, 1)

                    def square(k, src, done, used):
                        if k >= 3:
                            act.wait_ge(used, k - 2)
                        A(two(ACC if k == 0 else TMP[k % 2]), src, ACT.Square).then_inc(done, 1)

                    split_w(I_OUT)
                    for n, k in enumerate(XORDER):
                        leading(XH[:, k], X[:, k], x_hi)
                        if n in (0, 1):
                            split_w(I_OUT + n + 1)
                    for k in range(KT):
                        name = f"out{k}"
                        act.wait_ge(lin_mm, Q[name] + 1)
                        ps = pair[Q[name] % 2][:, :, 0:HALF]
                        square(k, ps, sq_mix, acc_mix)
                        A(two(Y[:, k]), ps, ACT.Copy).then_inc(lin_ev, 1)
                        if k < KT - 1:
                            split_w(I_OUT + k + SPLITS)

                    def ple(n):
                        act.wait_ge(side_mm, n + 1)
                        A(two(PL[n]), pair[2 + n % 2][:, :, 0:HALF], ACT.Copy).then_inc(side_ev, 1)

                    act.wait_ge(x_split, 2 * KT)
                    ple(0)
                    ple(1)
                    rstd("sum_mix")
                    for k in range(KT):
                        if k + 2 < KT:
                            ple(k + 2)
                        act.wait_ge(h_mix, k + 1)
                        square(k, two(H[:, k]), sq_h, acc_h)
                    split_w(I_OUT + KT - 1 + SPLITS)
                    rstd("sum_mlp")
                    for k in range(KT):
                        act.wait_ge(xm_ready, k + 1)
                        leading(XH[:, k], XT[k % 2], x_hi)
                    for c in range(CHUNKS):
                        for j in range(KT):
                            g, i = c * KT + j, I_UP + 2 * KT * c + j
                            if g >= 2:
                                act.wait_ge(u_split, g - 1)
                            act.wait_ge(lin_mm, Q[f"up{g}"] + 1)
                            A(two(TMP[g % 2]), pair[Q[f"up{g}"] % 2][:, :, 0:HALF], ACT.Relu).then_inc(lin_ev, 1)
                            split_w(i + SPLITS)
                            act.wait_ge(u_sq, g + 1)
                            leading(UH[:, j], TMP[g % 2], u_hi)
                        for n in range(KT):
                            i, q = I_UP + 2 * KT * c + KT + n, D[f"down{c}{n}"]
                            if c == 0:
                                act.wait_ge(side_mm, q + 1)
                                A(two(Y[:, n]), pair[2 + q % 2][:, :, 0:HALF], ACT.Copy).then_inc(side_ev, 1)
                            split_w(i + SPLITS)
                            if c == CHUNKS - 1:
                                act.wait_ge(side_ev, q + 1)
                                if n == 0:
                                    act.wait_ge(u_split, FT)
                                square(n, two(Y[:, n]), sq_down, acc_down)
                    rstd("sum_down")
                    for k in range(KT):
                        act.wait_ge(h_down, k + 1)
                        leading(XH[:, k], H[:, k], x_hi)

                    def square_new(k):
                        act.wait_ge(z_used, k + 1)
                        if k >= 3:
                            act.wait_ge(acc_pre, k - 2)
                        A(X[:, 0] if k == 0 else SQN[k % 2], H[:, k], ACT.Square).then_inc(sq_pre, 1)

                    for k in range(KT):
                        name = f"gate{k}"
                        if k >= 2:
                            act.wait_ge(z_used, k - 1)
                        act.wait_ge(lin_mm, Q[name] + 1)
                        A(two(TMP[k % 2]), pair[Q[name] % 2][:, :, 0:HALF], ACT.Sigmoid).then_inc(lin_ev, 1)
                        split_w(I_GATE + k + SPLITS)
                        if k >= 1:
                            square_new(k - 1)
                    square_new(KT - 1)

                @block.vector
                def _(dve):
                    st = Steps(dve, dve_steps_b)
                    tt_, stt = nc.vector.tensor_tensor, nc.vector.scalar_tensor_tensor

                    def remainder(dst, src, hi, done):
                        return tt_(dst, src, hi.bitcast(F32), ALU.subtract).then_inc(done, 1)

                    def split_w(i):
                        if i < len(SPLIT):
                            dve.wait_ge(w_hi, i + 1)
                            remainder(w_part(wl_sb, i), raw(SPLIT[i]), w_part(wh_sb, i), w_split)

                    def rstd(name):
                        dve.wait_ge(rs_ready, [n for n in LIN if n.startswith("sum")].index(name) + 1)

                    def accumulate(k, squared, done):
                        dve.wait_ge(squared, k + 1)
                        if k >= 2:
                            dve.wait_ge(done, k - 1)
                        ins = tt_(ACC, ACC, TMP[k % 2], ALU.add)
                        ins.then_inc(acc_ready if k == KT - 1 else done, 1)

                    def two(ap):
                        return ap.rearrange("p (a t) -> p a t", a=2)

                    split_w(I_OUT)
                    for n, k in enumerate(XORDER):
                        dve.wait_ge(x_hi, KT + n + 1)
                        remainder(XL[:, k], X[:, k], XH[:, k], x_split)
                        if n in (0, 1):
                            split_w(I_OUT + n + 1)
                    for k in range(KT):
                        if k >= 1:
                            accumulate(k, sq_mix, acc_mix)
                        if k < KT - 1:
                            split_w(I_OUT + k + SPLITS)
                    rstd("sum_mix")

                    def normed(k, w):
                        return stt(Y[:, k], Y[:, k], par[:, w + k:w + k + 1], RS, ALU.mult, ALU.mult).then_inc(y_normed, 1)

                    def add_residual(k, n, ready):
                        dve.wait_ge(y_normed, n + 1)
                        tt_(H[:, k], H[:, k], Y[:, k], ALU.add).then_inc(ready, 1)

                    for k in range(KT + 2):
                        if k < KT:
                            normed(k, W_MIX)
                        if 1 <= k <= KT:
                            add_residual(k - 1, k - 1, h_mix)
                        if k >= 4:
                            accumulate(k - 3, sq_h, acc_h)
                    accumulate(KT - 1, sq_h, acc_h)
                    split_w(I_OUT + KT - 1 + SPLITS)
                    rstd("sum_mlp")
                    dve.wait_ge(h_mix, KT)
                    for k in range(KT + 1):
                        if k < KT:
                            if k >= 2:
                                dve.wait_ge(x_split, 2 * KT + k - 1)
                            stt(XT[k % 2], H[:, k], par[:, W_MLP + k:W_MLP + k + 1], RS, ALU.mult, ALU.mult).then_inc(xm_ready, 1)
                        if k >= 1:
                            dve.wait_ge(x_hi, 2 * KT + k)
                            remainder(XL[:, k - 1], XT[(k - 1) % 2], XH[:, k - 1], x_split)
                    for c in range(CHUNKS):
                        for j in range(KT):
                            g, i = c * KT + j, I_UP + 2 * KT * c + j
                            t = TMP[g % 2]
                            dve.wait_ge(lin_ev, Q[f"up{g}"] + 1)
                            tt_(t, t, t, ALU.mult).then_inc(u_sq, 1)
                            split_w(i + SPLITS)
                            dve.wait_ge(u_hi, g + 1)
                            remainder(UL[:, j], t, UH[:, j], u_split)
                        for n in range(KT):
                            i, q = I_UP + 2 * KT * c + KT + n, D[f"down{c}{n}"]
                            if c > 0:
                                dve.wait_ge(side_ev, D[f"down{c - 1}{n}"] + 1)
                                dve.wait_ge(side_mm, q + 1)
                                tt_(two(Y[:, n]), two(Y[:, n]), pair[2 + q % 2][:, :, 0:HALF], ALU.add).then_inc(side_ev, 1)
                            split_w(i + SPLITS)
                            if c == CHUNKS - 1 and n >= 2:
                                accumulate(n - 1, sq_down, acc_down)
                    accumulate(KT - 1, sq_down, acc_down)
                    rstd("sum_down")
                    for k in range(KT + 2):
                        if k < KT:
                            normed(k, W_DOWN)
                        if 1 <= k <= KT:
                            add_residual(k - 1, KT + k - 1, h_down)
                        if k >= 2:
                            dve.wait_ge(x_hi, 3 * KT + k - 1)
                            remainder(XL[:, k - 2], H[:, k - 2], XH[:, k - 2], x_split)
                    def add_square(k):
                        dve.wait_ge(sq_pre, k + 1)
                        if k >= 2:
                            dve.wait_ge(acc_pre, k - 1)
                        tt_(X[:, 0], X[:, 0], SQN[k % 2], ALU.add).then_inc(acc_pre, 1)

                    for k in range(KT):
                        split_w(I_GATE + k + SPLITS)
                        dve.wait_ge(lin_ev, Q[f"gate{k}"] + 1)
                        if k == 0:
                            dve.wait_ge(x_split, 4 * KT)
                        st.step(tt_(TMP[k % 2], TMP[k % 2], PL[k], ALU.mult))
                        tt_(H[:, k], H[:, k], TMP[k % 2], ALU.add).then_inc(z_used, 1)
                        if k >= 2:
                            add_square(k - 1)
                    add_square(KT - 1)

            nc.gpsimd.sem_clear(range(first, last + 1))
            nc.all_engine_barrier()

        with nc.Block() as block:
            @block.sync
            def _(sp):
                sp.dma_start(y_out, h_sb[:, :]).then_inc(s_y, 16)
                sp.wait_ge(s_y, 16)
                sp.wait_ge(copied, 16 * 2 * DEC_BATCH * DEPTH)


IN_SPLITS = (256, 256, 256, 256, 384, 384, 384, 192, 192, 384, 16, 384)
IN_NAMES = ("hq", "hf", "hi", "hg", "aq", "ak", "av", "gq", "gk", "gv", "lr", "gr")


def kernel(**inputs):
    import concourse.bacc as bacc
    from concourse.bass_utils import run_bass_kernel_spmd

    a = {k: np.asarray(v) for k, v in inputs.items()}
    f = np.float32

    def feature_major(x):
        n, d = x.shape
        return x.T.reshape(d // P, P, n).transpose(1, 0, 2).reshape(P, -1)

    def both(prompt, sample, d):
        return feature_major(np.concatenate([prompt.reshape(SEQ, d), sample.reshape(NEW, d)], 0))

    def units(w):
        k, n = w.shape
        return w.reshape(k // 1024, KT, P, n // P, P).transpose(3, 0, 2, 1, 4).reshape(-1, P, 1024)

    w_units = np.zeros((DEPTH, UNITS * P, 1024), f)
    par = np.zeros((DEPTH + 1, P, W_END), f)
    s0 = np.zeros((DEPTH, P, DEC_BATCH, 4, 64), f)
    cols = dict(zip(IN_NAMES, np.split(np.arange(sum(IN_SPLITS)), np.cumsum(IN_SPLITS)[:-1])))
    for l in range(DEPTH):
        w = a["w_in"][l]
        tile_cols = {}
        for n in ("hf", "hq", "aq", "ak", "hg", "gr"):
            for i in range(len(cols[n]) // P):
                tile_cols[f"{n}{i}"] = cols[n][i * P:(i + 1) * P]
        tile_cols["gq0"], tile_cols["gk0"] = cols["gq"][:P], cols["gk"][:P]
        tile_cols["gq1"] = np.concatenate([cols["gq"][P:], cols["lr"]])
        tile_cols["gk1"] = cols["gk"][P:]
        u = []

        def in_unit(n):
            t = np.zeros((D_MODEL, P), f)
            t[:, :len(tile_cols[n])] = w[:, tile_cols[n]]
            u.append(units(t)[0])

        for n in IN1:
            in_unit(n)
        wv = w[:, np.concatenate([cols["hi"], cols["gv"], cols["av"]])]
        for g in range(2):
            for j in range(4):
                blk = wv[256 * j:256 * (j + 1), 512 * g:512 * (g + 1)]
                u.append(blk.reshape(2, P, 512).transpose(1, 0, 2).reshape(P, 1024))
        for n in IN2:
            in_unit(n)
        u.extend(units(a["w_out"][l]))
        wp = a["w_ple"][l].reshape(2, P, 2, 4, P).transpose(2, 1, 3, 0, 4).reshape(2, P, 1024)
        u.extend(wp)
        up, down = units(a["w_up"][l]), units(a["w_down"][l]).reshape(KT, CHUNKS, P, 1024)
        for c in range(CHUNKS):
            u.extend(up[c * KT:(c + 1) * KT])
            u.extend(down[:, c])
        u.extend(units(a["w_ple_gate"][l]))
        assert len(u) == UNITS
        w_units[l] = np.concatenate(u, 0)

        def col(v):
            return v.reshape(-1, P).T

        par[l, :, W_PRE:W_PRE + 8] = col(a["norm_pre_mix"][l])
        par[l, :, W_MIX:W_MIX + 8] = col(a["norm_post_mix"][l])
        par[l, :, W_MLP:W_MLP + 8] = col(a["norm_pre_mlp"][l])
        par[l, :, W_DOWN:W_DOWN + 8] = col(a["norm_post_mlp"][l])
        par[l, :, W_O:W_O + 8] = col(np.concatenate([a["hgrn_norm"][l], a["attn_norm"][l], a["gla_norm"][l]]))
        par[l, :, W_B] = a["gla_b_gate"][l][:P]
        par[l, :64, W_B + 1] = a["gla_b_gate"][l][P:]
        for i in range(DEPTH):
            par[l, :, W_LB + 2 * i:W_LB + 2 * i + 2] = col(a["hgrn_lb"][i])
        par[l, :, W_FLAG] = l
        par[l, 64:80, W_G2:W_G2 + 192] = a["gla_w_gate2"][l]
        for h in range(4):
            r, row, n = HEAD_AT[h]
            s0[l, row:row + n, :, r] = a["state_hgrn"][l][:, h].transpose(1, 0, 2)
        for h in range(6):
            r, row, n = HEAD_AT[4 + h]
            s0[l, row:row + n, :, r] = a["state_gla"][l][:, h].transpose(1, 0, 2)
    order = cache_order()
    ck = a["cache_k"].reshape(DEPTH, DEC_BATCH, WIN, 384)[:, :, order].transpose(0, 1, 3, 2)
    cv = a["cache_v"].reshape(DEPTH, DEC_BATCH, WIN, 384)[:, :, order]
    arrays = {
        "x_t": both(a["x_prompt"], a["x_sample"], D_MODEL),
        "consts": constants(),
        "params": par,
        "w_first": np.concatenate([w_units[:, :RAW * P], np.zeros((1, RAW * P, 1024), f)]),
        "p_t": np.stack([both(a["p_prompt"][l], a["p_sample"][l], 256) for l in range(DEPTH)]),
        "s0_in": s0.reshape(DEPTH, P, -1),
        "w_units": w_units,
        "ck": ck.reshape(DEPTH, DEC_BATCH * 384, WIN),
        "cv": cv.reshape(DEPTH, DEC_BATCH * WIN, 384),
    }
    arrays = {k: np.ascontiguousarray(v) for k, v in arrays.items()}
    outs = {
        "y_out": (P, KT * T), "kp_out": (DEPTH, P, 3 * SEQ), "kn_out": (DEPTH, P, 3 * NEW),
        "vp_out": (DEPTH, P, TT * 384), "vn_out": (DEPTH, NEW, 384),
        "ck_out": (DEPTH, DEC_BATCH * 384, KEPT), "cv_out": (DEPTH, DEC_BATCH * KEPT, 384),
        "sp_out": (DEPTH, P, 256), "ss_out": (DEPTH, P, 2048),
    }
    nc = bacc.Bacc("TRN2", target_bir_lowering=False, num_devices=1)
    args = {k: nc.dram_tensor(k, v.shape, F32, kind="ExternalInput").ap() for k, v in arrays.items()}
    args.update({k: nc.dram_tensor(k, s, F32, kind="ExternalOutput").ap() for k, s in outs.items()})
    build(nc, **args)
    r = run_bass_kernel_spmd(nc, [arrays], core_ids=[0]).results[0]

    y = r["y_out"].reshape(P, KT, T).transpose(2, 1, 0).reshape(T, D_MODEL)
    y_p = y[:SEQ].reshape(1, SEQ, D_MODEL)
    y_s = y[SEQ:].reshape(DEC_BATCH, DEC_SEQ, D_MODEL)

    def keys(x, n):
        return x.reshape(DEPTH, P, 3, n).transpose(0, 3, 2, 1).reshape(DEPTH, n, 6, 64)

    k_p = keys(r["kp_out"], SEQ)[:, None]
    v_p = r["vp_out"].reshape(DEPTH, P, TT, 384).transpose(0, 2, 1, 3).reshape(DEPTH, 1, SEQ, 6, 64)
    sp = r["sp_out"].reshape(DEPTH, P, 1, 4, 64)
    ss = r["ss_out"].reshape(DEPTH, P, DEC_BATCH, 4, 64)

    def states(s, heads):
        return np.stack([s[:, row:row + n, :, t].transpose(0, 2, 1, 3) for t, row, n in heads], 2)

    back = np.empty(KEPT, np.int64)
    back[order[DEC_SEQ:] - DEC_SEQ] = np.arange(KEPT)
    ck_n = r["ck_out"].reshape(DEPTH, DEC_BATCH, 384, KEPT)[:, :, :, back].transpose(0, 1, 3, 2)
    cv_n = r["cv_out"].reshape(DEPTH, DEC_BATCH, KEPT, 384)[:, :, back]
    kn = keys(r["kn_out"], NEW).reshape(DEPTH, DEC_BATCH, DEC_SEQ, 6, 64)
    vn = r["vn_out"].reshape(DEPTH, DEC_BATCH, DEC_SEQ, 6, 64)
    k_s = np.concatenate([ck_n.reshape(DEPTH, DEC_BATCH, KEPT, 6, 64), kn], 2)
    v_s = np.concatenate([cv_n.reshape(DEPTH, DEC_BATCH, KEPT, 6, 64), vn], 2)
    hg, gl = HEAD_AT[:4], HEAD_AT[4:]
    got = (y_p, y_s, states(sp, hg), states(sp, gl), k_p, v_p, states(ss, hg), states(ss, gl), k_s, v_s)
    return tuple(np.ascontiguousarray(x) for x in got)
```
